# Optimizing a Trainium2 kernel written in Bass

```python
import math
import jax
import jax.numpy as jnp
from jax import lax
import numpy as np

D_MODEL = 1024
BATCH = 1
SEQ = 1024
DEPTH = 2

CTX_LEN = 256
GRID_W = 64

SWA_HEADS = 4
SWA_KV_HEADS = 2
SWA_HEAD_DIM = 64
SWA_WINDOW = 128
SWA_BLOCK = 128
DN_HEADS = 4
DN_HEAD_DIM = 64
DN_CONV = 5
DN_CHUNK = 64
RET_HEADS = 4
RET_QK_DIM = 32
RET_V_DIM = 64
RET_CHUNK = 64
MLA_HEADS = 4
MLA_Q_RANK = 256
MLA_KV_RANK = 128
MLA_NOPE_DIM = 64
MLA_ROPE_DIM = 32
MLA_V_DIM = 64
MLA_BLOCK = 128

D_FF = 4 * D_MODEL
ROPE_BASE = 10000.0
NORM_EPS = 1e-6
LN_EPS = 1e-5
DEEPNORM_ALPHA = (2 * DEPTH) ** 0.25
DEEPNORM_BETA = (8 * DEPTH) ** -0.25

SWA_Q = SWA_HEADS * SWA_HEAD_DIM
SWA_KV = SWA_KV_HEADS * SWA_HEAD_DIM
DN_W = DN_HEADS * DN_HEAD_DIM
RET_QK = RET_HEADS * RET_QK_DIM
RET_V = RET_HEADS * RET_V_DIM
MLA_OUT = MLA_HEADS * MLA_V_DIM
MIX_WIDTH = SWA_Q + DN_W + RET_V + MLA_OUT
IN_SPLITS = (SWA_Q, SWA_KV, SWA_KV, 3 * DN_W, DN_W, 4 * DN_HEADS, RET_QK, RET_QK, RET_V, RET_V,
             MLA_Q_RANK, MLA_KV_RANK, MLA_ROPE_DIM)
IN_WIDTH = sum(IN_SPLITS)

kernel_name = 'hybrid_parallel_group_dit_block'

F32 = jnp.float32

def layer_norm(x, g, b):
    xf = x.astype(F32)
    mu = jnp.mean(xf, axis=-1, keepdims=True)
    var = jnp.mean(jnp.square(xf - mu), axis=-1, keepdims=True)
    return ((xf - mu) * lax.rsqrt(var + LN_EPS) * g.astype(F32) + b.astype(F32)).astype(x.dtype)

def rms_norm(x, g):
    xf = x.astype(F32)
    return (xf * lax.rsqrt(jnp.mean(xf * xf, axis=-1, keepdims=True) + NORM_EPS) * g.astype(F32)).astype(x.dtype)

def head_layer_norm(o, g):
    b_, t_, h_, d_ = o.shape
    mu = jnp.mean(o, axis=-1, keepdims=True)
    var = jnp.mean(jnp.square(o - mu), axis=-1, keepdims=True)
    return ((o - mu) * lax.rsqrt(var + NORM_EPS)).reshape(b_, t_, h_ * d_) * g.astype(F32)

def l2norm(t):
    return t * lax.rsqrt(jnp.sum(t * t, axis=-1, keepdims=True) + NORM_EPS)

def rope_freqs(dim):
    return ROPE_BASE ** (-jnp.arange(0, dim, 2, dtype=F32) / dim)

def axial_rope(rows, rot_dim):
    row = jnp.broadcast_to(jnp.arange(rows, dtype=F32)[:, None], (rows, GRID_W)).reshape(-1)
    col = jnp.broadcast_to(jnp.arange(GRID_W, dtype=F32)[None, :], (rows, GRID_W)).reshape(-1)
    inv = rope_freqs(rot_dim // 2)
    ang = jnp.concatenate([row[:, None] * inv, col[:, None] * inv], axis=-1)
    return jnp.cos(ang), jnp.sin(ang)

def sequence_rope(n_tok, rot_dim):
    ang = jnp.arange(n_tok, dtype=F32)[:, None] * rope_freqs(rot_dim)
    return jnp.cos(ang), jnp.sin(ang)

def apply_rope(x, cos, sin):
    xf = x.astype(F32)
    x1, x2 = jnp.split(xf, 2, axis=-1)
    c = cos[:, None, :]
    s = sin[:, None, :]
    return jnp.concatenate([x1 * c - x2 * s, x1 * s + x2 * c], axis=-1).astype(x.dtype)

def _flip_t(t):
    return jnp.flip(t, axis=2)

def _split_columns(z):
    idx = np.cumsum(np.array(IN_SPLITS))[:-1].tolist()
    return jnp.split(z, idx, axis=-1)

def short_conv(x, w):
    k_width, ch = w.shape
    pad = k_width // 2
    return lax.conv_general_dilated(x, w[:, None, :].astype(x.dtype), window_strides=(1,),
                                    padding=[(pad, pad)], dimension_numbers=('NWC', 'WIO', 'NWC'),
                                    feature_group_count=ch)

def swa_group(q, k, v, qc, kc, vc, sink, cos, sin, with_ctx_out):
    b_, s_, _ = q.shape
    l_ = kc.shape[1]
    grp = SWA_HEADS // SWA_KV_HEADS
    w_ = SWA_BLOCK
    nb = s_ // w_
    d = SWA_HEAD_DIM
    scale = d ** -0.5
    q = apply_rope(q.reshape(b_, s_, SWA_HEADS, d), cos, sin).reshape(b_, nb, w_, SWA_KV_HEADS, grp, d)
    k = apply_rope(k.reshape(b_, s_, SWA_KV_HEADS, d), cos, sin)
    v = v.reshape(b_, s_, SWA_KV_HEADS, d)
    kc = kc.reshape(b_, l_, SWA_KV_HEADS, d)
    vc = vc.reshape(b_, l_, SWA_KV_HEADS, d)

    def band(t):
        tp = jnp.pad(t, ((0, 0), (w_, w_), (0, 0), (0, 0))).reshape(b_, nb + 2, w_, SWA_KV_HEADS, d)
        return jnp.concatenate([tp[:, :-2], tp[:, 1:-1], tp[:, 2:]], axis=2)

    kb, vb = band(k), band(v)
    qpos = jnp.arange(s_).reshape(nb, w_)
    kpos = (jnp.arange(nb) * w_ - w_)[:, None] + jnp.arange(3 * w_)[None, :]
    rel = kpos[:, None, :] - qpos[:, :, None]
    valid = (jnp.abs(rel) <= SWA_WINDOW) & (kpos >= 0)[:, None, :] & (kpos < s_)[:, None, :]
    sink_hg = sink.astype(F32).reshape(SWA_KV_HEADS, grp)
    s_loc = jnp.where(valid, jnp.einsum('bnqhgd,bnkhd->bhgnqk', q, kb).astype(F32) * scale, -jnp.inf)
    s_ctx = jnp.einsum('bnqhgd,bkhd->bhgnqk', q, kc).astype(F32) * scale
    s_sink = jnp.broadcast_to(sink_hg[None, :, :, None, None, None], s_ctx.shape[:-1] + (1,))
    p = jax.nn.softmax(jnp.concatenate([s_loc, s_ctx, s_sink], axis=-1), axis=-1).astype(v.dtype)
    y = (jnp.einsum('bhgnqk,bnkhd->bnqhgd', p[..., :3 * w_], vb)
         + jnp.einsum('bhgnqk,bkhd->bnqhgd', p[..., 3 * w_:3 * w_ + l_], vc)).reshape(b_, s_, SWA_Q)
    yc = None
    if with_ctx_out:
        qcg = qc.reshape(b_, l_, SWA_KV_HEADS, grp, d)
        sc = jnp.einsum('bqhgd,bkhd->bhgqk', qcg, kc).astype(F32) * scale
        ss = jnp.broadcast_to(sink_hg[None, :, :, None, None], sc.shape[:-1] + (1,))
        pc = jax.nn.softmax(jnp.concatenate([sc, ss], axis=-1), axis=-1).astype(vc.dtype)
        yc = jnp.einsum('bhgqk,bkhd->bqhgd', pc[..., :l_], vc).reshape(b_, l_, SWA_Q)
    return y, yc

def _delta_update(s, w_i, u_i, kt_i, gl_i):
    v_new = u_i - jnp.einsum('bhcd,bhde->bhce', w_i, s)
    s_new = s * jnp.exp(gl_i)[..., None, None] + jnp.einsum('bhcd,bhce->bhde', kt_i, v_new)
    return s_new, v_new

def gated_delta_chunked(q, k, v, log_g, beta, state0):
    b_, h_, t_, dk = k.shape
    dv = v.shape[-1]
    c_ = DN_CHUNK
    n = t_ // c_
    k = k.reshape(b_, h_, n, c_, dk)
    v = v.reshape(b_, h_, n, c_, dv)
    g_cum = jnp.cumsum(log_g.reshape(b_, h_, n, c_), axis=-1)
    beta = beta.reshape(b_, h_, n, c_, 1)
    incl = jnp.tril(jnp.ones((c_, c_), bool))
    strict = jnp.tril(jnp.ones((c_, c_), bool), -1)
    decay = jnp.exp(jnp.where(incl, g_cum[..., :, None] - g_cum[..., None, :], -jnp.inf))
    kb = k * beta
    a_mat = jnp.where(strict, jnp.einsum('bhncd,bhnsd->bhncs', kb, k) * decay, 0.0)
    lhs = a_mat + jnp.eye(c_, dtype=a_mat.dtype)
    rhs = jnp.concatenate([kb * jnp.exp(g_cum)[..., None], v * beta], axis=-1)
    wu = lax.linalg.triangular_solve(lhs, rhs, left_side=True, lower=True)
    w, u = wu[..., :dk], wu[..., dk:]
    g_last = g_cum[..., -1]
    k_tail = k * jnp.exp(g_last[..., None] - g_cum)[..., None]
    chunks = lambda t: jnp.moveaxis(t, 2, 0)
    if q is None:
        def step_state(s, inp):
            s_new, _ = _delta_update(s, *inp)
            return s_new, None
        s_last, _ = lax.scan(step_state, state0, (chunks(w), chunks(u), chunks(k_tail), chunks(g_last)))
        return None, s_last
    q = q.reshape(b_, h_, n, c_, dk)
    qk = jnp.einsum('bhncd,bhnsd->bhncs', q, k) * decay
    q_dec = q * jnp.exp(g_cum)[..., None]

    def step(s, inp):
        w_i, u_i, kt_i, gl_i, qd_i, qk_i = inp
        s_new, v_new = _delta_update(s, w_i, u_i, kt_i, gl_i)
        o_i = jnp.einsum('bhcd,bhde->bhce', qd_i, s) + jnp.einsum('bhcs,bhse->bhce', qk_i, v_new)
        return s_new, o_i

    s_last, o = lax.scan(step, state0, (chunks(w), chunks(u), chunks(k_tail), chunks(g_last),
                                        chunks(q_dec), chunks(qk)))
    return jnp.moveaxis(o, 0, 2).reshape(b_, h_, t_, dv), s_last

def deltanet_group(qkv, z, ab, qkv_c, z_c, ab_c, conv_w, a_log, dt_bias, norm_g, with_ctx_out):
    def prep(qkv_, ab_):
        b_, t_, _ = qkv_.shape
        y = jax.nn.silu(short_conv(qkv_, conv_w)).astype(F32)
        q, k, v = [t.reshape(b_, t_, DN_HEADS, DN_HEAD_DIM).transpose(0, 2, 1, 3) for t in jnp.split(y, 3, axis=-1)]
        q = l2norm(q) * DN_HEAD_DIM ** -0.5
        k = l2norm(k)
        ab_ = ab_.astype(F32).reshape(b_, t_, 2, 2, DN_HEADS)
        log_g = -jnp.exp(a_log.astype(F32)) * jax.nn.softplus(ab_[:, :, :, 0] + dt_bias.astype(F32))
        beta = jax.nn.sigmoid(ab_[:, :, :, 1])
        return q, k, v, log_g.transpose(2, 0, 3, 1), beta.transpose(2, 0, 3, 1)

    def out(o, z_):
        b_, t_, _ = z_.shape
        o = rms_norm(o.transpose(0, 2, 1, 3), norm_g) * jax.nn.silu(z_.astype(F32)).reshape(b_, t_, DN_HEADS, DN_HEAD_DIM)
        return o.reshape(b_, t_, DN_W).astype(z_.dtype)

    qc, kc, vc, lgc, bc = prep(qkv_c, ab_c)
    q, k, v, lg, bt = prep(qkv, ab)
    zero = jnp.zeros((qkv.shape[0], DN_HEADS, DN_HEAD_DIM, DN_HEAD_DIM), F32)
    oc_f, s_f = gated_delta_chunked(qc if with_ctx_out else None, kc, vc, lgc[0], bc[0], zero)
    oc_b, s_b = gated_delta_chunked(_flip_t(qc) if with_ctx_out else None, _flip_t(kc), _flip_t(vc),
                                    _flip_t(lgc[1]), _flip_t(bc[1]), zero)
    o_f, _ = gated_delta_chunked(q, k, v, lg[0], bt[0], s_f)
    o_b, _ = gated_delta_chunked(_flip_t(q), _flip_t(k), _flip_t(v), _flip_t(lg[1]), _flip_t(bt[1]), s_b)
    y = out(o_f + _flip_t(o_b), z)
    yc = out(oc_f + _flip_t(oc_b), z_c) if with_ctx_out else None
    return y, yc

def retention_scan(k, v, log_gamma, state0, emit_starts):
    b_, h_, t_, dk = k.shape
    c_ = RET_CHUNK
    n = t_ // c_
    pos = jnp.arange(c_, dtype=F32)
    zeta = jnp.exp((c_ - 1 - pos)[None, :] * log_gamma[:, None])
    kv = jnp.einsum('bhncd,bhnce->bhnde', k.reshape(b_, h_, n, c_, dk) * zeta[None, :, None, :, None],
                    v.reshape(b_, h_, n, c_, v.shape[-1]))
    g_chunk = jnp.exp(c_ * log_gamma)[None, :, None, None]

    def step(r, kv_i):
        return r * g_chunk + kv_i, (r if emit_starts else None)

    r_last, starts = lax.scan(step, state0, jnp.moveaxis(kv, 2, 0))
    return (jnp.moveaxis(starts, 0, 2) if emit_starts else None), r_last

def retention_readout(q, k, v, log_gamma, starts):
    b_, h_, t_, dk = q.shape
    dv = v.shape[-1]
    c_ = RET_CHUNK
    n = t_ // c_
    pos = jnp.arange(c_, dtype=F32)
    rel = pos[:, None] - pos[None, :]
    dmat = jnp.where(rel >= 0, jnp.exp(jnp.maximum(rel, 0.0)[None] * log_gamma[:, None, None]), 0.0)
    qr = q.reshape(b_, h_, n, c_, dk)
    kr = k.reshape(b_, h_, n, c_, dk)
    vr = v.reshape(b_, h_, n, c_, dv)
    inner = jnp.einsum('bhncs,bhnse->bhnce', jnp.einsum('bhncd,bhnsd->bhncs', qr, kr) * dmat[None, :, None], vr)
    xi = jnp.exp((pos + 1.0)[None, :] * log_gamma[:, None])
    cross = jnp.einsum('bhncd,bhnde->bhnce', qr * xi[None, :, None, :, None], starts)
    return (inner + cross).reshape(b_, h_, t_, dv)

def retention_group(q, k, v, g, qc, kc, vc, gc, log1m_gamma, norm_g, cos, sin, with_ctx_out):
    log_gamma = jnp.log1p(-jnp.exp(log1m_gamma.astype(F32)))
    heads = lambda t, dh: t.reshape(t.shape[0], t.shape[1], RET_HEADS, dh)
    bhtd = lambda t: t.astype(F32).transpose(0, 2, 1, 3)
    sc = RET_QK_DIM ** -0.5
    q = bhtd(apply_rope(heads(q, RET_QK_DIM), cos, sin)) * sc
    k = bhtd(apply_rope(heads(k, RET_QK_DIM), cos, sin))
    v = bhtd(heads(v, RET_V_DIM))
    kc = bhtd(heads(kc, RET_QK_DIM))
    vc = bhtd(heads(vc, RET_V_DIM))
    zero = jnp.zeros((q.shape[0], RET_HEADS, RET_QK_DIM, RET_V_DIM), F32)

    def out(o, g_):
        y = head_layer_norm(o.transpose(0, 2, 1, 3), norm_g) * jax.nn.silu(g_.astype(F32))
        return y.astype(g_.dtype)

    st_cf, r_f = retention_scan(kc, vc, log_gamma[0], zero, with_ctx_out)
    st_cb, r_b = retention_scan(_flip_t(kc), _flip_t(vc), log_gamma[1], zero, with_ctx_out)
    st_f, _ = retention_scan(k, v, log_gamma[0], r_f, True)
    st_b, _ = retention_scan(_flip_t(k), _flip_t(v), log_gamma[1], r_b, True)
    o = (retention_readout(q, k, v, log_gamma[0], st_f)
         + _flip_t(retention_readout(_flip_t(q), _flip_t(k), _flip_t(v), log_gamma[1], st_b)))
    y = out(o, g)
    yc = None
    if with_ctx_out:
        qcs = bhtd(heads(qc, RET_QK_DIM)) * sc
        oc = (retention_readout(qcs, kc, vc, log_gamma[0], st_cf)
              + _flip_t(retention_readout(_flip_t(qcs), _flip_t(kc), _flip_t(vc), log_gamma[1], st_cb)))
        yc = out(oc, gc)
    return y, yc

def mla_queries(cq, q_norm, w_uq, cos, sin):
    b_, t_, _ = cq.shape
    q = (rms_norm(cq, q_norm) @ w_uq).reshape(b_, t_, MLA_HEADS, MLA_NOPE_DIM + MLA_ROPE_DIM)
    if cos is None:
        return q
    return jnp.concatenate([q[..., :MLA_NOPE_DIM], apply_rope(q[..., MLA_NOPE_DIM:], cos, sin)], axis=-1)

def mla_keys_values(ckv, kr, kv_norm, w_ukv, cos, sin):
    b_, t_, _ = ckv.shape
    kv = (rms_norm(ckv, kv_norm) @ w_ukv).reshape(b_, t_, MLA_HEADS, MLA_NOPE_DIM + MLA_V_DIM)
    kr = kr[:, :, None, :]
    if cos is not None:
        kr = apply_rope(kr, cos, sin)
    k = jnp.concatenate([kv[..., :MLA_NOPE_DIM], jnp.broadcast_to(kr, (b_, t_, MLA_HEADS, MLA_ROPE_DIM))], axis=-1)
    return k, kv[..., MLA_NOPE_DIM:]

def mla_attend(q, k_all, v_all):
    b_, t_, h_, dq = q.shape
    nb = t_ // MLA_BLOCK
    scale = dq ** -0.5
    qb = q.reshape(b_, nb, MLA_BLOCK, h_, dq).transpose(1, 0, 2, 3, 4)

    def one_block(qi):
        s = jnp.einsum('bqhd,bkhd->bhqk', qi, k_all).astype(F32) * scale
        p = jax.nn.softmax(s, axis=-1).astype(v_all.dtype)
        return jnp.einsum('bhqk,bkhd->bqhd', p, v_all)

    o = lax.map(one_block, qb)
    return o.transpose(1, 0, 2, 3, 4).reshape(b_, t_, h_ * v_all.shape[-1])

def mla_group(cq, ckv, kr, cq_c, ckv_c, kr_c, q_norm, w_uq, kv_norm, w_ukv, cos, sin, with_ctx_out):
    q = mla_queries(cq, q_norm, w_uq, cos, sin)
    k, v = mla_keys_values(ckv, kr, kv_norm, w_ukv, cos, sin)
    kc, vc = mla_keys_values(ckv_c, kr_c, kv_norm, w_ukv, None, None)
    y = mla_attend(q, jnp.concatenate([k, kc], axis=1), jnp.concatenate([v, vc], axis=1))
    yc = mla_attend(mla_queries(cq_c, q_norm, w_uq, None, None), kc, vc) if with_ctx_out else None
    return y, yc

def token_mixers(h, hc, w_in, swa_sink, dn_conv_w, dn_a_log, dn_dt_bias, dn_norm_g, ret_log1m_gamma,
                 ret_norm_g, mla_q_norm, mla_w_uq, mla_kv_norm, mla_w_ukv, rope, with_ctx_out):
    (a_q, a_k, a_v, b_qkv, b_z, b_ab, c_q, c_k, c_v, c_g, d_cq, d_ckv, d_kr) = _split_columns(h @ w_in)
    (a_qc, a_kc, a_vc, b_qkvc, b_zc, b_abc, c_qc, c_kc, c_vc, c_gc, d_cqc, d_ckvc, d_krc) = _split_columns(hc @ w_in)
    swa_cos, swa_sin, ret_cos, ret_sin, mla_cos, mla_sin = rope
    ya, yac = swa_group(a_q, a_k, a_v, a_qc, a_kc, a_vc, swa_sink, swa_cos, swa_sin, with_ctx_out)
    yb, ybc = deltanet_group(b_qkv, b_z, b_ab, b_qkvc, b_zc, b_abc, dn_conv_w, dn_a_log, dn_dt_bias,
                             dn_norm_g, with_ctx_out)
    yr, yrc = retention_group(c_q, c_k, c_v, c_g, c_qc, c_kc, c_vc, c_gc, ret_log1m_gamma, ret_norm_g,
                              ret_cos, ret_sin, with_ctx_out)
    yd, ydc = mla_group(d_cq, d_ckv, d_kr, d_cqc, d_ckvc, d_krc, mla_q_norm, mla_w_uq, mla_kv_norm,
                        mla_w_ukv, mla_cos, mla_sin, with_ctx_out)
    y = jnp.concatenate([ya, yb, yr, yd], axis=-1)
    yc = jnp.concatenate([yac, ybc, yrc, ydc], axis=-1) if with_ctx_out else None
    return y, yc

def squared_relu_mlp(h, w1, w2):
    return jnp.square(jax.nn.relu(h @ w1)) @ w2

def setup_inputs(seed: int = 0) -> dict:
    key = jax.random.key(seed)
    ks = jax.random.split(key, 32)
    nrm = lambda k, shape, scale: jax.random.normal(k, shape, F32) * scale
    dt = jnp.exp(jax.random.uniform(ks[10], (DEPTH, 2, DN_HEADS), F32, math.log(1e-3), math.log(1e-1)))
    return {
        'x': nrm(ks[0], (BATCH, SEQ, D_MODEL), 1.0),
        'c': nrm(ks[1], (BATCH, D_MODEL), 1.0),
        'ctx': nrm(ks[2], (BATCH, CTX_LEN, D_MODEL), 1.0),
        'c_ctx': nrm(ks[3], (D_MODEL,), 1.0),
        'ada_w': nrm(ks[4], (DEPTH, D_MODEL, 6 * D_MODEL), D_MODEL ** -0.5),
        'ada_b': nrm(ks[5], (DEPTH, 6 * D_MODEL), 0.02),
        'w_in': nrm(ks[6], (DEPTH, D_MODEL, IN_WIDTH), D_MODEL ** -0.5),
        'swa_sink': nrm(ks[7], (DEPTH, SWA_HEADS), 0.5),
        'dn_conv_w': nrm(ks[8], (DEPTH, DN_CONV, 3 * DN_W), DN_CONV ** -0.5),
        'dn_a_log': jnp.log(jax.random.uniform(ks[9], (DEPTH, 2, DN_HEADS), F32, 1.0, 16.0)),
        'dn_dt_bias': dt + jnp.log(-jnp.expm1(-dt)),
        'dn_norm_g': 1.0 + nrm(ks[11], (DEPTH, DN_HEAD_DIM), 0.02),
        'ret_log1m_gamma': (-(5.0 + jnp.arange(RET_HEADS, dtype=F32)) * math.log(2.0)
                            + nrm(ks[12], (DEPTH, 2, RET_HEADS), 0.05)),
        'ret_norm_g': 1.0 + nrm(ks[13], (DEPTH, RET_V), 0.02),
        'mla_q_norm': 1.0 + nrm(ks[14], (DEPTH, MLA_Q_RANK), 0.02),
        'mla_w_uq': nrm(ks[15], (DEPTH, MLA_Q_RANK, MLA_HEADS * (MLA_NOPE_DIM + MLA_ROPE_DIM)), MLA_Q_RANK ** -0.5),
        'mla_kv_norm': 1.0 + nrm(ks[16], (DEPTH, MLA_KV_RANK), 0.02),
        'mla_w_ukv': nrm(ks[17], (DEPTH, MLA_KV_RANK, MLA_HEADS * (MLA_NOPE_DIM + MLA_V_DIM)), MLA_KV_RANK ** -0.5),
        'w_out': nrm(ks[18], (DEPTH, MIX_WIDTH, D_MODEL), MIX_WIDTH ** -0.5 * DEEPNORM_BETA),
        'ln1_g': 1.0 + nrm(ks[19], (DEPTH, D_MODEL), 0.02),
        'ln1_b': nrm(ks[20], (DEPTH, D_MODEL), 0.02),
        'w_ff1': nrm(ks[21], (DEPTH, D_MODEL, D_FF), D_MODEL ** -0.5),
        'w_ff2': nrm(ks[22], (DEPTH, D_FF, D_MODEL), D_FF ** -0.5 * DEEPNORM_BETA),
        'ln2_g': 1.0 + nrm(ks[23], (DEPTH, D_MODEL), 0.02),
        'ln2_b': nrm(ks[24], (DEPTH, D_MODEL), 0.02),
    }

def reference(x, c, ctx, c_ctx, ada_w, ada_b, w_in, swa_sink, dn_conv_w, dn_a_log, dn_dt_bias, dn_norm_g,
              ret_log1m_gamma, ret_norm_g, mla_q_norm, mla_w_uq, mla_kv_norm, mla_w_ukv, w_out, ln1_g, ln1_b,
              w_ff1, w_ff2, ln2_g, ln2_b):
    n_tok = x.shape[1]
    rows = n_tok // GRID_W
    rope = (*axial_rope(rows, SWA_HEAD_DIM), *sequence_rope(n_tok, RET_QK_DIM), *axial_rope(rows, MLA_ROPE_DIM))
    silu_c = jax.nn.silu(c)
    silu_cc = jax.nn.silu(c_ctx)
    xc = ctx
    for layer in range(DEPTH):
        with_ctx_out = layer < DEPTH - 1
        sh1, sc1, g1, sh2, sc2, g2 = jnp.split((silu_c @ ada_w[layer] + ada_b[layer])[:, None, :], 6, axis=-1)
        csh1, csc1, cg1, csh2, csc2, cg2 = jnp.split((silu_cc @ ada_w[layer] + ada_b[layer])[None, None, :], 6, axis=-1)
        y, yc = token_mixers(x * (1 + sc1) + sh1, xc * (1 + csc1) + csh1, w_in[layer], swa_sink[layer],
                             dn_conv_w[layer], dn_a_log[layer], dn_dt_bias[layer], dn_norm_g[layer],
                             ret_log1m_gamma[layer], ret_norm_g[layer], mla_q_norm[layer], mla_w_uq[layer],
                             mla_kv_norm[layer], mla_w_ukv[layer], rope, with_ctx_out)
        x = layer_norm(DEEPNORM_ALPHA * x + g1 * (y @ w_out[layer]), ln1_g[layer], ln1_b[layer])
        x = layer_norm(DEEPNORM_ALPHA * x + g2 * squared_relu_mlp(x * (1 + sc2) + sh2, w_ff1[layer], w_ff2[layer]),
                       ln2_g[layer], ln2_b[layer])
        if with_ctx_out:
            xc = layer_norm(DEEPNORM_ALPHA * xc + cg1 * (yc @ w_out[layer]), ln1_g[layer], ln1_b[layer])
            xc = layer_norm(DEEPNORM_ALPHA * xc + cg2 * squared_relu_mlp(xc * (1 + csc2) + csh2, w_ff1[layer], w_ff2[layer]),
                            ln2_g[layer], ln2_b[layer])
    return x


_drawn_inputs = setup_inputs


def setup_inputs(seed=0):
    import zlib

    import numpy as np

    out = dict(_drawn_inputs(seed))
    spreads = {}
    factors = {'swa_sink': 64.0,
     'dn_norm_g': 8.0,
     'ret_norm_g': 8.0,
     'mla_q_norm': 8.0,
     'mla_w_uq': 3.423,
     'mla_kv_norm': 8.0}
    for name, (base, spread) in spreads.items():
        noise = np.random.default_rng([zlib.crc32(name.encode()), seed]).standard_normal(out[name].shape)
        drawn = base * np.exp(spread * noise) if base else spread * noise
        out[name] = jnp.asarray(drawn.astype(out[name].dtype))
    for name, factor in factors.items():
        out[name] = (out[name] * factor).astype(out[name].dtype)
    return out
```

```python
from contextlib import ExitStack, contextmanager

import numpy as np

import concourse.bass as bass
from concourse import mybir

ALU = mybir.AluOpType
ACT = mybir.ActivationFunctionType
AX = mybir.AxisListType
F32 = mybir.dt.float32

P = 128
DM = 1024
KT = DM // P
NCTX, NLAT = 256, 1024
NTOK = NCTX + NLAT
NT = NTOK // P
CT = NCTX // P
DEPTH = 2
GRID_W = 64
H = 4
CW = 512
FG = 4
ALPHA = float((2 * DEPTH) ** 0.25)
LN_EPS, EPS = 1e-5, 1e-6
NEG = -1e30
LEVELS = 7
CHUNKS = 12 + 1 + 2 + 1 + 2 + 1 + 2 + 4 * FG
SEGMENTS = [(0, 256), (256, 768), (768, 1280)]


def chunk_params():
    at, out = 0, {}
    for name, n in (("sink", H), ("log1m", 2 * H), ("log1m_row", 2), ("a_log", 2 * H),
                    ("dt", 2 * H), ("dn_g", 64), ("ret_g", 256), ("ln1_g", KT), ("ln1_b", KT),
                    ("ln2_g", KT), ("ln2_b", KT), ("conv", 30), ("q_norm", 2), ("kv_norm", 1)):
        out[name] = (at, at + n)
        at += n
    return out, at


PARAMS, NPARAM = chunk_params()


def rope_tables():
    f = np.float32
    freqs = lambda dim: (f(10000.0) ** (-np.arange(0, dim, 2, dtype=f) / f(dim))).astype(f)
    pos = np.arange(NLAT)
    row, col = (pos // GRID_W).astype(f), (pos % GRID_W).astype(f)
    angs = []
    for dim in (64, None, 32):
        if dim is None:
            angs.append(pos.astype(f)[:, None] * freqs(32))
        else:
            inv = freqs(dim // 2)
            angs.append(np.concatenate([row[:, None] * inv, col[:, None] * inv], -1))
    lat = np.concatenate([g(a.astype(f)) for a in angs for g in (np.cos, np.sin)], -1).astype(f)
    head = np.concatenate([np.full((NCTX, a.shape[1]), v, f) for a in angs for v in (1.0, 0.0)], -1)
    return np.concatenate([head, lat], 0).reshape(NT, P, 128).transpose(1, 0, 2)


def constants():
    i = np.arange(P)
    a, b = i[:, None], i[None, :]
    f = np.float32
    out = {
        "ident": a == b,
        "tri": np.stack([a <= b, a >= b], 1),
        "upto": np.stack([np.where(b >= a, 0, NEG), np.where(b <= a, 0, NEG)], 1),
        "ones": np.ones((P, P)),
        "mean": np.full((P, P), 1.0 / DM),
        "rel": np.stack([np.maximum(b - a, 0), np.maximum(a - b, 0)], 1),
        "age": np.stack([np.broadcast_to(b + 1, (P, P)), np.broadcast_to(P - b, (P, P))], 1),
        "left": np.stack([P - 1 - i, i], 1),
        "heads_diag": (a // 32) == (np.arange(256)[None, :] // 64),
        "rope": rope_tables(),
    }
    return {k: np.ascontiguousarray(v, dtype=f).reshape(P, -1) for k, v in out.items()}


def level_masks():
    i = np.arange(P)
    c, s = i[:, None], i[None, :]
    out = np.zeros((P, 2, LEVELS, P), np.float32)
    for lv in range(LEVELS):
        same = (c >> (lv + 1)) == (s >> (lv + 1))
        out[:, 0, lv] = -1.0 * (same & (((c >> lv) & 1) == 1) & (((s >> lv) & 1) == 0))
        out[:, 1, lv] = -1.0 * (same & (((c >> lv) & 1) == 0) & (((s >> lv) & 1) == 1))
    return out.reshape(P, -1)


def spread(ap, axis, n):
    shape = list(ap.shape)
    shape.insert(axis, n)
    return ap.unsqueeze(axis).broadcast_to(shape)


class Lane:

    def __init__(self, eng, name, sems, book):
        self.e, self.name, self.sems, self.book = eng, name, sems, book
        self.seen, self.at = {}, {}
        self.i, self.times, self.loops, self.n, self.base, self.phase = None, 1, 0, 0, 0, 0

    def nth(self, name, k=1, per=0):
        v = self.seen.get(name, 0) + k
        return v + self.i * per if per and self.i is not None else v

    def passed(self, name, n):
        self.seen[name] = self.seen.get(name, 0) + n

    def tally(self, name, n=1):
        key = (self.phase, name)
        self.book["new"][key] = self.book["new"].get(key, 0) + n * self.times
        return n

    def link(self, ins):
        self.n += 1
        ins.then_inc(self.sems["chain_" + self.name], 1)
        v = self.base + self.n
        if self.i is not None:
            v = v + self.i * self.book["links"].get((self.name, self.loops), 1)
        self.e.wait_ge(self.sems["chain_" + self.name], v)

    @contextmanager
    def loop(self, count, signals=(), down_from=None):
        self.base, self.n, self.times = self.base + self.n, 0, count
        if down_from is not None:
            tile = self.e.alloc_register(f"down_{self.name}_{self.loops}")
            self.e.reg_mov(tile, down_from)
        with self.e.Fori(0, count) as i:
            self.i = i
            if down_from is not None:
                self.down = self.e.snap(tile, min_val=down_from - count + 1, max_val=down_from)
            yield i
            if down_from is not None:
                self.e.reg_sub(tile, tile, 1)
            self.i = None
        self.book["links"][(self.name, self.loops)] = self.n
        self.loops += 1
        self.base, self.n, self.times = self.base + self.n * count, 0, 1
        for name, per in signals:
            self.passed(name, per * count)

    def barrier(self):
        self.e.drain().then_inc(self.sems["phase"], 1)
        self.phase += 1
        self.e.wait_ge(self.sems["phase"], 4 * self.phase)
        self.book["phases"] = self.phase
        for (phase, name), n in self.book["old"].items():
            if phase == self.phase - 1:
                self.at[name] = self.at.get(name, 0) + n
        self.seen = dict(self.at)


SEM_NAMES = [
    "phase", "chain_pe", "chain_act", "chain_dve", "chain_pool",
    "chunk_in_0", "chunk_in_1", "chunk_used", "consts_in", "x_in", "params_in", "weights_in", "masks_in", "out_done",
    "silu_c", "silu_ready", "ada_mm", "ada_sum", "h_lat", "h_ctx", "h_scaled",
    "prod", "evac_act", "evac_dve", "relu", "sq_done", "ln_mean", "ln_centred", "ln_square", "ln_var", "ln_veps", "ln_root",
    "ln_rstd", "ln_scaled",
    "tile_in", "tile_used",
    "z_mm", "z_sb", "ss", "veps", "rstd", "normed", "cT_mm", "cT_sb", "up_mm", "up_v", "qk_roped", "qkT_mm", "qkT_sb",
    "maxrow_mm", "maxrow", "v_staged", "keyed", "exped", "weighed", "y_done", "q_staged", "q_free", "scores", "rowmax", "probs", "pT_mm", "pT_act", "pT_dve", "pv", "y_norm", "yT_mm", "yT_sb",
    "s_free", "tables",
    "r_roped", "r_kT_mm", "r_kT_sb", "r_kz", "r_kv", "r_state", "r_stage", "r_scores", "r_probs", "r_out", "r_o",
    "g_sq", "g_tanh", "g_veps", "g_rstd", "g_y",
    "c_y", "c_tanh", "c_silu", "d_stage", "d_tok", "d_sq", "d_veps", "d_rstd", "d_norm", "d_kT", "d_v", "d_kTs", "dn_gates",
    "dn_gates2", "r_centred", "g_row", "r_kcopy", "sk",
] + [f"{n}{d}" for d in range(2) for n in (
    "u_stage", "u_g", "u_arg", "u_dt", "u_gram", "u_inv", "u_tmm", "u_tsb", "u_ymm", "u_ysb", "u_umm", "u_usb",
    "u_keg", "u_wmm", "u_wsb", "u_vmm", "u_vsb", "u_omm", "u_done", "u_e", "u_kfree", "u_gc")]

CREDITS = {"pe": {}, "dve": {"u_done0": 1, "u_done1": 1}, "act": {}, "pool": {}}


def build(nc, d, book):
    with ExitStack() as ctx:
        sb = lambda name, shape: ctx.enter_context(nc.sbuf_tensor(name, shape, F32))
        ps = ctx.enter_context(nc.psum_tensor("ps", [P, 8, 512], F32))
        sems = {n: ctx.enter_context(nc.semaphore(n)) for n in SEM_NAMES}

        X = sb("X", [P, KT, NTOK])
        Hn = sb("Hn", [P, KT * NTOK])
        Hm = Hn[:].rearrange("p (k n) -> p k n", k=KT)
        Yn = sb("Yn", [P, KT * NTOK])
        Y = Yn[:].rearrange("p (k n) -> p k n", k=KT)
        ring = sb("ring", [P, 2, KT * CW])
        cshape = {"ident": 128, "tri": 256, "upto": 256, "ones": 128, "mean": 128, "rel": 256, "age": 256,
                  "left": 2, "heads_diag": 256, "rope": NT * 128}
        consts = sb("consts", [P, sum(cshape.values())])
        cst, at = {}, 0
        for n_, w_ in cshape.items():
            cst[n_] = consts[:, at:at + w_]
            at += w_
        ident, ones, mean_w = cst["ident"], cst["ones"], cst["mean"]
        two = lambda n_: cst[n_].rearrange("p (a b) -> p a b", a=2)
        tri, upto, rel, age = (two(n_) for n_ in ("tri", "upto", "rel", "age"))
        window = upto
        rope = cst["rope"].rearrange("p (t c) -> p t c", t=NT)
        params = sb("params", [P, NPARAM])
        par = {n_: params[:, a:b] for n_, (a, b) in PARAMS.items()}
        silu_c = sb("silu_c_sb", [P, KT, 2])
        mods = sb("mods", [P, DEPTH, 48, 2])
        ada_b = sb("ada_bias", [P, DEPTH, 48])
        small = sb("small", [P, 168])
        temp = sb("temp", [P, 10448])
        cc = temp[:, 10432:10448].rearrange("p (k s) -> p k s", k=KT)

        def cut(region, base, *shape):
            n = int(np.prod(shape))
            ap = region[:, base:base + n]
            if len(shape) == 2:
                ap = ap.rearrange("p (a b) -> p a b", a=shape[0])
            if len(shape) == 3:
                ap = ap.rearrange("p (a b c) -> p a b c", a=shape[0], b=shape[1])
            return ap, base + n

        SH1, SC1, G1, SH2, SC2, G2 = (8 * j for j in range(6))

        ss = small[:, 0:8]
        rs = small[:, 8:16]
        rowneg, den, esink, rden, nsink = (small[:, 16 + 4 * j:20 + 4 * j] for j in range(5))
        lg_ret = small[:, 36:44]
        lg_row = small[:, 44:46]
        zeta = small[:, 46:54].rearrange("p (a b) -> p a b", a=2)
        gch = small[:, 54:56]
        nega = small[:, 56:64]
        gc = [small[:, 64 + 8 * j:72 + 8 * j] for j in range(2)]
        egt = [small[:, 80 + 12 * j:92 + 12 * j] for j in range(2)]
        tl = [small[:, 104 + 12 * j:116 + 12 * j] for j in range(2)]
        ss2 = small[:, 136:144]
        rs2 = small[:, 144:152]
        sume = small[:, 152:156]
        mhalf = small[:, 160:168]
        musum = small[:, 128:132]

        hst, a0 = cut(temp, 0, KT, P)
        zst, a1 = cut(temp, a0, 512)
        m_qk, a2 = cut(temp, a1, 8, 96)
        m_cT, a3 = cut(temp, a2, 3, P)
        m_a, a4 = cut(temp, a3, 8, 32)
        m_b, a5 = cut(temp, a4, 8, 32)
        m_uq, a6 = cut(temp, a5, 2, 384)
        m_ukv, a7 = cut(temp, a6, 512)
        m_sq, a8 = cut(temp, a7, 384)
        m_q, a9 = cut(temp, a8, H, NTOK)
        assert a9 <= 10448
        m_k, b0 = cut(Yn, 0, H, NTOK)
        m_v, b1 = cut(Yn, b0, NT, 256)
        p_sb, c0 = cut(temp, 0, NT, P)
        pT0, c1 = cut(temp, c0, NT, P)
        pT1, c2 = cut(temp, c1, NT, P)
        qst, c3 = cut(temp, c2, H, P)
        yst, c4 = cut(temp, c3, H, 64)
        assert c4 <= a8
        pT = [pT0, pT1]
        w_qk, e0 = cut(temp, c4, 384)
        w_a, e1 = cut(temp, e0, 384)
        w_b, e2 = cut(temp, e1, 384)
        w_qT, e3 = cut(temp, e2, 2, NTOK)
        w_kT, e4 = cut(temp, e3, NTOK)
        w_v, e5 = cut(Yn, 2 * NTOK, NT, P)
        kst, e6 = cut(Yn, e5, 3, P)
        assert e4 <= 10448 and e6 <= 4 * NTOK
        r_z = temp[:, 1024:1792]
        r_R, f0 = cut(temp, 1792, 2, P)
        r_a, f1 = cut(temp, f0, 256)
        r_b, f2 = cut(temp, f1, 256)
        r_kz, f3 = cut(temp, f2, P)
        r_tmp, f4 = cut(temp, f3, 256)
        r_S, f5 = cut(temp, f4, NT + 1, 256)
        r_v, f6 = cut(temp, f5, NT, 256)
        r_k, f7 = cut(temp, f6, NT, P)
        r_dt, f8 = cut(temp, f7, H, P)
        r_xi, f9 = cut(temp, f8, 2, P)
        assert f9 <= 10448
        r_qkT, g0 = cut(Yn, 0, 2, NTOK)
        r_g, g1 = cut(Yn, g0, NT, 256)
        assert g1 <= 4 * NTOK
        r_qst, h0 = cut(temp, 0, 4, P)
        r_p, h1 = cut(temp, h0, H, P)
        r_o, h2 = cut(temp, h1, H, 64)
        r_sq, h3 = cut(temp, h2, H, 64)
        r_gt, h4 = cut(temp, h3, H, 64)
        r_Sb = r_R[:, :, :].rearrange("p a b -> p (a b)")
        assert h4 <= 1792
        PADDED = NTOK + 8
        raw, i0 = cut(temp, 0, 6, PADDED)
        d_z, i1 = cut(temp, i0, NT, 256)
        d_ab, i2 = cut(temp, i1, NT, 16)
        assert i2 <= 10448
        d_o = temp[:, 4 * PADDED:4 * PADDED + NT * 256].rearrange("p (t c) -> p t c", t=NT)
        d_hst, _ = cut(Yn, 2 * NTOK, KT, P)
        kv_tok, j0 = cut(Hn, 0, NT, 512)
        levels, j1 = cut(Hn, j0, 2, LEVELS, P)
        d_st, j2 = cut(Hn, j1, 6, P)
        d_n, j3 = cut(Hn, j2, 8, 64)
        d_sq, j4 = cut(Hn, j3, 8, 64)
        d_lg, j5 = cut(Hn, j4, NT, 8)
        d_bt, j6 = cut(Hn, j5, NT, 8)
        d_x, j7 = cut(Hn, j6, NT, 8)
        d_w, j8 = cut(Hn, j7, NT, 8)
        assert j8 <= 10240
        cv_y, _ = cut(Yn, 2 * NTOK, PADDED - 4)
        cv_t, _ = cut(Hn, j1, PADDED - 4)
        ringf = ring[:].rearrange("p a b -> p (a b)")
        sc, y0 = [], 2 * NTOK
        for q_ in range(2):
            b = {}
            o_ = q_ * 4096
            for n_, shape in (("qk", (4, P)), ("gm", (H, P)), ("dt", (H, P)), ("at", (H, P)), ("qkd", (H, P)),
                              ("u", (H, P)), ("ym", (H, P)), ("S", (2, P)), ("o", (H, 64))):
                b[n_], o_ = cut(ringf, o_, *shape)
            assert o_ <= (q_ + 1) * 4096
            for n_ in ("keg", "kt", "wt", "vn"):
                b[n_], y0 = cut(Yn, y0, 256)
            sc.append(b)
        assert y0 <= 4 * NTOK
        relu_sb, _ = cut(temp, 0, 4, 512)
        ln_r, _ = cut(temp, 2048, 3, 512)

        r_th, _ = cut(temp, f0, H, 64)
        r_gt_dn, k0 = cut(Hn, j8, H, 64)
        g_o, k1 = cut(Hn, k0, H, 64)
        g_s, k2 = cut(Hn, k1, H, 64)
        g_th, k3 = cut(Hn, k2, H, 64)
        assert k3 <= KT * NTOK

        def lowest(t, nband):
            return t if nband == 2 and t == CT else t - 1

        v_ones, n0 = zip(cut(temp, 0, NT, P), cut(temp, NT * P, NT, P))
        m_pT, n1 = cut(temp, n0[1], 3, 512)
        m_rec, n2 = cut(temp, n1, 512)
        m_max, n3 = cut(temp, n2, 2, 4)
        assert n3 <= a8

        def latent_plan(L):
            units = []
            for h in range(H):
                units += ([(h, 0, NCTX, CT)] if L == 0 else []) + [(h, NCTX + 512 * c, NCTX + 512 * c + 512, NT) for c in range(2)]
            tiles = lambda u: [(("max"), u, t) for t in range((units[u][2] - units[u][1]) // P)]
            plan = tiles(0) + [("rows", 0, 0)]
            for u, (h, lo, hi, nk) in enumerate(units):
                ahead = tiles(u + 1) if u + 1 < len(units) else []
                for j in range(nk):
                    plan.append(("keys", u, j))
                    if j:
                        plan.append(("weigh", u, j - 1))
                    if ahead and j % 2 == 1:
                        plan.append(ahead.pop(0))
                plan += ahead
                if u + 1 < len(units):
                    plan.append(("rows", u + 1, 0))
                plan += [("weigh", u, nk - 1), ("done", u, 0)]
                if u + 1 < len(units) and units[u + 1][0] != h:
                    plan.append(("ada", 2 + h, 0))
            return units, plan

        block = ctx.enter_context(nc.Block())

        def start(lane):
            for n_, k_ in CREDITS[lane.name].items():
                lane.e.sem_inc(sems[n_], k_)

        def tokens(L):
            return SEGMENTS if L == 0 else SEGMENTS[1:]

        def tile_cols(t):
            return bass.ds(t * P, P)

        @block.sync
        def _(sp):
            for s in range(2):
                sp.dma_start(ring[:, s, :], d["weights"][s]).then_inc(sems[f"chunk_in_{s}"], 16)
            with sp.Fori(1, DEPTH * CHUNKS // 2) as i:
                for s in range(2):
                    sp.wait_ge(sems["chunk_used"], 2 * i - 1 + s)
                    sp.dma_start(ring[:, s, :], d["weights"][2 * i + s]).then_inc(sems[f"chunk_in_{s}"], 16)
            sp.wait_ge(sems["phase"], 4 * book.get("phases_old", 1))
            sp.dma_start(d["out"], X[:, :, NCTX:NTOK]).then_inc(sems["out_done"], 16)
            sp.wait_ge(sems["out_done"], 16)

        @block.tensor
        def _(pe):
            ln = Lane(pe, "pe", sems, book)
            start(ln)
            nth, tally = ln.nth, ln.tally
            state = {"chunk": 0, "ada": 0}

            def slot(j=0):
                return (state["chunk"] + j) % 2

            def arrived(j=0, i=None, per=0):
                n_ = state["chunk"] + j
                v = 16 * (n_ // 2 + 1)
                pe.wait_ge(sems[f"chunk_in_{n_ % 2}"], v if i is None else v + i * (8 * per))
                return ring[:, n_ % 2, :].rearrange("p (k n) -> p k n", k=KT)

            def turn(out, src, rows=P):
                return pe.transpose(out, src, ident[0:rows, 0:rows])

            def ada(L, v):
                if state["ada"] == 0:
                    pe.wait_ge(sems["silu_ready"], 1)
                for s_ in range(2):
                    w = arrived()
                    for j in range(4):
                        for k in range(KT):
                            m = pe.matmul(ps[:, 7, (s_ * 4 + j) * 2:(s_ * 4 + j) * 2 + 2], w[:, k, j * P:(j + 1) * P],
                                          silu_c[:, k, :], start=(k == 0), stop=(k == KT - 1))
                    m.then_inc(sems["chunk_used"], tally("chunk_used"))
                    state["chunk"] += 1
                pe.drain().then_inc(sems["ada_mm"], 1)
                state["ada"] += 1

            def ada_free():
                pe.wait_ge(sems["ada_sum"], state["ada"])

            def tile_products(widths, bank):
                pe.wait_ge(sems["tile_in"], nth("tile_in", 1, 1))
                for j, w_ in enumerate(widths):
                    w = ring[:, slot(j), :].rearrange("p (k n) -> p k n", k=KT)
                    for k in range(KT):
                        m = pe.matmul(ps[:, bank + j, 0:w_], tile_products.src[:, k, :], w[:, k, 0:w_],
                                      start=(k == 0), stop=(k == KT - 1))
                m.then_inc(sems["z_mm"], tally("z_mm"))

            def channel_products(n_out, src, cols, first_bank, count0, act_evac, release=True):
                w = arrived()
                n_ = count0
                for j in range(n_out):
                    for lo, hi in cols:
                        bank = first_bank + n_ % 4
                        act_evac(n_)
                        for k in range(KT):
                            m = pe.matmul(ps[:, bank, 0:hi - lo], w[:, k, j * P:(j + 1) * P], src[:, k, lo:hi],
                                          start=(k == 0), stop=(k == KT - 1))
                        m.then_inc(sems["prod"], tally("prod"))
                        n_ += 1
                if release:
                    pe.drain().then_inc(sems["chunk_used"], tally("chunk_used"))
                state["chunk"] += 1
                return n_

            def mla_prep(L):
                arrived()
                pe.wait_ge(sems["weights_in"], 32 * (L + 1))
                tile_products.src = hst
                with ln.loop(NT, [(n_, 1) for n_ in ("tile_in", "normed", "cT_sb", "qk_roped", "qkT_sb", "up_v")]):
                    tile_products([416], 0)
                    pe.wait_ge(sems["normed"], nth("normed", 1, 1))
                    for j in range(3):
                        m = turn(ps[:, 1, j * P:(j + 1) * P], zst[:, j * P:(j + 1) * P])
                    m.then_inc(sems["cT_mm"], tally("cT_mm"))
                    pe.wait_ge(sems["cT_sb"], nth("cT_sb", 1, 1))
                    for j in range(2):
                        pe.matmul(ps[:, 2, 0:384], m_cT[:, j, :], m_uq[:, j, :], start=(j == 0), stop=(j == 1))
                    pe.matmul(ps[:, 3, :], m_cT[:, 2, :], m_ukv, start=True, stop=True).then_inc(sems["up_mm"], tally("up_mm"))
                    pe.wait_ge(sems["qk_roped"], nth("qk_roped", 1, 1))
                    pe.wait_ge(sems["up_v"], nth("up_v", 1, 1))
                    for j in range(8):
                        m = turn(ps[0:96, 4 + j // 4, (j % 4) * P:(j % 4 + 1) * P], m_qk[:, j, :])
                    m.then_inc(sems["qkT_mm"], tally("qkT_mm"))
                    pe.wait_ge(sems["qkT_sb"], nth("qkT_sb", 1, 1))
                pe.drain().then_inc(sems["chunk_used"], tally("chunk_used"))
                state["chunk"] += 1

            def attend(count, heads, nk, keys, vals, qsrc, masks):
                rounds = [(r, min(4, nk - r)) for r in range(0, nk, 4)]
                nr = len(rounds)
                per = {"q_staged": 1, "rowmax": 4, "probs": 4, "pT_act": 4 * nr, "y_norm": 1, "yT_sb": 1}

                def body():
                    pe.wait_ge(sems["q_staged"], nth("q_staged", 1, 1))

                    def scores(h):
                        for out, lhs, rhs in keys(h, (h % 2) * 3):
                            m = pe.matmul(out, lhs, rhs, start=True, stop=True)
                        m.then_inc(sems["scores"], tally("scores"))

                    def weigh(h):
                        pe.wait_ge(sems["probs"], nth("probs", h + 1, 4))
                        for r, (r0, w_) in enumerate(rounds):
                            for j in range(w_):
                                m = turn(ps[:, 6, j * P:(j + 1) * P], p_sb[:, r0 + j, :])
                            m.then_inc(sems["pT_mm"], tally("pT_mm"))
                            pe.wait_ge(sems["pT_act"], nth("pT_act", h * nr + r + 1, 4 * nr))
                        for j in range(nk):
                            m = pe.matmul(ps[:, 7, h * 64:(h + 1) * 64], pT[h % 2][:, j, :], vals(h, j),
                                          start=(j == 0), stop=(j == nk - 1))
                        m.then_inc(sems["pv"], tally("pv"))

                    scores(0)
                    scores(1)
                    for h in range(H):
                        weigh(h)
                        if h + 2 < H:
                            scores(h + 2)
                    pe.wait_ge(sems["y_norm"], nth("y_norm", 1, 1))
                    for j in range(2):
                        m = turn(ps[:, 6, j * P:(j + 1) * P], yst[:, 2 * j:2 * j + 2, :].rearrange("p a b -> p (a b)"))
                    m.then_inc(sems["yT_mm"], tally("yT_mm"))
                    pe.wait_ge(sems["yT_sb"], nth("yT_sb", 1, 1))

                return body, per

            def run(count, make, first, looped=True):
                if looped:
                    with ln.loop(count) as i:
                        body, per = make(first + i)
                        body()
                else:
                    body, per = make(first)
                    body()
                for n_, k_ in per.items():
                    ln.passed(n_, k_ * count)

            def latent_attention(L):
                units, plan = latent_plan(L)
                n_max = n_keys = n_weigh = 0
                flat = ps[:, 0:3, :].rearrange("p a b -> p (a b)")
                fresh_ada = False
                for what, u, j in plan:
                    h, lo, hi, nk = units[u] if what != "ada" else units[0]
                    if what == "max":
                        if n_max:
                            pe.wait_ge(sems["rowmax"], nth("rowmax", n_max))
                        for c in range(0, nk * P, 512):
                            w_ = min(512, nk * P - c)
                            m = pe.matmul(flat[:, c:c + w_], m_q[0:96, h, lo + j * P:lo + (j + 1) * P], m_k[0:96, h, c:c + w_],
                                          start=True, stop=True)
                        m.then_inc(sems["scores"], tally("scores"))
                        n_max += 1
                    if what == "rows":
                        pe.wait_ge(sems["rowmax"], nth("rowmax", n_max))
                        if u:
                            pe.wait_ge(sems["maxrow"], nth("maxrow", u))
                        if fresh_ada:
                            ada_free()
                            fresh_ada = False
                        for t in range((hi - lo) // P):
                            m = turn(ps[0:1, 7, t * P:(t + 1) * P], m_max[:, u % 2, t:t + 1])
                        m.then_inc(sems["maxrow_mm"], tally("maxrow_mm"))
                    if what == "keys":
                        pe.wait_ge(sems["maxrow"], nth("maxrow", u + 1))
                        if n_keys == 0:
                            pe.wait_ge(sems["v_staged"], nth("v_staged", 1))
                        if n_keys >= 2:
                            pe.wait_ge(sems["exped"], nth("exped", n_keys - 1))
                        pe.matmul(ps[:, 3 + n_keys % 2, 0:hi - lo], m_k[0:97, h, j * P:(j + 1) * P], m_q[0:97, h, lo:hi],
                                  start=True, stop=True).then_inc(sems["keyed"], tally("keyed"))
                        n_keys += 1
                    if what == "weigh":
                        if j == 0:
                            pe.wait_ge(sems["v_staged"], nth("v_staged", h + 1))
                            if u >= 2:
                                pe.wait_ge(sems["y_done"], nth("y_done", u - 1))
                        pe.wait_ge(sems["exped"], nth("exped", n_weigh + 1))
                        pe.matmul(ps[:, 5 + u % 2, 0:hi - lo], v_ones[h % 2][:, j, :], m_pT[:, n_weigh % 3, 0:hi - lo],
                                  start=(j == 0), stop=(j == nk - 1)).then_inc(sems["weighed"], tally("weighed"))
                        n_weigh += 1
                    if what == "ada":
                        pe.wait_ge(sems["maxrow"], nth("maxrow", u_rows))
                        ada(L, u)
                        fresh_ada = True
                    if what == "rows":
                        u_rows = u + 1

            def swa_make(nk, nband):
                def make(t):
                    def keys(h, bank):
                        flat = ps[:, bank:bank + 3, :].rearrange("p a b -> p (a b)")
                        at_ = 64 * (h // 2)
                        q_ = qst[at_:at_ + 64, h % 2, :]
                        out = [(flat[:, 0:NCTX], q_, w_kT[at_:at_ + 64, 0:NCTX])]
                        for j in range(nband):
                            out.append((flat[:, (2 + j) * P:(3 + j) * P], q_, kst[at_:at_ + 64, j, :]))
                        return out

                    def vals(h, j):
                        c_ = slice(64 * (h // 2), 64 * (h // 2) + 64)
                        return w_v[:, j, c_] if j < 2 else w_v[:, lowest(t, nband) + (j - 2), c_]
                    return attend(1, H, nk, keys, vals, None, None)
                return make

            def swa_prep():
                arrived()
                tile_products.src = hst
                with ln.loop(NT, [(n_, 1) for n_ in ("tile_in", "qk_roped", "qkT_sb", "z_sb")]):
                    tile_products([512], 0)
                    pe.wait_ge(sems["qk_roped"], nth("qk_roped", 1, 1))
                    for j in range(3):
                        m = turn(ps[:, 1, j * P:(j + 1) * P], w_qk[:, j * P:(j + 1) * P])
                    m.then_inc(sems["qkT_mm"], tally("qkT_mm"))
                    pe.wait_ge(sems["z_sb"], nth("z_sb", 1, 1))
                    pe.wait_ge(sems["qkT_sb"], nth("qkT_sb", 1, 1))
                pe.drain().then_inc(sems["chunk_used"], tally("chunk_used"))
                state["chunk"] += 1

            def ret_forward():
                arrived()
                arrived(1)
                tile_products.src = hst
                with ln.loop(NT, [(n_, 1) for n_ in ("tile_in", "r_roped", "r_kT_sb", "r_kz", "r_state", "z_sb")]) as i:
                    tile_products([512, 256], 0)
                    pe.wait_ge(sems["r_roped"], nth("r_roped", 1, 1))
                    for j in range(2):
                        m = turn(ps[:, 2, j * P:(j + 1) * P], r_R[:, j, :])
                    m.then_inc(sems["r_kT_mm"], tally("r_kT_mm"))
                    pe.wait_ge(sems["r_kz"], nth("r_kz", 1, 1))
                    pe.wait_ge(sems["z_sb"], nth("z_sb", 1, 1))
                    pe.matmul(ps[:, 3, 0:256], r_kz, r_z[:, 256:512], start=True, stop=True).then_inc(sems["r_kv"], tally("r_kv"))
                    pe.wait_ge(sems["r_kT_sb"], nth("r_kT_sb", 1, 1))
                    pe.wait_ge(sems["r_state"], nth("r_state", 1, 1))
                m = pe.drain()
                m.then_inc(sems["chunk_used"], tally("chunk_used", 2))
                state["chunk"] += 2

            def gate_turn():
                pe.wait_ge(sems["g_y"], nth("g_y", 1, 1))
                for j in range(2):
                    m = turn(ps[:, 6, j * P:(j + 1) * P], r_gt_flat(j))
                m.then_inc(sems["yT_mm"], tally("yT_mm"))
                pe.wait_ge(sems["yT_sb"], nth("yT_sb", 1, 1))

            def r_gt_flat(j):
                return gate_turn.src[:, 2 * j:2 * j + 2, :].rearrange("p a b -> p (a b)")

            def ret_backward(count, first):
                with ln.loop(count, [(n_, 1) for n_ in ("r_stage", "r_probs", "r_kz", "r_o", "r_state", "g_y", "yT_sb")], down_from=first) as i:
                    t = ln.down
                    pe.wait_ge(sems["r_stage"], nth("r_stage", 1, 1))
                    for h in range(H):
                        rows = slice(32 * h, 32 * h + 32)
                        m = pe.matmul(ps[:, h, 0:P], r_qst[rows, 1, :], r_qst[rows, 0, :],
                                      start=True, stop=True)
                    m.then_inc(sems["r_scores"], tally("r_scores"))
                    pe.matmul(ps[:, 4, 0:256], r_qst[:, 2, :], r_S[:, t, :], start=True, stop=False, skip_group_check=True)
                    pe.matmul(ps[:, 4, 0:256], r_qst[:, 3, :], r_Sb, start=False, stop=False, skip_group_check=True)
                    pe.wait_ge(sems["r_probs"], nth("r_probs", 1, 1))
                    for h in range(H):
                        m = pe.matmul(ps[:, 4, h * 64:(h + 1) * 64], r_p[:, h, :], r_v[:, t, h * 64:(h + 1) * 64],
                                      start=False, stop=True, skip_group_check=True)
                    m.then_inc(sems["r_out"], tally("r_out"))
                    pe.wait_ge(sems["r_kz"], nth("r_kz", 1, 1))
                    pe.matmul(ps[:, 3, 0:256], r_kz, r_v[:, t, :], start=True, stop=True).then_inc(sems["r_kv"], tally("r_kv"))
                    pe.wait_ge(sems["r_o"], nth("r_o", 1, 1))
                    pe.wait_ge(sems["r_state"], nth("r_state", 1, 1))
                    gate_turn()

            def dn_project():
                def before(n_):
                    if n_ >= 4:
                        pe.wait_ge(sems["evac_act" if n_ % 2 == 0 else "evac_dve"], nth("evac_act" if n_ % 2 == 0 else "evac_dve", (n_ - 4) // 2 + 1))
                n_ = channel_products(3, Hm, SEGMENTS, 0, 0, before)
                n_ = channel_products(3, Hm, SEGMENTS, 0, n_, before, release=False)
                ln.passed("evac_act", 9)
                ln.passed("evac_dve", 9)
                arrived()
                tile_products.src = d_hst
                with ln.loop(NT, [("tile_in", 1), ("z_sb", 1)]):
                    tile_products([272], 4)
                    pe.wait_ge(sems["z_sb"], nth("z_sb", 1, 1))
                state["chunk"] += 1

            def dn_norm():
                with ln.loop(NT, [(n_, 1) for n_ in ("d_stage", "d_norm", "d_kTs", "d_v")]):
                    pe.wait_ge(sems["d_stage"], nth("d_stage", 1, 1))
                    for j in range(6):
                        m = turn(ps[:, j // 4, (j % 4) * P:(j % 4 + 1) * P], d_st[:, j, :])
                    m.then_inc(sems["d_tok"], tally("d_tok"))
                    pe.wait_ge(sems["d_norm"], nth("d_norm", 1, 1))
                    for j in range(4):
                        m = turn(ps[:, 2, j * P:(j + 1) * P], d_n[:, 2 * j:2 * j + 2, :].rearrange("p a b -> p (a b)"))
                    m.then_inc(sems["d_kT"], tally("d_kT"))
                    pe.wait_ge(sems["d_v"], nth("d_v", 1, 1))
                    pe.wait_ge(sems["d_kTs"], nth("d_kTs", 1, 1))

            def dn_scan(count, first, last):
                names = ("u_stage", "u_arg", "u_inv", "u_keg", "u_wsb", "u_vsb", "u_done", "u_dt", "u_gc")
                sig = [(f"{n_}{q}", 1) for n_ in names for q in range(2)]
                sig += [(f"u_tsb{q}", 6) for q in range(2)]
                sig += [(f"u_ysb{q}", 6) for q in range(2)] + [(f"u_usb{q}", 6) for q in range(2)]
                with ln.loop(count, sig, down_from=last) as i:
                    tt = (first + i, ln.down)
                    for q in range(2):
                        b, A, B, C, D = sc[q], *(ps[:, 4 * q + z, :] for z in range(4))
                        pe.wait_ge(sems[f"u_done{q}"], nth(f"u_done{q}", 1, 1))
                        pe.wait_ge(sems[f"u_stage{q}"], nth(f"u_stage{q}", 1, 1))
                        pe.matmul(A, ones, b["gm"].rearrange("p a b -> p (a b)"), start=True, stop=True)
                        lg = d_lg[:, tt[q], 4 * q:4 * q + 4]
                        pe.matmul(D[:, 0:4], tri[:, q, :], lg, start=True, stop=True)
                        pe.matmul(D[:, 4:8], ones, lg, start=True, stop=True).then_inc(sems[f"u_g{q}"], tally(f"u_g{q}"))
                        for h in range(H):
                            rows = slice(64 * (h % 2), 64 * (h % 2) + 64)
                            kk = b["qk"][rows, 2 + h // 2, :]
                            out = (B, C)[h % 2].rearrange("p (a j c) -> p a j c", a=2, j=2)[:, :, h // 2, :]
                            pe.matmul(out[:, 0, :], kk, kk, start=True, stop=True)
                            m = pe.matmul(out[:, 1, :], kk, b["qk"][rows, h // 2, :], start=True, stop=True)
                        m.then_inc(sems[f"u_gram{q}"], tally(f"u_gram{q}"))
                    for lv in range(LEVELS):
                        for q in range(2):
                            b, A, B, C, D = sc[q], *(ps[:, 4 * q + z, :] for z in range(4))
                            if lv == 0:
                                pe.wait_ge(sems[f"u_inv{q}"], nth(f"u_inv{q}", 1, 1))
                            else:
                                pe.wait_ge(sems[f"u_tsb{q}"], nth(f"u_tsb{q}", lv, 6))
                                for h in range(H):
                                    m = pe.matmul(B[:, h * P:(h + 1) * P], b["at"][:, h, :], b["dt"][:, h, :],
                                                  start=True, stop=True)
                                m.then_inc(sems[f"u_ymm{q}"], tally(f"u_ymm{q}"))
                        for q in range(2):
                            b, A, B, C, D = sc[q], *(ps[:, 4 * q + z, :] for z in range(4))
                            if lv:
                                pe.wait_ge(sems[f"u_ysb{q}"], nth(f"u_ysb{q}", lv, 6))
                                for h in range(H):
                                    m = pe.matmul(C[:, h * P:(h + 1) * P], b["ym"][:, h, :], b["u"][:, h, :],
                                                  start=True, stop=True)
                                m.then_inc(sems[f"u_umm{q}"], tally(f"u_umm{q}"))
                        for q in range(2):
                            b, A, B, C, D = sc[q], *(ps[:, 4 * q + z, :] for z in range(4))
                            if lv:
                                pe.wait_ge(sems[f"u_usb{q}"], nth(f"u_usb{q}", lv, 6))
                            if lv < LEVELS - 1:
                                for h in range(H):
                                    m = turn(A[:, h * P:(h + 1) * P], b["u"][:, h, :])
                                m.then_inc(sems[f"u_tmm{q}"], tally(f"u_tmm{q}"))
                    for q in range(2):
                        b, A, B, C, D = sc[q], *(ps[:, 4 * q + z, :] for z in range(4))
                        pe.wait_ge(sems[f"u_keg{q}"], nth(f"u_keg{q}", 1, 1))
                        for h in range(H):
                            r0 = 64 * (h % 2)
                            m = pe.matmul(D[r0:r0 + 64, (h // 2) * P:(h // 2 + 1) * P], b["keg"][:, h * 64:(h + 1) * 64],
                                          b["u"][:, h, :], start=True, stop=True)
                        m.then_inc(sems[f"u_wmm{q}"], tally(f"u_wmm{q}"))
                    for q in range(2):
                        b, A, B, C, D = sc[q], *(ps[:, 4 * q + z, :] for z in range(4))
                        for h in range(H):
                            pe.matmul(B[:, h * 64:(h + 1) * 64], b["u"][:, h, :], kv_tok[:, tt[q], 256 + h * 64:320 + h * 64],
                                      start=(h == 0), stop=False, skip_group_check=True)
                        pe.wait_ge(sems[f"u_wsb{q}"], nth(f"u_wsb{q}", 1, 1))
                        for j in range(2):
                            m = pe.matmul(B[:, j * P:(j + 1) * P], b["wt"][:, j * P:(j + 1) * P], b["S"][:, j, :],
                                          start=False, stop=True, skip_group_check=True)
                        m.then_inc(sems[f"u_vmm{q}"], tally(f"u_vmm{q}"))
                    for q in range(2):
                        b, A, B, C, D = sc[q], *(ps[:, 4 * q + z, :] for z in range(4))
                        for j in range(2):
                            pe.matmul(C[:, j * P:(j + 1) * P], b["qk"][:, j, :], b["S"][:, j, :],
                                      start=(j == 0), stop=True, skip_group_check=True)
                        pe.wait_ge(sems[f"u_vsb{q}"], nth(f"u_vsb{q}", 1, 1))
                        for h in range(H):
                            pe.matmul(C[:, 256 + h * 64:320 + h * 64], b["qkd"][:, h, :], b["vn"][:, h * 64:(h + 1) * 64],
                                      start=False, stop=True, skip_group_check=True)
                        for j in range(2):
                            m = pe.matmul(A[:, j * P:(j + 1) * P], b["kt"][:, j * P:(j + 1) * P],
                                          b["vn"][:, j * P:(j + 1) * P], start=True, stop=True)
                        m.then_inc(sems[f"u_omm{q}"], tally(f"u_omm{q}"))

            def dn_out(count):
                gate_turn.src = r_gt_dn
                with ln.loop(count, [("g_y", 1), ("yT_sb", 1)]):
                    gate_turn()

            def project_out(L):
                def before(n_):
                    if n_ >= 4:
                        pe.wait_ge(sems["evac_dve"], nth("evac_dve", n_ - 3))
                n_ = channel_products(4, Y, tokens(L), 0, 0, before)
                n_ = channel_products(4, Y, tokens(L), 0, n_, before)
                ln.passed("evac_dve", n_)

            def mlp(L):
                cols = tokens(L)
                g = 8 * len(cols)
                with ln.loop(FG, [("relu", g), ("sq_done", g), ("evac_dve", g)]) as i:
                    n_ = 0
                    for s in range(4):
                        if s == 2:
                            pe.wait_ge(sems["sq_done"], nth("sq_done", g, g))
                            n_ = 0
                        w = arrived(s, i, 4)
                        for j in range(4):
                            for lo, hi in cols:
                                if s < 2:
                                    if n_ >= 4:
                                        pe.wait_ge(sems["relu"], nth("relu", n_ - 3, g))
                                    bank, src = n_ % 4, Hm
                                else:
                                    if n_ >= 4:
                                        pe.wait_ge(sems["evac_dve"], nth("evac_dve", n_ - 3, g))
                                    bank, src = 4 + n_ % 4, Y
                                for k in range(KT):
                                    m = pe.matmul(ps[:, bank, 0:hi - lo], w[:, k, j * P:(j + 1) * P], src[:, k, lo:hi],
                                                  start=(k == 0), stop=(k == KT - 1))
                                m.then_inc(sems["prod"], tally("prod"))
                                n_ += 1
                        pe.drain().then_inc(sems["chunk_used"], tally("chunk_used"))
                    pe.wait_ge(sems["evac_dve"], nth("evac_dve", g, g))
                state["chunk"] += 4 * FG

            def layer_norm(L):
                for name, src in (("ln_mean", X), ("ln_var", Hm)):
                    for c, (lo, hi) in enumerate(tokens(L)):
                        if name == "ln_var":
                            pe.wait_ge(sems["ln_square"], nth("ln_square", c + 1))
                        for k in range(KT):
                            m = pe.matmul(ps[:, c + (3 if name == "ln_var" else 0), 0:hi - lo], mean_w, src[:, k, lo:hi],
                                          start=(k == 0), stop=(k == KT - 1))
                        m.then_inc(sems[name], tally(name))
                ln.passed("ln_square", len(tokens(L)))

            pe.wait_ge(sems["consts_in"], 32)
            for L in range(DEPTH):
                ln.barrier()
                if L == 0:
                    ada(0, 0)
                    ada_free()
                    ada(0, 1)
                ln.barrier()
                ln.barrier()
                mla_prep(L)
                ln.barrier()
                latent_attention(L)
                ln.barrier()
                ln.barrier()
                ret_forward()
                ln.barrier()
                ada(L, 5)
                gate_turn.src = r_gt
                ret_backward(CT, CT - 1)
                ret_backward(NT - CT, NT - 1)
                ln.barrier()
                swa_prep()
                ln.barrier()
                if L == 0:
                    ada(1, 0)
                    run(CT, swa_make(2, 0), 0)
                run(1, swa_make(4, 2), CT, False)
                run(NT - CT - 2, swa_make(5, 3), CT + 1)
                run(1, swa_make(4, 2), NT - 1, False)
                ln.barrier()
                dn_project()
                ln.barrier()
                ln.barrier()
                dn_norm()
                ln.barrier()
                dn_scan(CT, 0, CT - 1)
                dn_scan(NT - CT, CT, NT - 1)
                ln.barrier()
                pe.drain().then_inc(sems["chunk_used"], tally("chunk_used", 2))
                dn_out(NT)
                ln.barrier()
                project_out(L)
                ln.barrier()
                if L == 0:
                    ada(1, 1)
                layer_norm(L)
                ln.barrier()
                ln.barrier()
                mlp(L)
                ln.barrier()
                layer_norm(L)
                ln.barrier()

        @block.scalar
        def _(act):
            ln = Lane(act, "act", sems, book)
            start(ln)
            nth, tally = ln.nth, ln.tally
            A = act.activation

            def flat(ap):
                return ap.rearrange("p a b -> p (a b)")

            def silu_conditions():
                A(flat(silu_c[:]), flat(cc[:]), ACT.Tanh, scale=0.5).then_inc(sems["silu_c"], 1)

            def modulate(L, shift, scale):
                mod = mods[:, L]
                with ln.loop(KT) as k:
                    A(Hm[:, k, NCTX:NTOK], X[:, k, NCTX:NTOK], ACT.Identity, bias=mod[:, shift + k, 0:1],
                          scale=mod[:, scale + k, 0:1]).then_inc(sems["h_lat"], tally("h_lat"))

            def mla_prep():
                with ln.loop(NT, [(n_, 1) for n_ in ("z_mm", "cT_mm", "up_mm", "qkT_mm")]) as i:
                    act.wait_ge(sems["z_mm"], nth("z_mm", 1, 1))
                    ln.link(A(zst[:, 0:416], ps[:, 0, 0:416], ACT.Copy))
                    A(m_sq[:, 0:256], zst[:, 0:256], ACT.Square, accum_out=ss[:, 0:1])
                    ln.link(A(m_sq[:, 256:384], zst[:, 256:384], ACT.Square, accum_out=ss[:, 1:2]))
                    act.sem_inc(sems["ss"], tally("ss"))
                    act.wait_ge(sems["cT_mm"], nth("cT_mm", 1, 1))
                    for j in range(3):
                        g_ = par["q_norm"][:, j:j + 1] if j < 2 else par["kv_norm"]
                        m = A(m_cT[:, j, :], ps[:, 1, j * P:(j + 1) * P], ACT.Copy, scale=g_)
                    m.then_inc(sems["cT_sb"], tally("cT_sb"))
                    act.wait_ge(sems["up_mm"], nth("up_mm", 1, 1))
                    A(m_qk[:, 4:8, 0:64], ps[:, 3, :].rearrange("p (h c) -> p h c", h=H)[:, :, 0:64], ACT.Copy)
                    A(m_v[:, i, :].rearrange("p (h c) -> p h c", h=H),
                          ps[:, 3, :].rearrange("p (h c) -> p h c", h=H)[:, :, 64:128], ACT.Copy).then_inc(sems["up_v"], tally("up_v"))
                    act.wait_ge(sems["qkT_mm"], nth("qkT_mm", 1, 1))
                    A(m_q[0:96, :, tile_cols(i)], ps[0:96, 4, :].rearrange("p (h c) -> p h c", h=H), ACT.Copy)
                    A(m_k[0:96, :, tile_cols(i)], ps[0:96, 5, :].rearrange("p (h c) -> p h c", h=H), ACT.Copy).then_inc(sems["qkT_sb"], tally("qkT_sb"))

            def attend(nk, scale, sink, rows, t):
                rounds = [(r, min(4, nk - r)) for r in range(0, nk, 4)]
                nr = len(rounds)
                per = {"rowmax": 4, "pT_mm": 4 * nr, "yT_mm": 1, "pv": 4, "den": 0}

                def exp(h):
                    act.wait_ge(sems["rowmax"], nth("rowmax", h + 1, 4))
                    src = ps[:, 3 * (h % 2):3 * (h % 2) + 3, :].rearrange("p a b -> p (a b)")[:, 0:nk * P]
                    if sink:
                        A(esink[:, h:h + 1], par["sink"][:, h:h + 1], ACT.Exp, bias=rowneg[:, h:h + 1])
                    A(p_sb[:, 0:nk, :].rearrange("p a b -> p (a b)"), src, ACT.Exp, bias=rowneg[:, h:h + 1],
                          scale=scale, accum_out=den[:, h:h + 1]).then_inc(sems["probs"], tally("probs"))

                def body():
                    for h in range(H):
                        if h:
                            act.wait_ge(sems["pT_mm"], nth("pT_mm", h * nr, 4 * nr))
                        exp(h)
                        for r, (r0, w_) in enumerate(rounds):
                            act.wait_ge(sems["pT_mm"], nth("pT_mm", h * nr + r + 1, 4 * nr))
                            if r == 0 and h >= 2:
                                act.wait_ge(sems["pv"], nth("pv", h - 1, 4))
                            A(pT[h % 2][:, r0:r0 + w_, :].rearrange("p a b -> p (a b)"), ps[:, 6, 0:w_ * P], ACT.Copy).then_inc(sems["pT_act"], tally("pT_act"))
                    act.wait_ge(sems["yT_mm"], nth("yT_mm", 1, 1))
                    A(Y[:, rows:rows + 2, tile_cols(t)], ps[:, 6, 0:256].rearrange("p (a b) -> p a b", a=2), ACT.Copy).then_inc(sems["yT_sb"], tally("yT_sb"))
                return body, per

            def run(count, nk, scale, sink, rows, first, looped=True):
                if looped:
                    with ln.loop(count) as i:
                        body, per = attend(nk, scale, sink, rows, first + i)
                        body()
                else:
                    body, per = attend(nk, scale, sink, rows, first)
                    body()
                for n_, k_ in per.items():
                    ln.passed(n_, k_ * count)

            def latent_attention(L):
                units, plan = latent_plan(L)
                n_ = 0
                for what, u, j in plan:
                    if what == "keys":
                        h, lo, hi, nk = units[u]
                        act.wait_ge(sems["keyed"], nth("keyed", n_ + 1))
                        if n_ >= 3:
                            act.wait_ge(sems["weighed"], nth("weighed", n_ - 2))
                        A(m_pT[:, n_ % 3, 0:hi - lo], ps[:, 3 + n_ % 2, 0:hi - lo], ACT.Exp, scale=96 ** -0.5)\
                            .then_inc(sems["exped"], tally("exped"))
                        n_ += 1

            def swa_prep():
                with ln.loop(NT, [("z_mm", 1), ("qkT_mm", 1)]) as i:
                    act.wait_ge(sems["z_mm"], nth("z_mm", 1, 1))
                    A(zst[:, 0:512], ps[:, 0, :], ACT.Copy).then_inc(sems["z_sb"], tally("z_sb"))
                    act.wait_ge(sems["qkT_mm"], nth("qkT_mm", 1, 1))
                    A(w_qT[:, :, tile_cols(i)], ps[:, 1, 0:256].rearrange("p (a b) -> p a b", a=2), ACT.Copy)
                    A(w_kT[:, tile_cols(i)], ps[:, 1, 256:384], ACT.Copy).then_inc(sems["qkT_sb"], tally("qkT_sb"))

            def ret_tables():
                ln.link(A(lg_ret, par["log1m"], ACT.Exp))
                A(lg_row, par["log1m_row"], ACT.Exp).then_inc(sems["tables"], tally("tables"))
                act.wait_ge(sems["sk"], nth("sk", 1))
                A(lg_ret, lg_ret, ACT.Ln)
                ln.link(A(lg_row, lg_row, ACT.Ln))
                for q in range(2):
                    for h in range(H):
                        A(r_qst[:, h, :] if q == 0 else r_p[:, h, :], rel[:, q, :], ACT.Exp, scale=lg_ret[:, 4 * q + h:4 * q + h + 1])
                    A(zeta[:, q, :], lg_ret[:, 4 * q:4 * q + 4], ACT.Exp, scale=cst["left"][:, q:q + 1])
                    A(r_xi[:, q, :], age[:, q, :], ACT.Exp, scale=lg_row[:, q:q + 1])
                    m = A(gch[:, q:q + 1], lg_row[:, q:q + 1], ACT.Exp, scale=float(P))
                m.then_inc(sems["tables"], tally("tables"))
                ln.passed("sk", 1)

            def ret_forward():
                with ln.loop(NT, [(n_, 1) for n_ in ("z_mm", "r_kT_mm", "r_roped", "r_kv")]) as i:
                    act.wait_ge(sems["z_mm"], nth("z_mm", 1, 1))
                    A(r_z[:, 0:512], ps[:, 0, :], ACT.Copy)
                    ln.link(A(r_z[:, 512:768], ps[:, 1, 0:256], ACT.Copy))
                    act.sem_inc(sems["z_sb"], tally("z_sb"))
                    A(r_v[:, i, :], r_z[:, 256:512], ACT.Copy)
                    A(r_g[:, i, :], r_z[:, 512:768], ACT.Copy)
                    act.wait_ge(sems["r_roped"], nth("r_roped", 1, 1))
                    A(r_k[:, i, :], r_R[:, 1, :], ACT.Copy)
                    act.wait_ge(sems["r_kT_mm"], nth("r_kT_mm", 1, 1))
                    A(r_qkT[:, 0, tile_cols(i)], ps[:, 2, 0:P], ACT.Copy, scale=float(32 ** -0.5))
                    A(r_qkT[:, 1, tile_cols(i)], ps[:, 2, P:2 * P], ACT.Copy).then_inc(sems["r_kT_sb"], tally("r_kT_sb"))
                    act.wait_ge(sems["r_kv"], nth("r_kv", 1, 1))

            def gate(z, t, rows):
                A(gate.th.rearrange("p a b -> p (a b)"), z, ACT.Tanh, scale=0.5).then_inc(sems["g_tanh"], tally("g_tanh"))
                act.wait_ge(sems["yT_mm"], nth("yT_mm", 1, 1))
                A(Y[:, rows:rows + 2, tile_cols(t)], ps[:, 6, 0:256].rearrange("p (a b) -> p a b", a=2), ACT.Copy).then_inc(sems["yT_sb"], tally("yT_sb"))

            def ret_backward(count, first):
                with ln.loop(count, [(n_, 1) for n_ in ("r_centred", "yT_mm")], down_from=first) as i:
                    t = ln.down
                    act.wait_ge(sems["r_centred"], nth("r_centred", 1, 1))
                    A(flat(r_sq), flat(r_o), ACT.Square).then_inc(sems["g_sq"], tally("g_sq"))
                    gate.th = r_th
                    gate(r_g[:, t, :], t, 4)

            def dn_project():
                for n_ in range(0, 18, 2):
                    j, (lo, hi) = n_ // 3, SEGMENTS[n_ % 3]
                    act.wait_ge(sems["prod"], nth("prod", n_ + 1))
                    off = 2 if lo < NCTX else 6
                    A(raw[:, j, lo + off:hi + off], ps[:, n_ % 4, 0:hi - lo], ACT.Copy).then_inc(sems["evac_act"], tally("evac_act"))
                ln.passed("prod", 18)
                with ln.loop(NT, [("z_mm", 1)]) as i:
                    act.wait_ge(sems["z_mm"], nth("z_mm", 1, 1))
                    A(d_z[:, i, :], ps[:, 4, 0:256], ACT.Copy)
                    A(d_ab[:, i, :], ps[:, 4, 256:272], ACT.Copy).then_inc(sems["z_sb"], tally("z_sb"))

            def dn_gates_():
                ab = d_ab.rearrange("p t (q a h) -> p t q a h", q=2, a=2)
                act.wait_ge(sems["dn_gates"], nth("dn_gates", 1))
                A(nega, par["a_log"], ACT.Exp)
                ln.link(A(flat(d_w), flat(d_w), ACT.Exp))
                for q in range(2):
                    m = A(d_bt[:, :, 4 * q:4 * q + 4], ab[:, :, q, 1, :], ACT.Tanh, scale=0.5)
                m.then_inc(sems["dn_gates2"], tally("dn_gates2"))
                act.wait_ge(sems["dn_gates"], nth("dn_gates", 2))
                A(flat(d_w), flat(d_w), ACT.Ln).then_inc(sems["dn_gates2"], tally("dn_gates2"))
                ln.passed("dn_gates", 2)

            def dn_conv():
                with ln.loop(6, [("c_y", 1)]):
                    act.wait_ge(sems["c_y"], nth("c_y", 1, 1))
                    A(cv_t, cv_y, ACT.Tanh, scale=0.5).then_inc(sems["c_tanh"], tally("c_tanh"))

            def dn_norm():
                with ln.loop(NT, [(n_, 1) for n_ in ("d_tok", "d_kT", "d_norm")]) as i:
                    act.wait_ge(sems["d_tok"], nth("d_tok", 1, 1))
                    A(flat(d_sq), ps[:, 0, :], ACT.Square).then_inc(sems["d_sq"], tally("d_sq"))
                    A(kv_tok[:, i, 256:512], ps[:, 1, 0:256], ACT.Copy, scale=0.5).then_inc(sems["d_v"], tally("d_v"))
                    act.wait_ge(sems["d_norm"], nth("d_norm", 1, 1))
                    A(kv_tok[:, i, 0:256], d_n[:, 4:8, :].rearrange("p a b -> p (a b)"), ACT.Copy)
                    act.wait_ge(sems["d_kT"], nth("d_kT", 1, 1))
                    A(raw[:, 0:4, tile_cols(i)], ps[:, 2, :].rearrange("p (a b) -> p a b", a=4), ACT.Copy).then_inc(sems["d_kTs"], tally("d_kTs"))

            def dn_scan(count, first, last):
                sig = [(f"{n_}{q}", 1) for n_ in ("u_arg", "u_wmm", "u_e") for q in range(2)] + [(f"u_tmm{q}", 6) for q in range(2)]
                with ln.loop(count, sig, down_from=last) as i:
                    for q in range(2):
                        b = sc[q]
                        act.wait_ge(sems[f"u_arg{q}"], nth(f"u_arg{q}", 1, 1))
                        A(egt[q], tl[q], ACT.Exp)
                        A(flat(b["dt"]), flat(b["dt"]), ACT.Exp).then_inc(sems[f"u_dt{q}"], tally(f"u_dt{q}"))
                    for lv in range(LEVELS - 1):
                        for q in range(2):
                            act.wait_ge(sems[f"u_tmm{q}"], nth(f"u_tmm{q}", lv + 1, 6))
                            A(flat(sc[q]["dt"]), ps[:, 4 * q, :], ACT.Copy).then_inc(sems[f"u_tsb{q}"], tally(f"u_tsb{q}"))
                    for q in range(2):
                        act.wait_ge(sems[f"u_wmm{q}"], nth(f"u_wmm{q}", 1, 1))
                        A(sc[q]["wt"], ps[:, 4 * q + 3, 0:256], ACT.Copy, scale=-1.0).then_inc(sems[f"u_wsb{q}"], tally(f"u_wsb{q}"))

            def dn_out(count):
                with ln.loop(count, [("yT_mm", 1), ("g_row", 1)]) as i:
                    act.wait_ge(sems["g_row"], nth("g_row", 1, 1))
                    A(flat(g_s), d_o[:, i, :], ACT.Square).then_inc(sems["g_sq"], tally("g_sq"))
                    gate.th = g_th
                    gate(d_z[:, i, :], i, 2)

            def mlp(L):
                cols = tokens(L)
                g = 8 * len(cols)
                with ln.loop(FG, [("prod", 2 * g), ("sq_done", g)]):
                    for n_ in range(g):
                        w_ = cols[n_ % len(cols)][1] - cols[n_ % len(cols)][0]
                        act.wait_ge(sems["prod"], nth("prod", n_ + 1, 2 * g))
                        if n_ >= 4:
                            act.wait_ge(sems["sq_done"], nth("sq_done", n_ - 3, g))
                        A(relu_sb[:, n_ % 4, 0:w_], ps[:, n_ % 4, 0:w_], ACT.Relu).then_inc(sems["relu"], tally("relu"))
                    act.wait_ge(sems["sq_done"], nth("sq_done", g, g))

            def layer_norm(L, g_, b_):
                for c, (lo, hi) in enumerate(tokens(L)):
                    act.wait_ge(sems["ln_centred"], nth("ln_centred", c + 1))
                    A(Hm[:, :, lo:hi], X[:, :, lo:hi], ACT.Square).then_inc(sems["ln_square"], tally("ln_square"))
                for c, (lo, hi) in enumerate(tokens(L)):
                    act.wait_ge(sems["ln_veps"], nth("ln_veps", c + 1))
                    A(ln_r[:, c, 0:hi - lo], ln_r[:, c, 0:hi - lo], ACT.Sqrt).then_inc(sems["ln_root"], tally("ln_root"))
                for c, (lo, hi) in enumerate(tokens(L)):
                    act.wait_ge(sems["ln_scaled"], nth("ln_scaled", c + 1))
                    for k in range(KT):
                        A(X[:, k, lo:hi], X[:, k, lo:hi], ACT.Identity, bias=par[b_][:, k:k + 1], scale=par[g_][:, k:k + 1])
                ln.passed("ln_centred", len(tokens(L)))
                ln.passed("ln_scaled", len(tokens(L)))

            act.dma_start(consts[:], d["consts"]).then_inc(sems["consts_in"], 16)
            act.dma_start(ada_b[:], d["ada_b"]).then_inc(sems["consts_in"], 16)
            act.dma_start(cc[:], d["cc"]).then_inc(sems["x_in"], 16)
            act.dma_start(X[:], d["x"]).then_inc(sems["x_in"], 16)
            act.wait_ge(sems["x_in"], 32)
            for L in range(DEPTH):
                act.dma_start(params[:], d["params"][L]).then_inc(sems["params_in"], 16)
                act.wait_ge(sems["params_in"], 16 * (L + 1))
                ln.barrier()
                if L == 0:
                    silu_conditions()
                ln.barrier()
                modulate(L, SH1, SC1)
                act.dma_start(m_uq, d["w_uq"][L]).then_inc(sems["weights_in"], 16)
                act.dma_start(m_ukv, d["w_ukv"][L]).then_inc(sems["weights_in"], 16)
                ln.barrier()
                mla_prep()
                ln.barrier()
                latent_attention(L)
                ln.barrier()
                ret_tables()
                ln.barrier()
                ret_forward()
                ln.barrier()
                ret_backward(CT, CT - 1)
                ret_backward(NT - CT, NT - 1)
                ln.barrier()
                swa_prep()
                ln.barrier()
                if L == 0:
                    run(CT, 2, 0.125, True, 0, 0)
                run(1, 4, 0.125, True, 0, CT, False)
                run(NT - CT - 2, 5, 0.125, True, 0, CT + 1)
                run(1, 4, 0.125, True, 0, NT - 1, False)
                ln.barrier()
                dn_project()
                ln.barrier()
                act.dma_start(Hn[:, j0:j1], d["levels"]).then_inc(sems["masks_in"], 16)
                dn_gates_()
                dn_conv()
                ln.barrier()
                dn_norm()
                ln.barrier()
                act.wait_ge(sems["masks_in"], 16 * (L + 1))
                dn_scan(CT, 0, CT - 1)
                dn_scan(NT - CT, CT, NT - 1)
                ln.barrier()
                dn_out(NT)
                ln.barrier()
                ln.barrier()
                layer_norm(L, "ln1_g", "ln1_b")
                ln.barrier()
                modulate(L, SH2, SC2)
                ln.barrier()
                mlp(L)
                ln.barrier()
                layer_norm(L, "ln2_g", "ln2_b")
                ln.barrier()

        @block.vector
        def _(dve):
            ln = Lane(dve, "dve", sems, book)
            start(ln)
            nth, tally, link = ln.nth, ln.tally, ln.link
            state = {"ada": 0}
            TT, TS, STT = dve.tensor_tensor, dve.tensor_scalar, dve.scalar_tensor_tensor

            def flat(ap):
                return ap.rearrange("p a b -> p (a b)")

            def ada(L, v):
                if state["ada"] == 0:
                    dve.wait_ge(sems["silu_c"], 1)
                    link(STT(silu_c[:], silu_c[:], 1.0, cc[:], ALU.add, ALU.mult))
                    dve.sem_inc(sems["silu_ready"], 1)
                state["ada"] += 1
                dve.wait_ge(sems["ada_mm"], state["ada"])
                out = mods[:, L, 8 * v:8 * v + 8, :]
                m = STT(out, ps[:, 7, 0:16].rearrange("p (a b) -> p a b", b=2), 0.5, spread(ada_b[:, L, 8 * v:8 * v + 8], 2, 2),
                        ALU.mult, ALU.add)
                if v in (1, 4):
                    link(m)
                    m = TS(out, out, 1.0, None, ALU.add)
                m.then_inc(sems["ada_sum"], 1)

            def modulate(L, shift, scale):
                mod = mods[:, L]
                for k in range(KT):
                    link(TS(Hm[:, k, 0:NCTX], X[:, k, 0:NCTX], mod[:, scale + k, 1:2], mod[:, shift + k, 1:2], ALU.mult, ALU.add))
                    dve.wait_ge(sems["h_lat"], nth("h_lat", k + 1))
                    TS(X[:, k, :], X[:, k, :], ALPHA, None, ALU.mult)

            def rotate(x, a_, b_, cos, sin, out, n):
                heads = x.shape[1]
                c_ = spread(spread(cos, 1, 2), 1, heads)
                s_ = spread(spread(sin, 1, 2), 1, heads)
                TT(a_, x, c_, ALU.mult)
                link(TT(b_, x, s_, ALU.mult))
                TT(out[:, :, 0, :], a_[:, :, 0, :], b_[:, :, 1, :], ALU.subtract)
                return TT(out[:, :, 1, :], b_[:, :, 0, :], a_[:, :, 1, :], ALU.add)

            def mla_prep():
                halves = lambda ap: ap.rearrange("p h (a c) -> p h a c", a=2)
                with ln.loop(NT, [(n_, 1) for n_ in ("ss", "rstd", "up_mm", "qkT_mm", "up_v")]) as i:
                    dve.wait_ge(sems["ss"], nth("ss", 1, 1))
                    TS(rs[:, 0:1], ss[:, 0:1], 1.0 / 256, EPS, ALU.mult, ALU.add)
                    TS(rs[:, 1:2], ss[:, 1:2], 1.0 / 128, EPS, ALU.mult, ALU.add).then_inc(sems["veps"], tally("veps"))
                    dve.wait_ge(sems["rstd"], nth("rstd", 1, 1))
                    TS(zst[:, 0:256], zst[:, 0:256], rs2[:, 0:1], None, ALU.mult)
                    TS(zst[:, 256:384], zst[:, 256:384], rs2[:, 1:2], None, ALU.mult).then_inc(sems["normed"], tally("normed"))
                    dve.wait_ge(sems["up_mm"], nth("up_mm", 1, 1))
                    TS(m_qk[:, 0:4, :], ps[:, 2, 0:384].rearrange("p (h c) -> p h c", h=H), 1.0, None, ALU.mult)
                    link(TS(m_qk[:, 4:8, 64:96], spread(zst[:, 384:416], 1, H), 1.0, None, ALU.mult))
                    x = halves(m_qk[:, :, 64:96])
                    rotate(x, halves(m_a), halves(m_b), rope[:, i, 96:112], rope[:, i, 112:128], x, 16).then_inc(sems["qk_roped"], tally("qk_roped"))
                    dve.wait_ge(sems["qkT_mm"], nth("qkT_mm", 1, 1))

            def attend(nk, scale, sink, masks):
                per = {"scores": 4, "pv": 4, "probs": 4, "yT_mm": 1}

                def row_max(h):
                    flatps = ps[:, 3 * (h % 2):3 * (h % 2) + 3, :].rearrange("p a b -> p (a b)")
                    dve.wait_ge(sems["scores"], nth("scores", h + 1, 4))
                    for j, side in masks:
                        s_ = flatps[:, j * P:(j + 1) * P]
                        m = TT(s_, s_, window[:, side, :], ALU.add)
                    if masks:
                        link(m)
                    link(dve.tensor_reduce(sume[:, h:h + 1], flatps[:, 0:nk * P], AX.X, ALU.max))
                    if sink:
                        m = TS(rowneg[:, h:h + 1], sume[:, h:h + 1], -scale, nsink[:, h:h + 1], ALU.mult, ALU.min)
                    else:
                        m = TS(rowneg[:, h:h + 1], sume[:, h:h + 1], -scale, None, ALU.mult)
                    m.then_inc(sems["rowmax"], tally("rowmax"))

                def body():
                    for h in range(H):
                        row_max(h)
                    dve.wait_ge(sems["probs"], nth("probs", 4, 4))
                    if sink:
                        link(TT(den, den, esink, ALU.add))
                    link(dve.reciprocal(rden, den))
                    dve.wait_ge(sems["pv"], nth("pv", 4, 4))
                    TT(yst, ps[:, 7, 0:256].rearrange("p (h c) -> p h c", h=H), spread(rden, 2, 64), ALU.mult).then_inc(sems["y_norm"], tally("y_norm"))
                    dve.wait_ge(sems["yT_mm"], nth("yT_mm", 1, 1))
                return body, per

            def run(count, nk, scale, sink, masks, looped=True):
                body, per = attend(nk, scale, sink, masks)
                if looped:
                    with ln.loop(count):
                        body()
                else:
                    body()
                for n_, k_ in per.items():
                    ln.passed(n_, k_ * count)

            def latent_attention(L):
                units, plan = latent_plan(L)
                n_max = n_weigh = 0
                flatps = ps[:, 0:3, :].rearrange("p a b -> p (a b)")
                for what, u, j in plan:
                    h, lo, hi, nk = units[u] if what != "ada" else units[0]
                    if what == "max":
                        n_max += 1
                        dve.wait_ge(sems["scores"], nth("scores", n_max))
                        dve.tensor_reduce(m_max[:, u % 2, j:j + 1], flatps[:, 0:nk * P], AX.X, ALU.max)\
                           .then_inc(sems["rowmax"], tally("rowmax"))
                    if what == "rows":
                        dve.wait_ge(sems["maxrow_mm"], nth("maxrow_mm", u + 1))
                        TS(m_q[96:97, h, lo:hi], ps[0:1, 7, 0:hi - lo], -1.0, None, ALU.mult)\
                            .then_inc(sems["maxrow"], tally("maxrow"))
                    if what == "done":
                        n_weigh += nk
                        dve.wait_ge(sems["weighed"], nth("weighed", n_weigh))
                        if u:
                            dve.wait_ge(sems["y_done"], nth("y_done", u))
                        y_, l_ = (slice(0, 64), slice(64, 128)) if h % 2 == 0 else (slice(64, 128), slice(0, 64))
                        link(dve.reciprocal(m_rec[y_, 0:hi - lo], ps[l_, 5 + u % 2, 0:hi - lo]))
                        TT(Y[y_, 6 + h // 2, lo:hi], ps[y_, 5 + u % 2, 0:hi - lo], m_rec[y_, 0:hi - lo], ALU.mult)\
                            .then_inc(sems["y_done"], tally("y_done"))
                    if what == "ada":
                        ada(L, u)

            def swa_prep():
                x = lambda ap: ap.rearrange("p (h a c) -> p h a c", h=6, a=2)
                link(TS(nsink, par["sink"], -1.0, None, ALU.mult))
                with ln.loop(NT, [("z_sb", 1), ("qkT_mm", 1)]) as i:
                    dve.wait_ge(sems["z_sb"], nth("z_sb", 1, 1))
                    TS(w_v[:, i, :], zst[:, 384:512], 1.0, None, ALU.mult)
                    rotate(x(zst[:, 0:384]), x(w_a), x(w_b), rope[:, i, 0:32], rope[:, i, 32:64], x(w_qk), 32).then_inc(sems["qk_roped"], tally("qk_roped"))
                    dve.wait_ge(sems["qkT_mm"], nth("qkT_mm", 1, 1))

            def ret_tables():
                dve.wait_ge(sems["tables"], nth("tables", 1))
                TS(lg_ret, lg_ret, -1.0, 1.0, ALU.mult, ALU.add)
                TS(lg_row, lg_row, -1.0, 1.0, ALU.mult, ALU.add).then_inc(sems["sk"], tally("sk"))
                dve.wait_ge(sems["tables"], nth("tables", 2))
                ln.passed("tables", 2)
                TT(r_qst, r_qst, spread(tri[:, 0, :], 1, H), ALU.mult)
                link(TT(r_p, r_p, spread(tri[:, 1, :], 1, H), ALU.mult))
                link(TT(r_dt, r_qst, r_p, ALU.add))
                link(dve.memset(r_S[:, 0, :], 0.0))

            def ret_forward():
                x = lambda ap: ap.rearrange("p (h a c) -> p h a c", h=8, a=2)
                hd = lambda ap: ap.rearrange("p (h c) -> p h c", h=H)
                with ln.loop(NT, [(n_, 1) for n_ in ("z_sb", "r_kT_mm", "r_kv", "r_kT_sb")]) as i:
                    dve.wait_ge(sems["z_sb"], nth("z_sb", 1, 1))
                    out = r_R.rearrange("p a (h b c) -> p (a h) b c", h=H, b=2)
                    rotate(x(r_z[:, 0:256]), x(r_a), x(r_b), rope[:, i, 64:80], rope[:, i, 80:96], out, 16).then_inc(sems["r_roped"], tally("r_roped"))
                    link(dve.drain())
                    TT(hd(r_kz), hd(r_R[:, 1, :]), spread(zeta[:, 0, :], 2, 32), ALU.mult).then_inc(sems["r_kz"], tally("r_kz"))
                    dve.wait_ge(sems["r_kv"], nth("r_kv", 1, 1))
                    link(STT(r_tmp, r_S[:, i, :], gch[:, 0:1], ps[:, 3, 0:256], ALU.mult, ALU.add))
                    link(TT(r_S[:, i + 1, :], r_tmp, cst["heads_diag"], ALU.mult))
                    dve.sem_inc(sems["r_state"], tally("r_state"))
                    dve.wait_ge(sems["r_kT_sb"], nth("r_kT_sb", 1, 1))

            def gated(o, z, th, gain, out):
                dve.wait_ge(sems["g_tanh"], nth("g_tanh", 1, 1))
                link(STT(flat(th), flat(th), 1.0, z, ALU.add, ALU.mult))
                link(TT(o, o, gain, ALU.mult))
                STT(flat(out), flat(o), 0.5, flat(th), ALU.mult, ALU.mult).then_inc(sems["g_y"], tally("g_y"))

            def ret_backward(count, first):
                hd = lambda ap: ap.rearrange("p (h c) -> p h c", h=H)
                with ln.loop(count, [(n_, 1) for n_ in ("r_scores", "r_out", "r_kv", "g_sq", "g_rstd", "g_tanh", "yT_mm", "yT_sb")], down_from=first) as i:
                    t = ln.down
                    dve.wait_ge(sems["r_scores"], nth("r_scores", 1, 1))
                    TT(r_p, ps[:, 0:4, 0:P], r_dt, ALU.mult).then_inc(sems["r_probs"], tally("r_probs"))
                    dve.wait_ge(sems["r_out"], nth("r_out", 1, 1))
                    link(dve.tensor_reduce(ss[:, 0:4], hd(ps[:, 4, 0:256]), AX.X, ALU.add))
                    link(TS(musum, ss[:, 0:4], 1.0 / 64, None, ALU.mult))
                    link(TT(r_o, hd(ps[:, 4, 0:256]), spread(musum, 2, 64), ALU.subtract))
                    dve.sem_inc(sems["r_o"], tally("r_o"))
                    dve.sem_inc(sems["r_centred"], tally("r_centred"))
                    dve.wait_ge(sems["r_kv"], nth("r_kv", 1, 1))
                    link(STT(r_tmp, r_Sb, gch[:, 1:2], ps[:, 3, 0:256], ALU.mult, ALU.add))
                    TT(r_Sb, r_tmp, cst["heads_diag"], ALU.mult).then_inc(sems["r_state"], tally("r_state"))
                    dve.wait_ge(sems["g_sq"], nth("g_sq", 1, 1))
                    link(dve.tensor_reduce(ss2[:, 0:4], r_sq, AX.X, ALU.add))
                    TS(rs[:, 0:4], ss2[:, 0:4], 1.0 / 64, EPS, ALU.mult, ALU.add).then_inc(sems["g_veps"], tally("g_veps"))
                    dve.wait_ge(sems["g_rstd"], nth("g_rstd", 1, 1))
                    link(TT(r_o, r_o, spread(rs2[:, 0:4], 2, 64), ALU.mult))
                    gated(r_o, r_g[:, t, :], r_th, hd(par["ret_g"]), r_gt)
                    dve.wait_ge(sems["yT_sb"], nth("yT_sb", 1, 1))

            def dn_project():
                for lo in (0, 2 + NCTX, 6 + NTOK):
                    m = dve.memset(raw[:, :, lo:lo + (4 if lo == 2 + NCTX else 2)], 0.0)
                for n_ in range(1, 18, 2):
                    j, (lo, hi) = n_ // 3, SEGMENTS[n_ % 3]
                    dve.wait_ge(sems["prod"], nth("prod", n_ + 1))
                    off = 2 if lo < NCTX else 6
                    TS(raw[:, j, lo + off:hi + off], ps[:, n_ % 4, 0:hi - lo], 1.0, None, ALU.mult).then_inc(sems["evac_dve"], tally("evac_dve"))
                ln.passed("prod", 18)

            def dn_gates_():
                ab = d_ab.rearrange("p t (q a h) -> p t q a h", q=2, a=2)
                for q in range(2):
                    m = TT(d_x[:, :, 4 * q:4 * q + 4], ab[:, :, q, 0, :], spread(par["dt"][:, 4 * q:4 * q + 4], 1, NT), ALU.add)
                link(m)
                link(TS(flat(d_w), flat(d_x), -1.0, None, ALU.mult))
                TT(flat(d_w), flat(d_w), flat(d_x), ALU.min).then_inc(sems["dn_gates"], tally("dn_gates"))
                link(dve.drain())
                TS(flat(d_x), flat(d_x), 0.0, None, ALU.max)
                dve.wait_ge(sems["dn_gates2"], nth("dn_gates2", 1))
                TS(flat(d_bt), flat(d_bt), 1.0, 0.5, ALU.add, ALU.mult)
                TS(flat(d_w), flat(d_w), 1.0, None, ALU.add).then_inc(sems["dn_gates"], tally("dn_gates"))
                dve.wait_ge(sems["dn_gates2"], nth("dn_gates2", 2))
                link(TT(flat(d_x), flat(d_x), flat(d_w), ALU.add))
                link(STT(d_lg, d_x, -1.0, spread(nega, 1, NT), ALU.mult, ALU.mult))
                ln.passed("dn_gates2", 2)

            def dn_conv():
                taps = par["conv"].rearrange("p (j k) -> p j k", j=6)
                n_ = PADDED - 4
                with ln.loop(6, [("c_tanh", 1)]) as j:
                    for k in range(5):
                        src = raw[:, j, k:k + n_]
                        w_ = taps[:, j, k:k + 1]
                        m = TS(cv_y, src, w_, None, ALU.mult) if k == 0 else STT(cv_y, src, w_, cv_y, ALU.mult, ALU.add)
                        link(m)
                    dve.sem_inc(sems["c_y"], tally("c_y"))
                    dve.wait_ge(sems["c_tanh"], nth("c_tanh", 1, 1))
                    STT(raw[:, j, 0:NCTX], cv_t[:, 0:NCTX], 1.0, cv_y[:, 0:NCTX], ALU.add, ALU.mult)
                    link(STT(raw[:, j, NCTX:NTOK], cv_t[:, NCTX + 4:NTOK + 4], 1.0, cv_y[:, NCTX + 4:NTOK + 4],
                             ALU.add, ALU.mult))

            def dn_norm():
                with ln.loop(NT, [(n_, 1) for n_ in ("d_sq", "d_rstd", "d_kT", "d_kTs")]) as i:
                    dve.wait_ge(sems["d_sq"], nth("d_sq", 1, 1))
                    link(dve.tensor_reduce(ss, d_sq, AX.X, ALU.add))
                    TS(rs, ss, 4 * EPS, None, ALU.add).then_inc(sems["d_veps"], tally("d_veps"))
                    dve.wait_ge(sems["d_rstd"], nth("d_rstd", 1, 1))
                    link(TS(rs2[:, 0:4], rs2[:, 0:4], 0.125, None, ALU.mult))
                    TT(d_n, ps[:, 0, :].rearrange("p (h c) -> p h c", h=8), spread(rs2, 2, 64), ALU.mult).then_inc(sems["d_norm"], tally("d_norm"))
                    dve.wait_ge(sems["d_kTs"], nth("d_kTs", 1, 1))

            def dn_scan(count, first, last):
                sig = [(f"{n_}{q}", 1) for n_ in ("u_g", "u_dt", "u_gram", "u_vmm", "u_omm") for q in range(2)]
                sig += [(f"{n_}{q}", 6) for n_ in ("u_ymm", "u_umm") for q in range(2)]
                hd = lambda ap: ap.rearrange("p (h c) -> p h c", h=H)
                with ln.loop(count, sig, down_from=last) as i:
                    tt = (first + i, ln.down)
                    for q in range(2):
                        b, Ab, Bb, Cb, Db = sc[q], *(ps[:, 4 * q + z, :] for z in range(4))
                        dve.wait_ge(sems[f"u_g{q}"], nth(f"u_g{q}", 1, 1))
                        link(TS(gc[q], Db[:, 0:8], 1.0, None, ALU.mult))
                        TS(tl[q][:, 0:4], gc[q][:, 0:4], 1.0, None, ALU.mult)
                        TT(tl[q][:, 4:8], gc[q][:, 4:8], gc[q][:, 0:4], ALU.subtract)
                        TS(tl[q][:, 8:12], gc[q][:, 4:8], 1.0, None, ALU.mult)
                        for h in range(H):
                            m = STT(b["dt"][:, h, :], hd(Ab)[:, h, :], gc[q][:, h:h + 1], upto[:, q, :], ALU.subtract, ALU.min)
                        m.then_inc(sems[f"u_arg{q}"], tally(f"u_arg{q}"))
                    for q in range(2):
                        b, Ab, Bb, Cb, Db = sc[q], *(ps[:, 4 * q + z, :] for z in range(4))
                        dve.wait_ge(sems[f"u_gram{q}"], nth(f"u_gram{q}", 1, 1))
                        dve.wait_ge(sems[f"u_dt{q}"], nth(f"u_dt{q}", 1, 1))
                        gram = ps[:, 4 * q + 1:4 * q + 3, :].rearrange("p e (a j c) -> p e a j c", a=2, j=2)
                        for h in range(H):
                            STT(b["at"][:, h, :], gram[:, h % 2, 0, h // 2, :], d_bt[:, tt[q], 4 * q + h:4 * q + h + 1], b["dt"][:, h, :],
                                ALU.mult, ALU.mult)
                        by_half = lambda ap: ap.rearrange("p (j e) c -> p e j c", e=2)
                        link(TT(by_half(b["qkd"]), gram[:, :, 1, :, :], by_half(b["dt"]), ALU.mult))
                        link(TT(b["u"], b["at"], spread(levels[:, 1 - q, 0, :], 1, H), ALU.mult))
                        TT(b["u"], b["u"], spread(ident, 1, H), ALU.add).then_inc(sems[f"u_inv{q}"], tally(f"u_inv{q}"))
                    for lv in range(1, LEVELS):
                        for q in range(2):
                            b = sc[q]
                            dve.wait_ge(sems[f"u_ymm{q}"], nth(f"u_ymm{q}", lv, 6))
                            TT(b["ym"], hd(ps[:, 4 * q + 1, :]), spread(levels[:, q, lv, :], 1, H), ALU.mult).then_inc(sems[f"u_ysb{q}"], tally(f"u_ysb{q}"))
                        for q in range(2):
                            b = sc[q]
                            dve.wait_ge(sems[f"u_umm{q}"], nth(f"u_umm{q}", lv, 6))
                            TT(b["u"], hd(ps[:, 4 * q + 2, :]), b["u"], ALU.add).then_inc(sems[f"u_usb{q}"], tally(f"u_usb{q}"))
                    for q in range(2):
                        b = sc[q]
                        dve.wait_ge(sems[f"u_vmm{q}"], nth(f"u_vmm{q}", 1, 1))
                        TT(hd(b["vn"]), hd(ps[:, 4 * q + 1, 0:256]), spread(d_bt[:, tt[q], 4 * q:4 * q + 4], 2, 64), ALU.mult).then_inc(sems[f"u_vsb{q}"], tally(f"u_vsb{q}"))
                    for q in range(2):
                        b, Ab, Cb = sc[q], ps[:, 4 * q, :], ps[:, 4 * q + 2, :]
                        dve.wait_ge(sems[f"u_omm{q}"], nth(f"u_omm{q}", 1, 1))
                        for h in range(H):
                            rows = slice(64 * (h % 2), 64 * (h % 2) + 64)
                            S_ = b["S"][rows, h // 2, 64 * (h % 2):64 * (h % 2) + 64]
                            STT(S_, S_, egt[q][rows, 8 + h:9 + h], Ab[rows, h * 64:(h + 1) * 64], ALU.mult, ALU.add)
                        link(TT(b["o"], hd(Cb[:, 0:256]), spread(egt[q][:, 0:4], 2, 64), ALU.mult))
                        link(TT(flat(b["o"]), Cb[:, 256:512], flat(b["o"]), ALU.add))
                        link(TT(d_o[:, tt[q], :], d_o[:, tt[q], :], flat(b["o"]), ALU.add))
                        dve.sem_inc(sems[f"u_done{q}"], tally(f"u_done{q}"))

            def dn_out(count):
                hd = lambda ap: ap.rearrange("p (h c) -> p h c", h=H)
                with ln.loop(count, [(n_, 1) for n_ in ("g_sq", "g_rstd", "g_tanh", "yT_sb")]) as i:
                    dve.sem_inc(sems["g_row"], tally("g_row"))
                    dve.wait_ge(sems["g_sq"], nth("g_sq", 1, 1))
                    link(dve.tensor_reduce(ss2[:, 0:4], g_s, AX.X, ALU.add))
                    TS(rs[:, 0:4], ss2[:, 0:4], 1.0 / 64, EPS, ALU.mult, ALU.add).then_inc(sems["g_veps"], tally("g_veps"))
                    dve.wait_ge(sems["g_rstd"], nth("g_rstd", 1, 1))
                    link(TT(g_o, hd(d_o[:, i, :]), spread(rs2[:, 0:4], 2, 64), ALU.mult))
                    gated(g_o, d_z[:, i, :], g_th, spread(par["dn_g"], 1, H), r_gt_dn)
                    dve.wait_ge(sems["yT_sb"], nth("yT_sb", 1, 1))

            def add_gated(L, n_, bank, cols, gate_):
                j, (lo, hi) = n_ // len(cols), cols[n_ % len(cols)]
                which = 1 if lo < NCTX else 0
                STT(X[:, j, lo:hi], ps[:, bank, 0:hi - lo], mods[:, L, gate_ + j, which:which + 1], X[:, j, lo:hi],
                        ALU.mult, ALU.add).then_inc(sems["evac_dve"], tally("evac_dve"))

            def project_out(L):
                cols = tokens(L)
                for n_ in range(8 * len(cols)):
                    dve.wait_ge(sems["prod"], nth("prod", n_ + 1))
                    add_gated(L, n_, n_ % 4, cols, G1)
                ln.passed("prod", 8 * len(cols))

            def mlp(L):
                cols = tokens(L)
                g = 8 * len(cols)
                with ln.loop(FG, [("relu", g), ("prod", 2 * g)]):
                    for n_ in range(g):
                        j, (lo, hi) = n_ // len(cols), cols[n_ % len(cols)]
                        dve.wait_ge(sems["relu"], nth("relu", n_ + 1, g))
                        r_ = relu_sb[:, n_ % 4, 0:hi - lo]
                        TT(Y[:, j, lo:hi], r_, r_, ALU.mult).then_inc(sems["sq_done"], tally("sq_done"))
                    for n_ in range(g):
                        dve.wait_ge(sems["prod"], nth("prod", g + n_ + 1, 2 * g))
                        add_gated(L, n_, 4 + n_ % 4, cols, G2)

            def layer_norm(L):
                n = len(tokens(L))
                for c, (lo, hi) in enumerate(tokens(L)):
                    dve.wait_ge(sems["ln_mean"], nth("ln_mean", c + 1))
                    TT(X[:, :, lo:hi], X[:, :, lo:hi], spread(ps[:, c, 0:hi - lo], 1, KT), ALU.subtract).then_inc(sems["ln_centred"], tally("ln_centred"))
                for c, (lo, hi) in enumerate(tokens(L)):
                    dve.wait_ge(sems["ln_var"], nth("ln_var", c + 1))
                    TS(ln_r[:, c, 0:hi - lo], ps[:, c + 3, 0:hi - lo], LN_EPS, None, ALU.add).then_inc(sems["ln_veps"], tally("ln_veps"))
                for c, (lo, hi) in enumerate(tokens(L)):
                    dve.wait_ge(sems["ln_root"], nth("ln_root", c + 1))
                    link(dve.reciprocal(ln_r[:, c, 0:hi - lo], ln_r[:, c, 0:hi - lo]))
                    TT(X[:, :, lo:hi], X[:, :, lo:hi], spread(ln_r[:, c, 0:hi - lo], 1, KT), ALU.mult).then_inc(sems["ln_scaled"], tally("ln_scaled"))
                for n_ in ("ln_mean", "ln_var", "ln_root"):
                    ln.passed(n_, n)

            dve.wait_ge(sems["consts_in"], 32)
            dve.wait_ge(sems["x_in"], nth("x_in", 32))
            for L in range(DEPTH):
                ln.barrier()
                if L == 0:
                    ada(0, 0)
                    ada(0, 1)
                ln.barrier()
                modulate(L, SH1, SC1)
                ln.barrier()
                mla_prep()
                ln.barrier()
                latent_attention(L)
                ln.barrier()
                ret_tables()
                ln.barrier()
                ret_forward()
                ln.barrier()
                ada(L, 5)
                link(dve.memset(r_Sb, 0.0))
                dve.sem_inc(sems["r_kcopy"], tally("r_kcopy"))
                ret_backward(CT, CT - 1)
                ret_backward(NT - CT, NT - 1)
                ln.barrier()
                swa_prep()
                ln.barrier()
                if L == 0:
                    ada(1, 0)
                    run(CT, 2, 0.125, True, [])
                run(1, 4, 0.125, True, [(3, 1)], False)
                run(NT - CT - 2, 5, 0.125, True, [(2, 0), (4, 1)])
                run(1, 4, 0.125, True, [(2, 0)], False)
                ln.barrier()
                dn_project()
                ln.barrier()
                dn_gates_()
                dn_conv()
                ln.barrier()
                dn_norm()
                ln.barrier()
                dn_scan(CT, 0, CT - 1)
                dn_scan(NT - CT, CT, NT - 1)
                ln.barrier()
                dn_out(NT)
                ln.barrier()
                project_out(L)
                ln.barrier()
                if L == 0:
                    ada(1, 1)
                layer_norm(L)
                ln.barrier()
                modulate(L, SH2, SC2)
                ln.barrier()
                mlp(L)
                ln.barrier()
                layer_norm(L)
                ln.barrier()

        @block.gpsimd
        def _(pool):
            ln = Lane(pool, "pool", sems, book)
            start(ln)
            nth, tally, link = ln.nth, ln.tally, ln.link
            TT, TS, COPY = pool.tensor_tensor, pool.tensor_scalar, pool.tensor_copy

            def stage_tiles(dst):
                with ln.loop(NT, [("z_mm", 1)]) as i:
                    yield i, lambda: COPY(dst, Hm[:, :, tile_cols(i)]).then_inc(sems["tile_in"], tally("tile_in"))

            def root(dst, src, n):
                return TT(dst[:, 0:n], src[:, 0:n], mhalf[:, 0:n], ALU.pow)

            def mla_prep():
                with ln.loop(NT, [("z_mm", 1), ("veps", 1), ("qkT_mm", 1)]) as i:
                    COPY(hst, Hm[:, :, tile_cols(i)]).then_inc(sems["tile_in"], tally("tile_in"))
                    pool.wait_ge(sems["veps"], nth("veps", 1, 1))
                    root(rs2, rs, 2).then_inc(sems["rstd"], tally("rstd"))
                    pool.wait_ge(sems["qkT_mm"], nth("qkT_mm", 1, 1))

            def attend(count, stage, per_looped=True):
                if per_looped:
                    with ln.loop(count, [("yT_mm", 1)]) as i:
                        stage(i)
                        pool.wait_ge(sems["yT_mm"], nth("yT_mm", 1, 1))
                else:
                    stage(0)
                    pool.wait_ge(sems["yT_mm"], nth("yT_mm", 1))
                    ln.passed("yT_mm", count)

            def mla_stage(first):
                return lambda i: COPY(qst[0:96], m_q[0:96, :, tile_cols(first + i)]).then_inc(sems["q_staged"], tally("q_staged"))

            def swa_stage(first, nband):
                def stage(i):
                    t = first + i
                    if nband:
                        lo = lowest(t, nband)
                        COPY(kst[:, 0:nband, :].rearrange("p a b -> p (a b)"), w_kT[:, bass.ds(lo * P, nband * P)])
                    COPY(qst[:, 0:2, :], w_qT[:, :, tile_cols(t)]).then_inc(sems["q_staged"], tally("q_staged"))
                return stage

            def plain_prep():
                with ln.loop(NT, [("z_mm", 1)]) as i:
                    COPY(plain_prep.dst, Hm[:, :, tile_cols(i)]).then_inc(sems["tile_in"], tally("tile_in"))
                    pool.wait_ge(sems["z_mm"], nth("z_mm", 1, 1))

            def ret_backward(count, first):
                hd = lambda ap: ap.rearrange("p (h c) -> p h c", h=H)
                with ln.loop(count, [(n_, 1) for n_ in ("g_veps", "yT_mm")], down_from=first) as i:
                    t = ln.down
                    COPY(r_qst[:, 0:2, :], r_qkT[:, :, tile_cols(t)])
                    TT(r_qst[:, 2, :], r_qkT[:, 0, tile_cols(t)], r_xi[:, 0, :], ALU.mult)
                    TT(r_qst[:, 3, :], r_qkT[:, 0, tile_cols(t)], r_xi[:, 1, :], ALU.mult).then_inc(sems["r_stage"], tally("r_stage"))
                    TT(hd(r_kz), hd(r_k[:, t, :]), spread(zeta[:, 1, :], 2, 32), ALU.mult).then_inc(sems["r_kz"], tally("r_kz"))
                    pool.wait_ge(sems["g_veps"], nth("g_veps", 1, 1))
                    root(rs2, rs, 4).then_inc(sems["g_rstd"], tally("g_rstd"))
                    pool.wait_ge(sems["yT_mm"], nth("yT_mm", 1, 1))

            def dn_norm():
                with ln.loop(NT, [("d_veps", 1), ("d_kT", 1)]) as i:
                    COPY(d_st, raw[:, :, tile_cols(i)]).then_inc(sems["d_stage"], tally("d_stage"))
                    pool.wait_ge(sems["d_veps"], nth("d_veps", 1, 1))
                    root(rs2, rs, 8).then_inc(sems["d_rstd"], tally("d_rstd"))
                    pool.wait_ge(sems["d_kT"], nth("d_kT", 1, 1))

            def dn_scan(count, first, last):
                hd = lambda ap: ap.rearrange("p (h c) -> p h c", h=H)
                with ln.loop(count, [(f"{n_}{q}", 1) for n_ in ("u_dt", "u_omm") for q in range(2)], down_from=last) as i:
                    tt = (first + i, ln.down)
                    for q in range(2):
                        b = sc[q]
                        COPY(b["qk"], raw[:, 0:4, tile_cols(tt[q])])
                        TT(b["gm"], spread(tri[:, q, :], 1, H), spread(d_lg[:, tt[q], 4 * q:4 * q + 4], 2, P), ALU.mult).then_inc(sems[f"u_stage{q}"], tally(f"u_stage{q}"))
                    for q in range(2):
                        b = sc[q]
                        pool.wait_ge(sems[f"u_dt{q}"], nth(f"u_dt{q}", 1, 1))
                        k_ = hd(kv_tok[:, tt[q], 0:256])
                        TT(hd(b["kt"]), k_, spread(egt[q][:, 4:8], 2, 64), ALU.mult)
                        TT(hd(b["keg"]), k_, spread(egt[q][:, 0:4], 2, 64), ALU.mult).then_inc(sems[f"u_keg{q}"], tally(f"u_keg{q}"))
                    for q in range(2):
                        pool.wait_ge(sems[f"u_omm{q}"], nth(f"u_omm{q}", 1, 1))

            def dn_out(count):
                with ln.loop(count, [("g_veps", 1)]):
                    pool.wait_ge(sems["g_veps"], nth("g_veps", 1, 1))
                    root(rs2, rs, 4).then_inc(sems["g_rstd"], tally("g_rstd"))

            def latent_attention(L):
                units, plan = latent_plan(L)
                last = {}
                for n_, (h, lo, hi, nk) in enumerate(units):
                    last[h] = n_
                link(pool.memset(m_k[96:97, :, :], 1.0))
                link(pool.memset(v_ones[0][:, :, 64:128], 1.0))
                link(pool.memset(v_ones[1][:, :, 0:64], 1.0))
                for h in range(H):
                    if h >= 2:
                        pool.wait_ge(sems["y_done"], nth("y_done", last[h - 2] + 1))
                    at_ = 64 * (h % 2)
                    COPY(v_ones[h % 2][:, :, at_:at_ + 64], m_v[:, :, h * 64:(h + 1) * 64]).then_inc(sems["v_staged"], tally("v_staged"))

            pool.memset(mhalf, -0.5)
            pool.wait_ge(sems["consts_in"], 32)
            for L in range(DEPTH):
                ln.barrier()
                ln.barrier()
                ln.barrier()
                mla_prep()
                ln.barrier()
                latent_attention(L)
                ln.barrier()
                ln.barrier()
                plain_prep.dst = hst
                plain_prep()
                ln.barrier()
                pool.wait_ge(sems["r_kcopy"], nth("r_kcopy", 1))
                ln.passed("r_kcopy", 1)
                ret_backward(CT, CT - 1)
                ret_backward(NT - CT, NT - 1)
                ln.barrier()
                plain_prep()
                ln.barrier()
                if L == 0:
                    attend(CT, swa_stage(0, 0))
                attend(1, swa_stage(CT, 2), False)
                attend(NT - CT - 2, swa_stage(CT + 1, 3))
                attend(1, swa_stage(NT - 1, 2), False)
                ln.barrier()
                plain_prep.dst = d_hst
                plain_prep()
                ln.barrier()
                ln.barrier()
                dn_norm()
                ln.barrier()
                link(pool.memset(d_o[:], 0.0))
                for q in range(2):
                    pool.memset(sc[q]["S"], 0.0)
                dn_scan(CT, 0, CT - 1)
                dn_scan(NT - CT, CT, NT - 1)
                ln.barrier()
                dn_out(NT)
                ln.barrier()
                ln.barrier()
                ln.barrier()
                ln.barrier()
                ln.barrier()
                ln.barrier()


def pack_chunk(w, rows, cols):
    part = w[rows:rows + DM][:, cols]
    out = np.zeros((KT, P, CW), np.float32)
    out[:, :, :part.shape[1]] = part.reshape(KT, P, -1)
    return out.transpose(1, 0, 2).reshape(P, KT * CW)


def pack_weights(w):
    r = np.arange
    out = []
    ada = lambda L, v: [pack_chunk(w["ada_w"][L], 0, r(c * CW, (c + 1) * CW)) for c in (2 * v, 2 * v + 1)]
    heads = np.concatenate([r(64 * h, 64 * h + 64) for h in (0, 2, 1, 3)])
    for L in range(DEPTH):
        mixers = [pack_chunk(w["w_in"][L], 0, cols) for cols in (
            r(2320, 2736), r(1552, 2064), r(2064, 2320), np.concatenate([heads, r(256, 512)]),
            r(512, 896), r(896, 1280), r(1280, 1552))]
        if L == 0:
            out += ada(0, 0) + ada(0, 1)
        out += mixers[:1] + ada(L, 2) + ada(L, 3) + ada(L, 4) + mixers[1:3] + ada(L, 5) + mixers[3:4]
        if L == 0:
            out += ada(1, 0)
        out += mixers[4:]
        out += [pack_chunk(w["w_out"][L], 0, r(c * CW, (c + 1) * CW)) for c in range(2)]
        if L == 0:
            out += ada(1, 1)
        for g in range(FG):
            out += [pack_chunk(w["w_ff1"][L], 0, r(g * DM + c * CW, g * DM + (c + 1) * CW)) for c in range(2)]
            out += [pack_chunk(w["w_ff2"][L], g * DM, r(c * CW, (c + 1) * CW)) for c in range(2)]
    return np.stack(out)


def pack_params(w, L):
    rows = lambda a: np.broadcast_to(np.ravel(a)[None, :], (P, np.size(a)))
    chan = lambda a: np.reshape(a, (-1, P)).T
    out = np.zeros((P, NPARAM), np.float32)
    g = w["ret_log1m_gamma"][L]
    conv = np.asarray(w["dn_conv_w"][L]).reshape(5, 6, P).transpose(2, 1, 0).reshape(P, 30)
    values = {
        "sink": rows(w["swa_sink"][L]), "log1m": rows(g),
        "log1m_row": np.repeat(g, 32, axis=1).T, "a_log": rows(w["dn_a_log"][L]), "dt": rows(w["dn_dt_bias"][L]),
        "dn_g": rows(w["dn_norm_g"][L]), "ret_g": rows(w["ret_norm_g"][L]), "ln1_g": chan(w["ln1_g"][L]),
        "ln1_b": chan(w["ln1_b"][L]), "ln2_g": chan(w["ln2_g"][L]), "ln2_b": chan(w["ln2_b"][L]), "conv": conv,
        "q_norm": chan(w["mla_q_norm"][L]), "kv_norm": chan(w["mla_kv_norm"][L]),
    }
    for name, v in values.items():
        a, b = PARAMS[name]
        out[:, a:b] = v
    return out


def kernel(**inputs):
    import concourse.bacc as _bacc
    from concourse.bass_utils import run_bass_kernel_spmd as _run

    w = {k: np.asarray(v) for k, v in inputs.items()}
    channels = lambda a: a.T.reshape(KT, P, -1).transpose(1, 0, 2)
    arrays = {
        "x": channels(np.concatenate([w["ctx"][0], w["x"][0]], 0)),
        "cc": channels(np.stack([w["c"][0], w["c_ctx"]], 0)),
        "weights": pack_weights(w),
        "params": np.stack([pack_params(w, L) for L in range(DEPTH)]),
        "w_uq": w["mla_w_uq"].reshape(DEPTH, 2, P, 384).transpose(0, 2, 1, 3),
        "w_ukv": w["mla_w_ukv"],
        "consts": np.concatenate(list(constants().values()), 1),
        "levels": level_masks(),
        "ada_b": w["ada_b"].reshape(DEPTH, 48, P).transpose(2, 0, 1),
    }
    arrays = {k: np.ascontiguousarray(v, dtype=np.float32) for k, v in arrays.items()}

    def program(book):
        nc = _bacc.Bacc("TRN2", target_bir_lowering=False, num_devices=1)
        d = {k: nc.dram_tensor("in_" + k, v.shape, F32, kind="ExternalInput").ap() for k, v in arrays.items()}
        d["out"] = nc.dram_tensor("out_x", (P, KT, NLAT), F32, kind="ExternalOutput").ap()
        build(nc, d, book)
        return nc

    book = {"links": {}, "new": {}, "old": {}}
    program(book)
    book = {"links": book["links"], "old": book["new"], "new": {}, "phases_old": book["phases"]}
    nc = program(book)
    r = _run(nc, [{"in_" + k: v for k, v in arrays.items()}], core_ids=[0])
    out = r.results[0]["out_x"]
    return np.ascontiguousarray(out.transpose(2, 1, 0).reshape(1, NLAT, DM))
```

```python
from contextlib import ExitStack, contextmanager

import numpy as np

import concourse.bass as bass
from concourse import mybir

ALU = mybir.AluOpType
ACT = mybir.ActivationFunctionType
AX = mybir.AxisListType
F32 = mybir.dt.float32
F32R = mybir.dt.float32r

P = 128
DM = 1024
KT = DM // P
NCTX, NLAT = 256, 1024
NTOK = NCTX + NLAT
NT = NTOK // P
CT = NCTX // P
DEPTH = 2
GRID_W = 64
H = 4
CW = 512
FG = 8
FW = 4 * DM // FG
HALF = KT * CW // 2
ALPHA = float((2 * DEPTH) ** 0.25)
LN_EPS, EPS = 1e-5, 1e-6
NEG = -1e30
LEVELS = 7
CHUNKS = [7 + 2 + 2 * 8, 7 + 2 + 2 * 4]
SEGMENTS = [(0, 256), (256, 768), (768, 1280)]


def chunk_params():
    at, out = 0, {}
    for name, n in (("sink", H), ("log1m", 2 * H), ("log1m_row", 2), ("a_log", 2 * H),
                    ("dt", 2 * H), ("dn_g", 64), ("ret_g", 256), ("ln1_g", KT), ("ln1_b", KT),
                    ("ln2_g", KT), ("ln2_b", KT), ("conv", 30), ("q_norm", 2), ("kv_norm", 1)):
        out[name] = (at, at + n)
        at += n
    return out, at


PARAMS, NPARAM = chunk_params()


def rope_tables():
    f = np.float32
    freqs = lambda dim: (f(10000.0) ** (-np.arange(0, dim, 2, dtype=f) / f(dim))).astype(f)
    pos = np.arange(NLAT)
    row, col = (pos // GRID_W).astype(f), (pos % GRID_W).astype(f)
    angs = []
    for dim in (64, None, 32):
        if dim is None:
            angs.append(pos.astype(f)[:, None] * freqs(32))
        else:
            inv = freqs(dim // 2)
            angs.append(np.concatenate([row[:, None] * inv, col[:, None] * inv], -1))
    lat = np.concatenate([g(a.astype(f)) for a in angs for g in (np.cos, np.sin)], -1).astype(f)
    head = np.concatenate([np.full((NCTX, a.shape[1]), v, f) for a in angs for v in (1.0, 0.0)], -1)
    return np.concatenate([head, lat], 0).reshape(NT, P, 128).transpose(1, 0, 2)


def constants():
    i = np.arange(P)
    a, b = i[:, None], i[None, :]
    f = np.float32
    out = {
        "ident": a == b,
        "tri": np.stack([a <= b, a >= b], 1),
        "upto": np.stack([np.where(b >= a, 0, NEG), np.where(b <= a, 0, NEG)], 1),
        "ones": np.ones((P, P)),
        "mean": np.full((P, P), 1.0 / DM),
        "rel": np.stack([np.maximum(b - a, 0), np.maximum(a - b, 0)], 1),
        "age": np.stack([np.broadcast_to(b + 1, (P, P)), np.broadcast_to(P - b, (P, P))], 1),
        "left": np.stack([P - 1 - i, i], 1),
        "heads_diag": (a // 32) == (np.arange(256)[None, :] // 64),
        "rope": rope_tables(),
    }
    return {k: np.ascontiguousarray(v, dtype=f).reshape(P, -1) for k, v in out.items()}


def level_masks():
    i = np.arange(P)
    c, s = i[:, None], i[None, :]
    out = np.zeros((P, 2, LEVELS, P), np.float32)
    for lv in range(LEVELS):
        same = (c >> (lv + 1)) == (s >> (lv + 1))
        out[:, 0, lv] = -1.0 * (same & (((c >> lv) & 1) == 1) & (((s >> lv) & 1) == 0))
        out[:, 1, lv] = -1.0 * (same & (((c >> lv) & 1) == 0) & (((s >> lv) & 1) == 1))
    return out.reshape(P, -1)


def spread(ap, axis, n):
    shape = list(ap.shape)
    shape.insert(axis, n)
    return ap.unsqueeze(axis).broadcast_to(shape)


class Lane:

    def __init__(self, eng, name, sems, book):
        self.e, self.name, self.sems, self.book = eng, name, sems, book
        self.seen, self.at = {}, {}
        self.i, self.times, self.loops, self.n, self.base, self.phase = None, 1, 0, 0, 0, 0

    def nth(self, name, k=1, per=0):
        v = self.seen.get(name, 0) + k
        return v + self.i * per if per and self.i is not None else v

    def passed(self, name, n):
        self.seen[name] = self.seen.get(name, 0) + n

    def tally(self, name, n=1):
        key = (self.phase, name)
        self.book["new"][key] = self.book["new"].get(key, 0) + n * self.times
        return n

    def link(self, ins):
        self.n += 1
        ins.then_inc(self.sems["chain_" + self.name], 1)
        v = self.base + self.n
        if self.i is not None:
            v = v + self.i * self.book["links"].get((self.name, self.loops), 1)
        self.e.wait_ge(self.sems["chain_" + self.name], v)

    @contextmanager
    def loop(self, count, signals=(), down_from=None):
        self.base, self.n, self.times = self.base + self.n, 0, count
        if down_from is not None:
            tile = self.e.alloc_register(f"down_{self.name}_{self.loops}")
            self.e.reg_mov(tile, down_from)
        with self.e.Fori(0, count) as i:
            self.i = i
            if down_from is not None:
                self.down = self.e.snap(tile, min_val=down_from - count + 1, max_val=down_from)
            yield i
            if down_from is not None:
                self.e.reg_sub(tile, tile, 1)
            self.i = None
        self.book["links"][(self.name, self.loops)] = self.n
        self.loops += 1
        self.base, self.n, self.times = self.base + self.n * count, 0, 1
        for name, per in signals:
            self.passed(name, per * count)

    def barrier(self):
        self.e.drain().then_inc(self.sems["phase"], 1)
        self.phase += 1
        self.e.wait_ge(self.sems["phase"], 4 * self.phase)
        self.book["phases"] = self.phase
        for (phase, name), n in self.book["old"].items():
            if phase == self.phase - 1:
                self.at[name] = self.at.get(name, 0) + n
        self.seen = dict(self.at)


SEM_NAMES = [
    "phase", "chain_pe", "chain_act", "chain_dve", "chain_pool",
    "chunk_in_0", "chunk_in_1", "chunk_used", "half_in_0", "half_in_1", "half_used", "split", "h_high", "h_split", "hidden", "consts_in", "x_in", "params_in", "weights_in", "masks_in", "out_done",
    "silu_c", "silu_ready", "ada_mm", "ada_sum", "h_lat",
    "prod", "evac_act", "evac_dve", "relu", "sq_done", "ln_mean", "ln_centred", "ln_square", "ln_var", "ln_veps", "ln_root",
    "ln_scaled",
    "tile_in",     "z_mm", "z_sb", "ss", "veps", "rstd", "normed", "cT_mm", "cT_sb", "up_mm", "up_v", "qk_roped", "qkT_mm", "qkT_sb",
    "maxrow_mm", "maxrow", "v_staged", "keyed", "exped", "weighed", "y_done", "q_staged", "scores", "rowmax", "probs", "pT_mm", "pT_act", "pv", "y_norm", "yT_mm", "yT_sb",
    "tables",
    "r_roped", "r_kT_mm", "r_kT_sb", "r_kz", "r_kv", "r_state", "r_stage", "r_scores", "r_probs", "r_out", "r_o",
    "g_sq", "g_tanh", "g_veps", "g_rstd", "g_y",
    "c_y", "c_tanh", "d_stage", "d_sq", "d_sum", "d_root", "d_norm", "d_kT", "d_kTs", "dn_gates",
    "dn_gates2", "r_kcopy", "sk",
] + [f"{n}{d}" for d in range(2) for n in (
    "u_stage", "u_g", "u_arg", "u_dt", "u_gram", "u_inv", "u_tmm", "u_tsb", "u_ymm", "u_ysb", "u_umm", "u_usb",
    "u_keg", "u_wmm", "u_wsb", "u_vmm", "u_vsb", "u_omm", "u_done", "u_e", "u_gc")]

CREDITS = {"pe": {}, "dve": {"u_done0": 1, "u_done1": 1}, "act": {}, "pool": {}}


def build(nc, d, book):
    with ExitStack() as ctx:
        sb = lambda name, shape: ctx.enter_context(nc.sbuf_tensor(name, shape, F32))
        ps = ctx.enter_context(nc.psum_tensor("ps", [P, 8, 512], F32))
        sems = {n: ctx.enter_context(nc.semaphore(n)) for n in SEM_NAMES}

        X = sb("X", [P, KT, NTOK])
        cshape = {"ident": 128, "tri": 256, "upto": 256, "ones": 128, "mean": 128, "rel": 256, "age": 256,
                  "left": 2, "heads_diag": 256, "rope": NT * 128}
        consts = sb("consts", [P, sum(cshape.values())])
        cst, at = {}, 0
        for n_, w_ in cshape.items():
            cst[n_] = consts[:, at:at + w_]
            at += w_
        ident, ones, mean_w = cst["ident"], cst["ones"], cst["mean"]
        two = lambda n_: cst[n_].rearrange("p (a b) -> p a b", a=2)
        tri, upto, rel, age = (two(n_) for n_ in ("tri", "upto", "rel", "age"))
        window = upto
        rope = cst["rope"].rearrange("p (t c) -> p t c", t=NT)
        params = sb("params", [P, NPARAM])
        par = {n_: params[:, a:b] for n_, (a, b) in PARAMS.items()}
        silu_c = sb("silu_c_sb", [P, KT, 2])
        mods = sb("mods", [P, DEPTH, 48, 2])
        ada_b = sb("ada_bias", [P, DEPTH, 48])
        small = sb("small", [P, 168])
        shapes = {"Hn": [P, KT * NTOK], "Yn": [P, KT * NTOK], "ring": [P, 2, KT * CW], "temp": [P, 10448]}
        with ExitStack() as once:
            Hn, Yn, ring, temp = (once.enter_context(nc.sbuf_tensor(n, s_, F32)) for n, s_ in shapes.items())
        Hn_r, Yn_r, ring_r, temp_r = (ctx.enter_context(nc.sbuf_tensor(n + "_parts", s_, F32R)) for n, s_ in shapes.items())
        Hm = Hn[:].rearrange("p (k n) -> p k n", k=KT)
        Y = Yn[:].rearrange("p (k n) -> p k n", k=KT)
        cc = temp[:, 10432:10448].rearrange("p (k s) -> p k s", k=KT)

        def cut(region, base, *shape):
            n = int(np.prod(shape))
            ap = region[:, base:base + n]
            if len(shape) == 2:
                ap = ap.rearrange("p (a b) -> p a b", a=shape[0])
            if len(shape) == 3:
                ap = ap.rearrange("p (a b c) -> p a b c", a=shape[0], b=shape[1])
            return ap, base + n

        SH1, SC1, G1, SH2, SC2, G2 = (8 * j for j in range(6))

        ss = small[:, 0:8]
        rs = small[:, 8:16]
        rowneg, den, esink, rden, nsink = (small[:, 16 + 4 * j:20 + 4 * j] for j in range(5))
        lg_ret = small[:, 36:44]
        lg_row = small[:, 44:46]
        zeta = small[:, 46:54].rearrange("p (a b) -> p a b", a=2)
        gch = small[:, 54:56]
        nega = small[:, 56:64]
        gc = [small[:, 64 + 8 * j:72 + 8 * j] for j in range(2)]
        egt = [small[:, 80 + 12 * j:92 + 12 * j] for j in range(2)]
        tl = [small[:, 104 + 12 * j:116 + 12 * j] for j in range(2)]
        ss2 = small[:, 136:144]
        rs2 = small[:, 144:152]
        sume = small[:, 152:156]
        mhalf = small[:, 160:168]
        musum = small[:, 128:132]

        hst, a0 = cut(temp, 0, KT, P)
        zst, a1 = cut(temp, a0, 512)
        m_qk, a2 = cut(temp, a1, 8, 96)
        m_cT, a3 = cut(temp, a2, 3, P)
        m_a, a4 = cut(temp, a3, 8, 32)
        m_b, a5 = cut(temp, a4, 8, 32)
        m_uq, a6 = cut(temp, a5, 2, 384)
        m_ukv, a7 = cut(temp, a6, 512)
        m_sq, a8 = cut(temp, a7, 384)
        m_q, a9 = cut(temp, a8, H, NTOK)
        assert a9 <= 10448
        m_k, b0 = cut(Yn, 0, H, NTOK)
        m_v, b1 = cut(Yn, b0, NT, 256)
        p_sb, c0 = cut(temp, 0, NT, P)
        pT0, c1 = cut(temp, c0, NT, P)
        pT1, c2 = cut(temp, c1, NT, P)
        qst, c3 = cut(temp, c2, H, P)
        yst, c4 = cut(temp, c3, H, 64)
        assert c4 <= a8
        pT = [pT0, pT1]
        probs = [p_sb[:, 0:5, :], p_sb[:, 5:10, :]]
        turned = (6, 2)
        w_qk, e0 = cut(temp, c4, 384)
        w_a, e1 = cut(temp, e0, 384)
        w_b, e2 = cut(temp, e1, 384)
        w_qT, e3 = cut(temp, e2, 2, NTOK)
        w_kT, e4 = cut(temp, e3, NTOK)
        w_v, e5 = cut(Yn, 2 * NTOK, NT, P)
        kst, e6 = cut(Yn, e5, 3, P)
        assert e4 <= 10448 and e6 <= 4 * NTOK
        r_z = temp[:, 1024:1792]
        r_R, f0 = cut(temp, 1792, 2, P)
        r_a, f1 = cut(temp, f0, 256)
        r_b, f2 = cut(temp, f1, 256)
        r_kz, f3 = cut(temp, f2, P)
        r_tmp, f4 = cut(temp, f3, 256)
        r_S, f5 = cut(temp, f4, NT + 1, 256)
        r_v, f6 = cut(temp, f5, NT, 256)
        r_k, f7 = cut(temp, f6, NT, P)
        r_dt, f8 = cut(temp, f7, H, P)
        r_xi, f9 = cut(temp, f8, 2, P)
        assert f9 <= 10448
        r_qkT, g0 = cut(Yn, 0, 2, NTOK)
        r_g, g1 = cut(Yn, g0, NT, 256)
        assert g1 <= 4 * NTOK
        r_qst, h0 = cut(temp, 0, 4, P)
        r_p, h1 = cut(temp, h0, H, P)
        r_Sb = r_R[:, :, :].rearrange("p a b -> p (a b)")
        assert h1 <= 1792
        r_o = r_qkT
        PADDED = NTOK + 8
        raw, i0 = cut(temp, 0, 6, PADDED)
        d_z, i1 = cut(temp, i0, NT, 256)
        d_ab, i2 = cut(temp, i1, NT, 16)
        assert i2 <= 10448
        d_o = temp[:, 4 * PADDED:4 * PADDED + NT * 256].rearrange("p (t c) -> p t c", t=NT)
        d_hst = [cut(Yn, 2 * NTOK + s_ * DM, KT, P)[0] for s_ in range(2)]
        kv_tok, j0 = cut(Hn, 0, NT, 512)
        levels, j1 = cut(Hn, j0, 2, LEVELS, P)
        d_lg, j5 = cut(Hn, j1 + PADDED - 4, NT, 8)
        d_bt, j6 = cut(Hn, j5, NT, 8)
        d_x, j7 = cut(Hn, j6, NT, 8)
        d_w, j8 = cut(Hn, j7, NT, 8)
        norm_segments = [(0, 512), (512, 1024), (1024, NTOK)]
        cv_y, _ = cut(Yn, 2 * NTOK, PADDED - 4)
        cv_t, _ = cut(Hn, j1, PADDED - 4)
        ringf = ring[:].rearrange("p a b -> p (a b)")
        n_sq, l1 = cut(ringf, 0, 4, NTOK)
        n_block, l2 = cut(ringf, l1, P)
        n_root, l3 = cut(ringf, l2, 4, 512)
        n_eps, l4 = cut(ringf, l3, 2)
        assert l4 <= 2 * KT * CW
        sc, y0 = [], 2 * NTOK
        for q_ in range(2):
            b = {}
            o_ = q_ * 4096
            for n_, shape in (("qk", (4, P)), ("gm", (H, P)), ("dt", (H, P)), ("at", (H, P)), ("qkd", (H, P)),
                              ("u", (H, P)), ("ym", (H, P)), ("S", (2, P)), ("o", (H, 64))):
                b[n_], o_ = cut(ringf, o_, *shape)
            assert o_ <= (q_ + 1) * 4096
            for n_ in ("keg", "kt", "wt", "vn"):
                b[n_], y0 = cut(Yn, y0, 256)
            sc.append(b)
        assert y0 <= 4 * NTOK
        H_hi, _ = cut(temp_r, 0, KT, NTOK)
        H_lo, _ = cut(Hn_r, 0, KT, NTOK)
        U = Y[:, 0:FW // P, :]
        U_lo, m0 = cut(Yn_r, 0, FW // P, NTOK)
        U_hi, m1 = cut(Yn_r, m0, FW // P, NTOK)
        assert m1 <= KT * NTOK
        half = [ring[:, s, 0:HALF] for s in range(2)]
        half_lo = [ring_r[:, s, 0:HALF] for s in range(2)]
        half_hi = [ring_r[:, s, HALF:2 * HALF] for s in range(2)]
        ln_r, _ = cut(temp, 2048, 3, 512)

        def gate_buffers(region):
            out, at_ = {}, 0
            for n_, shape in (("sq", (NT * H, 64)), ("th", (NT, 256)), ("out", (NT, 256)), ("root", (NT * H,)), ("rs", (NT * H,))):
                out[n_], at_ = cut(region, at_, *shape)
            return out

        pairs = lambda ap, c: ap[:, 2 * c:2 * c + 2, :].rearrange("p t (a x) -> p a t x", a=2)
        gate_ret = dict(gate_buffers(temp), o=r_o.rearrange("p a b -> p (a b)"), z=r_g, gain=par["ret_g"], rows=4,
                        o_pair=lambda c: r_o[:, :, 2 * c * P:2 * (c + 1) * P].rearrange("p a (t x) -> p a t x", t=2),
                        rs_pair=lambda v, c: v.rearrange("p (a b) -> p a b", a=2)[:, :, 4 * c:4 * c + 4])
        gate_dn = dict(gate_buffers(Hn), o=d_o.rearrange("p a b -> p (a b)"), z=d_z, gain=par["dn_g"], rows=2,
                       o_pair=lambda c: pairs(d_o, c), rs_pair=None)
        assert j8 <= KT * NTOK
        NORM_ORDER = (2, 3, 0, 1)

        def lowest(t, nband):
            return t if nband == 2 and t == CT else t - 1

        v_ones, n0 = zip(cut(temp, 0, NT, P), cut(temp, NT * P, NT, P))
        m_pT, n1 = cut(temp, n0[1], 3, 512)
        m_rec, n2 = cut(temp, n1, 512)
        m_max, n3 = cut(temp, n2, 2, 4)
        assert n3 <= a8

        def latent_plan(L):
            units = []
            for h in range(H):
                units += ([(h, 0, NCTX, CT)] if L == 0 else []) + [(h, NCTX + 512 * c, NCTX + 512 * c + 512, NT) for c in range(2)]
            tiles = lambda u: [(("max"), u, t) for t in range((units[u][2] - units[u][1]) // P)]
            plan = tiles(0) + [("rows", 0, 0)]
            for u, (h, lo, hi, nk) in enumerate(units):
                ahead = tiles(u + 1) if u + 1 < len(units) else []
                for j in range(nk):
                    plan.append(("keys", u, j))
                    if j:
                        plan.append(("weigh", u, j - 1))
                    if ahead and j % 2 == 1:
                        plan.append(ahead.pop(0))
                plan += ahead
                if u + 1 < len(units):
                    plan.append(("rows", u + 1, 0))
                plan += [("weigh", u, nk - 1), ("done", u, 0)]
                if u + 1 < len(units) and units[u + 1][0] != h:
                    plan.append(("ada", 2 + h, 0))
            return units, plan

        block = ctx.enter_context(nc.Block())

        def start(lane):
            for n_, k_ in CREDITS[lane.name].items():
                lane.e.sem_inc(sems[n_], k_)

        def tokens(L):
            return SEGMENTS if L == 0 else SEGMENTS[1:]

        def tile_cols(t):
            return bass.ds(t * P, P)

        @block.sync
        def _(sp):
            for s in range(2):
                sp.dma_start(ring[:, s, :], d["weights"][s]).then_inc(sems[f"chunk_in_{s}"], 16)
            n_ = 2
            for L in range(DEPTH):
                if L:
                    sp.wait_ge(sems["half_used"], 4 * FG * L)
                end = sum(CHUNKS[:L + 1])
                if n_ % 2:
                    sp.wait_ge(sems["chunk_used"], n_ - 1)
                    sp.dma_start(ring[:, 1, :], d["weights"][n_]).then_inc(sems["chunk_in_1"], 16)
                    n_ += 1
                with sp.Fori(n_ // 2, end // 2) as i:
                    for s in range(2):
                        sp.wait_ge(sems["chunk_used"], 2 * i - 1 + s)
                        sp.dma_start(ring[:, s, :], d["weights"][2 * i + s]).then_inc(sems[f"chunk_in_{s}"], 16)
                if end % 2:
                    sp.wait_ge(sems["chunk_used"], end - 2)
                    sp.dma_start(ring[:, 0, :], d["weights"][end - 1]).then_inc(sems["chunk_in_0"], 16)
                n_ = end
                sp.wait_ge(sems["chunk_used"], end)
                for s in range(2):
                    sp.dma_start(ring[:, s, 0:HALF], d["ff"][4 * FG * L + s]).then_inc(sems[f"half_in_{s}"], 16)
                with sp.Fori(1, 2 * FG) as i:
                    for s in range(2):
                        sp.wait_ge(sems["half_used"], 2 * i + (4 * FG * L - 1 + s))
                        sp.dma_start(ring[:, s, 0:HALF], d["ff"][2 * i + (4 * FG * L + s)]).then_inc(sems[f"half_in_{s}"], 16)
            sp.wait_ge(sems["phase"], 4 * book.get("phases_old", 1))
            sp.dma_start(d["out"], X[:, :, NCTX:NTOK]).then_inc(sems["out_done"], 16)
            sp.wait_ge(sems["out_done"], 16)

        @block.tensor
        def _(pe):
            ln = Lane(pe, "pe", sems, book)
            start(ln)
            nth, tally = ln.nth, ln.tally
            state = {"chunk": 0, "ada": 0}

            def slot(j=0):
                return (state["chunk"] + j) % 2

            def arrived(j=0):
                n_ = state["chunk"] + j
                pe.wait_ge(sems[f"chunk_in_{n_ % 2}"], 16 * (n_ // 2 + 1))
                return ring[:, n_ % 2, :].rearrange("p (k n) -> p k n", k=KT)

            def turn(out, src, rows=P):
                return pe.transpose(out, src, ident[0:rows, 0:rows])

            def ada(L, v):
                if state["ada"] == 0:
                    pe.wait_ge(sems["silu_ready"], 1)
                for s_ in range(2):
                    w = arrived()
                    for j in range(4):
                        for k in range(KT):
                            m = pe.matmul(ps[:, 7, (s_ * 4 + j) * 2:(s_ * 4 + j) * 2 + 2], w[:, k, j * P:(j + 1) * P],
                                          silu_c[:, k, :], start=(k == 0), stop=(k == KT - 1))
                    m.then_inc(sems["chunk_used"], tally("chunk_used"))
                    state["chunk"] += 1
                pe.drain().then_inc(sems["ada_mm"], 1)
                state["ada"] += 1

            def ada_free():
                pe.wait_ge(sems["ada_sum"], state["ada"])

            def tile_products(src, widths, bank, tile=1, per=1, between=()):
                pe.wait_ge(sems["tile_in"], nth("tile_in", tile, per))
                step = 0
                for j, w_ in enumerate(widths):
                    w = ring[:, slot(j), :].rearrange("p (k n) -> p k n", k=KT)
                    for k in range(KT):
                        for at_, other in between:
                            if at_ == step:
                                other()
                        m = pe.matmul(ps[:, bank + j, 0:w_], src[:, k, :], w[:, k, 0:w_],
                                      start=(k == 0), stop=(k == KT - 1), skip_group_check=True)
                        step += 1
                m.then_inc(sems["z_mm"], tally("z_mm"))

            def tile_pipeline(widths, signals, between, last):
                tile_products(hst, widths, 0)
                with ln.loop(NT - 1, [(n_, 1) for n_ in signals]):
                    pe.wait_ge(sems["z_sb"], nth("z_sb", 1, 1))
                    tile_products(hst, widths, 0, 2, 1, between)
                    last()
                for _, other in between:
                    other()
                last()

            def channel_products(n_out, src, cols, first_bank, count0, act_evac, release=True):
                w = arrived()
                n_ = count0
                for j in range(n_out):
                    for lo, hi in cols:
                        bank = first_bank + n_ % 4
                        act_evac(n_)
                        for k in range(KT):
                            m = pe.matmul(ps[:, bank, 0:hi - lo], w[:, k, j * P:(j + 1) * P], src[:, k, lo:hi],
                                          start=(k == 0), stop=(k == KT - 1))
                        m.then_inc(sems["prod"], tally("prod"))
                        n_ += 1
                if release:
                    pe.drain().then_inc(sems["chunk_used"], tally("chunk_used"))
                state["chunk"] += 1
                return n_

            def mla_prep(L):
                arrived()
                pe.wait_ge(sems["weights_in"], 32 * (L + 1))

                def turn_latents():
                    pe.wait_ge(sems["normed"], nth("normed", 1, 1))
                    for j in range(3):
                        m = turn(ps[:, 1, j * P:(j + 1) * P], zst[:, j * P:(j + 1) * P])
                    m.then_inc(sems["cT_mm"], tally("cT_mm"))

                def expand():
                    pe.wait_ge(sems["cT_sb"], nth("cT_sb", 1, 1))
                    for j in range(2):
                        pe.matmul(ps[:, 2, 0:384], m_cT[:, j, :], m_uq[:, j, :], start=(j == 0), stop=(j == 1), skip_group_check=True)
                    pe.matmul(ps[:, 3, :], m_cT[:, 2, :], m_ukv, start=True, stop=True, skip_group_check=True)\
                      .then_inc(sems["up_mm"], tally("up_mm"))

                def turn_heads():
                    pe.wait_ge(sems["qk_roped"], nth("qk_roped", 1, 1))
                    pe.wait_ge(sems["up_v"], nth("up_v", 1, 1))
                    for j in range(8):
                        m = turn(ps[0:96, 4 + j // 4, (j % 4) * P:(j % 4 + 1) * P], m_qk[:, j, :])
                    m.then_inc(sems["qkT_mm"], tally("qkT_mm"))
                    pe.wait_ge(sems["qkT_sb"], nth("qkT_sb", 1, 1))

                tile_pipeline([416], ("tile_in", "z_sb", "normed", "cT_sb", "qk_roped", "qkT_sb", "up_v"),
                              [(4, turn_latents), (6, expand)], turn_heads)
                pe.drain().then_inc(sems["chunk_used"], tally("chunk_used"))
                state["chunk"] += 1

            def attend(count, heads, nk, keys, vals, qsrc, masks):
                rounds = [(r, min(4, nk - r)) for r in range(0, nk, 4)]
                nr = len(rounds)
                per = {"q_staged": 1, "rowmax": 4, "probs": 4, "pT_act": 4 * nr, "y_norm": 1, "yT_sb": 1}

                def body():
                    pe.wait_ge(sems["q_staged"], nth("q_staged", 1, 1))

                    def scores(h):
                        for out, lhs, rhs in keys(h, (h % 2) * 3):
                            m = pe.matmul(out, lhs, rhs, start=True, stop=True)
                        m.then_inc(sems["scores"], tally("scores"))

                    def turn_probs(h):
                        pe.wait_ge(sems["probs"], nth("probs", h + 1, 4))
                        for r, (r0, w_) in enumerate(rounds):
                            for j in range(w_):
                                m = turn(ps[:, turned[r], j * P:(j + 1) * P], probs[h % 2][:, r0 + j, :])
                            m.then_inc(sems["pT_mm"], tally("pT_mm"))

                    def weigh(h):
                        pe.wait_ge(sems["pT_act"], nth("pT_act", (h + 1) * nr, 4 * nr))
                        for j in range(nk):
                            m = pe.matmul(ps[:, 7, h * 64:(h + 1) * 64], pT[h % 2][:, j, :], vals(h, j),
                                          start=(j == 0), stop=(j == nk - 1))
                        m.then_inc(sems["pv"], tally("pv"))

                    scores(0)
                    scores(1)
                    for h in range(H):
                        turn_probs(h)
                        if h + 2 < H:
                            scores(h + 2)
                        weigh(h)
                    pe.wait_ge(sems["y_norm"], nth("y_norm", 1, 1))
                    for j in range(2):
                        m = turn(ps[:, 6, j * P:(j + 1) * P], yst[:, 2 * j:2 * j + 2, :].rearrange("p a b -> p (a b)"))
                    m.then_inc(sems["yT_mm"], tally("yT_mm"))
                    pe.wait_ge(sems["yT_sb"], nth("yT_sb", 1, 1))

                return body, per

            def run(count, make, first, looped=True):
                if looped:
                    with ln.loop(count) as i:
                        body, per = make(first + i)
                        body()
                else:
                    body, per = make(first)
                    body()
                for n_, k_ in per.items():
                    ln.passed(n_, k_ * count)

            def latent_attention(L):
                units, plan = latent_plan(L)
                n_max = n_keys = n_weigh = 0
                flat = ps[:, 0:3, :].rearrange("p a b -> p (a b)")
                fresh_ada = False
                for what, u, j in plan:
                    h, lo, hi, nk = units[u] if what != "ada" else units[0]
                    if what == "max":
                        if n_max:
                            pe.wait_ge(sems["rowmax"], nth("rowmax", n_max))
                        for c in range(0, nk * P, 512):
                            w_ = min(512, nk * P - c)
                            m = pe.matmul(flat[:, c:c + w_], m_q[0:96, h, lo + j * P:lo + (j + 1) * P], m_k[0:96, h, c:c + w_],
                                          start=True, stop=True)
                        m.then_inc(sems["scores"], tally("scores"))
                        n_max += 1
                    if what == "rows":
                        pe.wait_ge(sems["rowmax"], nth("rowmax", n_max))
                        if u:
                            pe.wait_ge(sems["maxrow"], nth("maxrow", u))
                        if fresh_ada:
                            ada_free()
                            fresh_ada = False
                        for t in range((hi - lo) // P):
                            m = turn(ps[0:1, 7, t * P:(t + 1) * P], m_max[:, u % 2, t:t + 1])
                        m.then_inc(sems["maxrow_mm"], tally("maxrow_mm"))
                    if what == "keys":
                        pe.wait_ge(sems["maxrow"], nth("maxrow", u + 1))
                        if n_keys == 0:
                            pe.wait_ge(sems["v_staged"], nth("v_staged", 1))
                        if n_keys >= 2:
                            pe.wait_ge(sems["exped"], nth("exped", n_keys - 1))
                        pe.matmul(ps[:, 3 + n_keys % 2, 0:hi - lo], m_k[0:97, h, j * P:(j + 1) * P], m_q[0:97, h, lo:hi],
                                  start=True, stop=True).then_inc(sems["keyed"], tally("keyed"))
                        n_keys += 1
                    if what == "weigh":
                        if j == 0:
                            pe.wait_ge(sems["v_staged"], nth("v_staged", h + 1))
                            if u >= 2:
                                pe.wait_ge(sems["y_done"], nth("y_done", u - 1))
                        pe.wait_ge(sems["exped"], nth("exped", n_weigh + 1))
                        pe.matmul(ps[:, 5 + u % 2, 0:hi - lo], v_ones[h % 2][:, j, :], m_pT[:, n_weigh % 3, 0:hi - lo],
                                  start=(j == 0), stop=(j == nk - 1)).then_inc(sems["weighed"], tally("weighed"))
                        n_weigh += 1
                    if what == "ada":
                        pe.wait_ge(sems["maxrow"], nth("maxrow", u_rows))
                        ada(L, u)
                        fresh_ada = True
                    if what == "rows":
                        u_rows = u + 1

            def swa_make(nk, nband):
                def make(t):
                    def keys(h, bank):
                        flat = ps[:, bank:bank + 3, :].rearrange("p a b -> p (a b)")
                        at_ = 64 * (h // 2)
                        q_ = qst[at_:at_ + 64, h % 2, :]
                        out = [(flat[:, 0:NCTX], q_, w_kT[at_:at_ + 64, 0:NCTX])]
                        for j in range(nband):
                            out.append((flat[:, (2 + j) * P:(3 + j) * P], q_, kst[at_:at_ + 64, j, :]))
                        return out

                    def vals(h, j):
                        c_ = slice(64 * (h // 2), 64 * (h // 2) + 64)
                        return w_v[:, j, c_] if j < 2 else w_v[:, lowest(t, nband) + (j - 2), c_]
                    return attend(1, H, nk, keys, vals, None, None)
                return make

            def swa_prep():
                arrived()

                def turn_roped():
                    pe.wait_ge(sems["qk_roped"], nth("qk_roped", 1, 1))
                    for j in range(3):
                        m = turn(ps[:, 1, j * P:(j + 1) * P], w_qk[:, j * P:(j + 1) * P])
                    m.then_inc(sems["qkT_mm"], tally("qkT_mm"))

                def turned():
                    pe.wait_ge(sems["qkT_sb"], nth("qkT_sb", 1, 1))

                tile_pipeline([512], ("tile_in", "z_sb", "qk_roped", "qkT_sb"), [(4, turn_roped)], turned)
                pe.drain().then_inc(sems["chunk_used"], tally("chunk_used"))
                state["chunk"] += 1

            def ret_forward():
                arrived()
                arrived(1)

                def turn_and_add():
                    pe.wait_ge(sems["r_roped"], nth("r_roped", 1, 1))
                    for j in range(2):
                        m = turn(ps[:, 2, j * P:(j + 1) * P], r_R[:, j, :])
                    m.then_inc(sems["r_kT_mm"], tally("r_kT_mm"))
                    pe.wait_ge(sems["r_kz"], nth("r_kz", 1, 1))
                    pe.matmul(ps[:, 3, 0:256], r_kz, r_z[:, 256:512], start=True, stop=True, skip_group_check=True)\
                      .then_inc(sems["r_kv"], tally("r_kv"))

                def taken():
                    pe.wait_ge(sems["r_kT_sb"], nth("r_kT_sb", 1, 1))
                    pe.wait_ge(sems["r_state"], nth("r_state", 1, 1))

                tile_pipeline([512, 256], ("tile_in", "r_roped", "r_kT_sb", "r_kz", "r_state", "z_sb"), [(4, turn_and_add)], taken)
                pe.drain().then_inc(sems["chunk_used"], tally("chunk_used", 2))
                state["chunk"] += 2

            def ret_backward(count, first):
                with ln.loop(count, [(n_, 1) for n_ in ("r_stage", "r_probs", "r_kz", "r_o", "r_state")], down_from=first) as i:
                    t = ln.down
                    pe.wait_ge(sems["r_stage"], nth("r_stage", 1, 1))
                    for h in range(H):
                        rows = slice(32 * h, 32 * h + 32)
                        m = pe.matmul(ps[:, h, 0:P], r_qst[rows, 1, :], r_qst[rows, 0, :],
                                      start=True, stop=True)
                    m.then_inc(sems["r_scores"], tally("r_scores"))
                    pe.matmul(ps[:, 4, 0:256], r_qst[:, 2, :], r_S[:, t, :], start=True, stop=False, skip_group_check=True)
                    pe.matmul(ps[:, 4, 0:256], r_qst[:, 3, :], r_Sb, start=False, stop=False, skip_group_check=True)
                    pe.wait_ge(sems["r_probs"], nth("r_probs", 1, 1))
                    for h in range(H):
                        m = pe.matmul(ps[:, 4, h * 64:(h + 1) * 64], r_p[:, h, :], r_v[:, t, h * 64:(h + 1) * 64],
                                      start=False, stop=True, skip_group_check=True)
                    m.then_inc(sems["r_out"], tally("r_out"))
                    pe.wait_ge(sems["r_kz"], nth("r_kz", 1, 1))
                    pe.matmul(ps[:, 3, 0:256], r_kz, r_v[:, t, :], start=True, stop=True).then_inc(sems["r_kv"], tally("r_kv"))
                    pe.wait_ge(sems["r_o"], nth("r_o", 1, 1))
                    pe.wait_ge(sems["r_state"], nth("r_state", 1, 1))

            def dn_project():
                def before(n_):
                    if n_ >= 4:
                        pe.wait_ge(sems["evac_act" if n_ % 2 == 0 else "evac_dve"], nth("evac_act" if n_ % 2 == 0 else "evac_dve", (n_ - 4) // 2 + 1))
                n_ = channel_products(3, Hm, SEGMENTS, 0, 0, before)
                n_ = channel_products(3, Hm, SEGMENTS, 0, n_, before, release=False)
                ln.passed("evac_act", 9)
                ln.passed("evac_dve", 9)
                arrived()
                with ln.loop(NT // 2, [("tile_in", 2), ("z_sb", 2)]):
                    for s_ in range(2):
                        pe.wait_ge(sems["z_sb"], nth("z_sb", s_ - 1, 2))
                        tile_products(d_hst[s_], [272], 4 + s_, 1 + s_, 2)
                state["chunk"] += 1

            def dn_norm():
                pe.wait_ge(sems["d_stage"], nth("d_stage", 1))
                n_ = 0
                for x_, j in enumerate(NORM_ORDER):
                    pe.wait_ge(sems["d_sq"], nth("d_sq", x_ + 1))
                    for lo, hi in norm_segments:
                        if n_ >= 4:
                            pe.wait_ge(sems["d_root"], nth("d_root", n_ - 3))
                        pe.matmul(ps[:, n_ % 4, 0:hi - lo], n_block, n_sq[:, j, lo:hi], start=True, stop=True)\
                          .then_inc(sems["d_sum"], tally("d_sum"))
                        n_ += 1
                pe.wait_ge(sems["d_norm"], nth("d_norm", n_ // 2))
                for t in range(NT):
                    if t >= 4:
                        pe.wait_ge(sems["d_kTs"], nth("d_kTs", t - 3))
                    for j in range(4):
                        m = turn(ps[:, 4 + t % 4, j * P:(j + 1) * P], raw[:, 2 + j, t * P:(t + 1) * P])
                    m.then_inc(sems["d_kT"], tally("d_kT"))

            def dn_scan(count, first, last):
                names = ("u_stage", "u_arg", "u_inv", "u_keg", "u_wsb", "u_vsb", "u_done", "u_dt", "u_gc")
                sig = [(f"{n_}{q}", 1) for n_ in names for q in range(2)]
                sig += [(f"u_tsb{q}", 6) for q in range(2)]
                sig += [(f"u_ysb{q}", 6) for q in range(2)] + [(f"u_usb{q}", 6) for q in range(2)]
                with ln.loop(count, sig, down_from=last) as i:
                    tt = (first + i, ln.down)
                    for q in range(2):
                        b, A, B, C, D = sc[q], *(ps[:, 4 * q + z, :] for z in range(4))
                        pe.wait_ge(sems[f"u_done{q}"], nth(f"u_done{q}", 1, 1))
                        pe.wait_ge(sems[f"u_stage{q}"], nth(f"u_stage{q}", 1, 1))
                        pe.matmul(A, ones, b["gm"].rearrange("p a b -> p (a b)"), start=True, stop=True)
                        lg = d_lg[:, tt[q], 4 * q:4 * q + 4]
                        pe.matmul(D[:, 0:4], tri[:, q, :], lg, start=True, stop=True)
                        pe.matmul(D[:, 4:8], ones, lg, start=True, stop=True).then_inc(sems[f"u_g{q}"], tally(f"u_g{q}"))
                        for h in range(H):
                            rows = slice(64 * (h % 2), 64 * (h % 2) + 64)
                            kk = b["qk"][rows, 2 + h // 2, :]
                            out = (B, C)[h % 2].rearrange("p (a j c) -> p a j c", a=2, j=2)[:, :, h // 2, :]
                            pe.matmul(out[:, 0, :], kk, kk, start=True, stop=True)
                            m = pe.matmul(out[:, 1, :], kk, b["qk"][rows, h // 2, :], start=True, stop=True)
                        m.then_inc(sems[f"u_gram{q}"], tally(f"u_gram{q}"))
                    for lv in range(LEVELS):
                        for q in range(2):
                            b, A, B, C, D = sc[q], *(ps[:, 4 * q + z, :] for z in range(4))
                            if lv == 0:
                                pe.wait_ge(sems[f"u_inv{q}"], nth(f"u_inv{q}", 1, 1))
                            else:
                                pe.wait_ge(sems[f"u_tsb{q}"], nth(f"u_tsb{q}", lv, 6))
                                for h in range(H):
                                    m = pe.matmul(B[:, h * P:(h + 1) * P], b["at"][:, h, :], b["dt"][:, h, :],
                                                  start=True, stop=True)
                                m.then_inc(sems[f"u_ymm{q}"], tally(f"u_ymm{q}"))
                        for q in range(2):
                            b, A, B, C, D = sc[q], *(ps[:, 4 * q + z, :] for z in range(4))
                            if lv:
                                pe.wait_ge(sems[f"u_ysb{q}"], nth(f"u_ysb{q}", lv, 6))
                                for h in range(H):
                                    m = pe.matmul(C[:, h * P:(h + 1) * P], b["ym"][:, h, :], b["u"][:, h, :],
                                                  start=True, stop=True)
                                m.then_inc(sems[f"u_umm{q}"], tally(f"u_umm{q}"))
                        for q in range(2):
                            b, A, B, C, D = sc[q], *(ps[:, 4 * q + z, :] for z in range(4))
                            if lv:
                                pe.wait_ge(sems[f"u_usb{q}"], nth(f"u_usb{q}", lv, 6))
                            if lv < LEVELS - 1:
                                for h in range(H):
                                    m = turn(A[:, h * P:(h + 1) * P], b["u"][:, h, :])
                                m.then_inc(sems[f"u_tmm{q}"], tally(f"u_tmm{q}"))
                    for q in range(2):
                        b, A, B, C, D = sc[q], *(ps[:, 4 * q + z, :] for z in range(4))
                        pe.wait_ge(sems[f"u_keg{q}"], nth(f"u_keg{q}", 1, 1))
                        for h in range(H):
                            r0 = 64 * (h % 2)
                            m = pe.matmul(D[r0:r0 + 64, (h // 2) * P:(h // 2 + 1) * P], b["keg"][:, h * 64:(h + 1) * 64],
                                          b["u"][:, h, :], start=True, stop=True)
                        m.then_inc(sems[f"u_wmm{q}"], tally(f"u_wmm{q}"))
                    for q in range(2):
                        b, A, B, C, D = sc[q], *(ps[:, 4 * q + z, :] for z in range(4))
                        for h in range(H):
                            pe.matmul(B[:, h * 64:(h + 1) * 64], b["u"][:, h, :], kv_tok[:, tt[q], 256 + h * 64:320 + h * 64],
                                      start=(h == 0), stop=False, skip_group_check=True)
                        pe.wait_ge(sems[f"u_wsb{q}"], nth(f"u_wsb{q}", 1, 1))
                        for j in range(2):
                            m = pe.matmul(B[:, j * P:(j + 1) * P], b["wt"][:, j * P:(j + 1) * P], b["S"][:, j, :],
                                          start=False, stop=True, skip_group_check=True)
                        m.then_inc(sems[f"u_vmm{q}"], tally(f"u_vmm{q}"))
                    for q in range(2):
                        b, A, B, C, D = sc[q], *(ps[:, 4 * q + z, :] for z in range(4))
                        for j in range(2):
                            pe.matmul(C[:, j * P:(j + 1) * P], b["qk"][:, j, :], b["S"][:, j, :],
                                      start=(j == 0), stop=True, skip_group_check=True)
                        pe.wait_ge(sems[f"u_vsb{q}"], nth(f"u_vsb{q}", 1, 1))
                        for h in range(H):
                            pe.matmul(C[:, 256 + h * 64:320 + h * 64], b["qkd"][:, h, :], b["vn"][:, h * 64:(h + 1) * 64],
                                      start=False, stop=True, skip_group_check=True)
                        for j in range(2):
                            m = pe.matmul(A[:, j * P:(j + 1) * P], b["kt"][:, j * P:(j + 1) * P],
                                          b["vn"][:, j * P:(j + 1) * P], start=True, stop=True)
                        m.then_inc(sems[f"u_omm{q}"], tally(f"u_omm{q}"))

            def gate_turn(g_):
                for c in range(NT // 2):
                    pe.wait_ge(sems["g_y"], nth("g_y", c + 1))
                    if c >= 2:
                        pe.wait_ge(sems["yT_sb"], nth("yT_sb", c - 1))
                    for s_ in range(2):
                        for j in range(2):
                            m = turn(ps[:, 5 + c % 2, j * 2 * P + s_ * P:j * 2 * P + (s_ + 1) * P], g_["out"][:, 2 * c + s_, j * P:(j + 1) * P])
                    m.then_inc(sems["yT_mm"], tally("yT_mm"))

            def project_out(L):
                def before(n_):
                    if n_ >= 4:
                        pe.wait_ge(sems["evac_dve"], nth("evac_dve", n_ - 3))
                n_ = channel_products(4, Y, tokens(L), 0, 0, before)
                n_ = channel_products(4, Y, tokens(L), 0, n_, before)
                ln.passed("evac_dve", n_)

            def mlp(L):
                cols = tokens(L)
                up, down = 4 * len(cols), 8 * len(cols)

                def product(bank, w, j, x, k_n, lo, hi):
                    for k in range(k_n):
                        for part, (a, b) in enumerate(((0, 0), (1, 0), (0, 1))):
                            m = pe.matmul(ps[:, bank, 0:hi - lo], w[a][:, k, j * P:(j + 1) * P],
                                          x[b][:, k, lo:hi], start=(k == 0 and part == 0),
                                          stop=(k == k_n - 1 and part == 2))
                    return m

                pe.wait_ge(sems["h_split"], nth("h_split", KT))
                with ln.loop(FG, [("relu", up), ("hidden", up), ("evac_dve", down), ("split", 4)]):
                    n_ = 0
                    for s in range(2):
                        pe.wait_ge(sems["split"], nth("split", s + 1, 4))
                        w = [a[s].rearrange("p (k n) -> p k n", k=KT) for a in (half_hi, half_lo)]
                        for j in range(2):
                            for lo, hi in cols:
                                if n_ >= 4:
                                    pe.wait_ge(sems["relu"], nth("relu", n_ - 3, up))
                                product(n_ % 4, w, j, (H_hi, H_lo), KT, lo, hi).then_inc(sems["prod"], tally("prod"))
                                n_ += 1
                        pe.drain().then_inc(sems["half_used"], tally("half_used"))
                    n_ = 0
                    pe.wait_ge(sems["evac_dve"], nth("evac_dve", 0, down))
                    for s in range(2):
                        pe.wait_ge(sems["split"], nth("split", s + 3, 4))
                        w = [a[s].rearrange("p (k n) -> p k n", k=FW // P) for a in (half_hi, half_lo)]
                        for j in range(4):
                            for c, (lo, hi) in enumerate(cols):
                                if s == 0 and j == 0:
                                    pe.wait_ge(sems["hidden"], nth("hidden", 3 * len(cols) + c + 1, up))
                                if n_ >= 4:
                                    pe.wait_ge(sems["evac_dve"], nth("evac_dve", n_ - 3, down))
                                product(4 + n_ % 4, w, j, (U_hi, U_lo), FW // P, lo, hi).then_inc(sems["prod"], tally("prod"))
                                n_ += 1
                        pe.drain().then_inc(sems["half_used"], tally("half_used"))

            def layer_norm(L):
                for name, src in (("ln_mean", X), ("ln_var", Hm)):
                    for c, (lo, hi) in enumerate(tokens(L)):
                        if name == "ln_var":
                            pe.wait_ge(sems["ln_square"], nth("ln_square", c + 1))
                        for k in range(KT):
                            m = pe.matmul(ps[:, c + (3 if name == "ln_var" else 0), 0:hi - lo], mean_w, src[:, k, lo:hi],
                                          start=(k == 0), stop=(k == KT - 1))
                        m.then_inc(sems[name], tally(name))
                ln.passed("ln_square", len(tokens(L)))

            pe.wait_ge(sems["consts_in"], 32)
            for L in range(DEPTH):
                ln.barrier()
                if L == 0:
                    ada(0, 0)
                    ada_free()
                    ada(0, 1)
                ln.barrier()
                ln.barrier()
                mla_prep(L)
                ln.barrier()
                latent_attention(L)
                ln.barrier()
                ln.barrier()
                ret_forward()
                ln.barrier()
                ada(L, 5)
                ret_backward(CT, CT - 1)
                ret_backward(NT - CT, NT - 1)
                ln.barrier()
                gate_turn(gate_ret)
                ln.barrier()
                swa_prep()
                ln.barrier()
                if L == 0:
                    ada(1, 0)
                    run(CT, swa_make(2, 0), 0)
                run(1, swa_make(4, 2), CT, False)
                run(NT - CT - 2, swa_make(5, 3), CT + 1)
                run(1, swa_make(4, 2), NT - 1, False)
                ln.barrier()
                dn_project()
                ln.barrier()
                ln.barrier()
                dn_norm()
                ln.barrier()
                dn_scan(CT, 0, CT - 1)
                dn_scan(NT - CT, CT, NT - 1)
                ln.barrier()
                pe.drain().then_inc(sems["chunk_used"], tally("chunk_used", 2))
                gate_turn(gate_dn)
                ln.barrier()
                project_out(L)
                ln.barrier()
                if L == 0:
                    ada(1, 1)
                layer_norm(L)
                ln.barrier()
                ln.barrier()
                mlp(L)
                ln.barrier()
                layer_norm(L)
                ln.barrier()

        @block.scalar
        def _(act):
            ln = Lane(act, "act", sems, book)
            start(ln)
            nth, tally = ln.nth, ln.tally
            A = act.activation

            def flat(ap):
                return ap.rearrange("p a b -> p (a b)")

            def silu_conditions():
                A(flat(silu_c[:]), flat(cc[:]), ACT.Tanh, scale=0.5).then_inc(sems["silu_c"], 1)

            def modulate(L, shift, scale):
                mod = mods[:, L]
                with ln.loop(KT) as k:
                    A(Hm[:, k, NCTX:NTOK], X[:, k, NCTX:NTOK], ACT.Identity, bias=mod[:, shift + k, 0:1],
                          scale=mod[:, scale + k, 0:1]).then_inc(sems["h_lat"], tally("h_lat"))

            def mla_prep():
                with ln.loop(NT, [(n_, 1) for n_ in ("z_mm", "cT_mm", "up_mm", "qkT_mm")]) as i:
                    act.wait_ge(sems["z_mm"], nth("z_mm", 1, 1))
                    ln.link(A(zst[:, 0:416], ps[:, 0, 0:416], ACT.Copy))
                    act.sem_inc(sems["z_sb"], tally("z_sb"))
                    A(m_sq[:, 0:256], zst[:, 0:256], ACT.Square, accum_out=ss[:, 0:1])
                    ln.link(A(m_sq[:, 256:384], zst[:, 256:384], ACT.Square, accum_out=ss[:, 1:2]))
                    act.sem_inc(sems["ss"], tally("ss"))
                    act.wait_ge(sems["cT_mm"], nth("cT_mm", 1, 1))
                    for j in range(3):
                        g_ = par["q_norm"][:, j:j + 1] if j < 2 else par["kv_norm"]
                        m = A(m_cT[:, j, :], ps[:, 1, j * P:(j + 1) * P], ACT.Copy, scale=g_)
                    m.then_inc(sems["cT_sb"], tally("cT_sb"))
                    act.wait_ge(sems["up_mm"], nth("up_mm", 1, 1))
                    A(m_qk[:, 4:8, 0:64], ps[:, 3, :].rearrange("p (h c) -> p h c", h=H)[:, :, 0:64], ACT.Copy)
                    A(m_v[:, i, :].rearrange("p (h c) -> p h c", h=H),
                          ps[:, 3, :].rearrange("p (h c) -> p h c", h=H)[:, :, 64:128], ACT.Copy).then_inc(sems["up_v"], tally("up_v"))
                    act.wait_ge(sems["qkT_mm"], nth("qkT_mm", 1, 1))
                    A(m_q[0:96, :, tile_cols(i)], ps[0:96, 4, :].rearrange("p (h c) -> p h c", h=H), ACT.Copy)
                    A(m_k[0:96, :, tile_cols(i)], ps[0:96, 5, :].rearrange("p (h c) -> p h c", h=H), ACT.Copy).then_inc(sems["qkT_sb"], tally("qkT_sb"))

            def attend(nk, scale, sink, rows, t):
                rounds = [(r, min(4, nk - r)) for r in range(0, nk, 4)]
                nr = len(rounds)
                per = {"rowmax": 4, "pT_mm": 4 * nr, "yT_mm": 1, "pv": 4, "den": 0}

                def exp(h):
                    act.wait_ge(sems["rowmax"], nth("rowmax", h + 1, 4))
                    src = ps[:, 3 * (h % 2):3 * (h % 2) + 3, :].rearrange("p a b -> p (a b)")[:, 0:nk * P]
                    if sink:
                        A(esink[:, h:h + 1], par["sink"][:, h:h + 1], ACT.Exp, bias=rowneg[:, h:h + 1])
                    A(probs[h % 2][:, 0:nk, :].rearrange("p a b -> p (a b)"), src, ACT.Exp, bias=rowneg[:, h:h + 1],
                          scale=scale, accum_out=den[:, h:h + 1]).then_inc(sems["probs"], tally("probs"))

                def body():
                    exp(0)
                    for h in range(H):
                        if h + 1 < H:
                            exp(h + 1)
                        for r, (r0, w_) in enumerate(rounds):
                            act.wait_ge(sems["pT_mm"], nth("pT_mm", h * nr + r + 1, 4 * nr))
                            if r == 0 and h >= 2:
                                act.wait_ge(sems["pv"], nth("pv", h - 1, 4))
                            A(pT[h % 2][:, r0:r0 + w_, :].rearrange("p a b -> p (a b)"), ps[:, turned[r], 0:w_ * P], ACT.Copy).then_inc(sems["pT_act"], tally("pT_act"))
                    act.wait_ge(sems["yT_mm"], nth("yT_mm", 1, 1))
                    A(Y[:, rows:rows + 2, tile_cols(t)], ps[:, 6, 0:256].rearrange("p (a b) -> p a b", a=2), ACT.Copy).then_inc(sems["yT_sb"], tally("yT_sb"))
                return body, per

            def run(count, nk, scale, sink, rows, first, looped=True):
                if looped:
                    with ln.loop(count) as i:
                        body, per = attend(nk, scale, sink, rows, first + i)
                        body()
                else:
                    body, per = attend(nk, scale, sink, rows, first)
                    body()
                for n_, k_ in per.items():
                    ln.passed(n_, k_ * count)

            def latent_attention(L):
                units, plan = latent_plan(L)
                n_ = 0
                for what, u, j in plan:
                    if what == "keys":
                        h, lo, hi, nk = units[u]
                        act.wait_ge(sems["keyed"], nth("keyed", n_ + 1))
                        if n_ >= 3:
                            act.wait_ge(sems["weighed"], nth("weighed", n_ - 2))
                        A(m_pT[:, n_ % 3, 0:hi - lo], ps[:, 3 + n_ % 2, 0:hi - lo], ACT.Exp, scale=96 ** -0.5)\
                            .then_inc(sems["exped"], tally("exped"))
                        n_ += 1

            def swa_prep():
                with ln.loop(NT, [("z_mm", 1), ("qkT_mm", 1)]) as i:
                    act.wait_ge(sems["z_mm"], nth("z_mm", 1, 1))
                    A(zst[:, 0:512], ps[:, 0, :], ACT.Copy).then_inc(sems["z_sb"], tally("z_sb"))
                    act.wait_ge(sems["qkT_mm"], nth("qkT_mm", 1, 1))
                    A(w_qT[:, :, tile_cols(i)], ps[:, 1, 0:256].rearrange("p (a b) -> p a b", a=2), ACT.Copy)
                    A(w_kT[:, tile_cols(i)], ps[:, 1, 256:384], ACT.Copy).then_inc(sems["qkT_sb"], tally("qkT_sb"))

            def ret_tables():
                ln.link(A(lg_ret, par["log1m"], ACT.Exp))
                A(lg_row, par["log1m_row"], ACT.Exp).then_inc(sems["tables"], tally("tables"))
                act.wait_ge(sems["sk"], nth("sk", 1))
                A(lg_ret, lg_ret, ACT.Ln)
                ln.link(A(lg_row, lg_row, ACT.Ln))
                for q in range(2):
                    for h in range(H):
                        A(r_qst[:, h, :] if q == 0 else r_p[:, h, :], rel[:, q, :], ACT.Exp, scale=lg_ret[:, 4 * q + h:4 * q + h + 1])
                    A(zeta[:, q, :], lg_ret[:, 4 * q:4 * q + 4], ACT.Exp, scale=cst["left"][:, q:q + 1])
                    A(r_xi[:, q, :], age[:, q, :], ACT.Exp, scale=lg_row[:, q:q + 1])
                    m = A(gch[:, q:q + 1], lg_row[:, q:q + 1], ACT.Exp, scale=float(P))
                m.then_inc(sems["tables"], tally("tables"))
                ln.passed("sk", 1)

            def ret_forward():
                with ln.loop(NT, [(n_, 1) for n_ in ("z_mm", "r_kT_mm", "r_roped", "r_kv")]) as i:
                    act.wait_ge(sems["z_mm"], nth("z_mm", 1, 1))
                    A(r_z[:, 0:512], ps[:, 0, :], ACT.Copy)
                    ln.link(A(r_z[:, 512:768], ps[:, 1, 0:256], ACT.Copy))
                    act.sem_inc(sems["z_sb"], tally("z_sb"))
                    A(r_v[:, i, :], r_z[:, 256:512], ACT.Copy)
                    ln.link(A(r_g[:, i, :], r_z[:, 512:768], ACT.Copy))
                    act.wait_ge(sems["r_roped"], nth("r_roped", 1, 1))
                    A(r_k[:, i, :], r_R[:, 1, :], ACT.Copy)
                    act.wait_ge(sems["r_kT_mm"], nth("r_kT_mm", 1, 1))
                    A(r_qkT[:, 0, tile_cols(i)], ps[:, 2, 0:P], ACT.Copy, scale=float(32 ** -0.5))
                    A(r_qkT[:, 1, tile_cols(i)], ps[:, 2, P:2 * P], ACT.Copy).then_inc(sems["r_kT_sb"], tally("r_kT_sb"))
                    act.wait_ge(sems["r_kv"], nth("r_kv", 1, 1))

            def dn_project():
                for n_ in range(0, 18, 2):
                    j, (lo, hi) = n_ // 3, SEGMENTS[n_ % 3]
                    act.wait_ge(sems["prod"], nth("prod", n_ + 1))
                    off = 2 if lo < NCTX else 6
                    A(raw[:, j, lo + off:hi + off], ps[:, n_ % 4, 0:hi - lo], ACT.Copy).then_inc(sems["evac_act"], tally("evac_act"))
                ln.passed("prod", 18)
                with ln.loop(NT // 2, [("z_mm", 2)]) as i:
                    for s_ in range(2):
                        act.wait_ge(sems["z_mm"], nth("z_mm", 1 + s_, 2))
                        A(d_z[:, 2 * i + s_, :], ps[:, 4 + s_, 0:256], ACT.Copy)
                        A(d_ab[:, 2 * i + s_, :], ps[:, 4 + s_, 256:272], ACT.Copy).then_inc(sems["z_sb"], tally("z_sb"))

            def dn_gates_():
                ab = d_ab.rearrange("p t (q a h) -> p t q a h", q=2, a=2)
                act.wait_ge(sems["dn_gates"], nth("dn_gates", 1))
                A(nega, par["a_log"], ACT.Exp)
                ln.link(A(flat(d_w), flat(d_w), ACT.Exp))
                for q in range(2):
                    m = A(d_bt[:, :, 4 * q:4 * q + 4], ab[:, :, q, 1, :], ACT.Tanh, scale=0.5)
                m.then_inc(sems["dn_gates2"], tally("dn_gates2"))
                act.wait_ge(sems["dn_gates"], nth("dn_gates", 2))
                A(flat(d_w), flat(d_w), ACT.Ln).then_inc(sems["dn_gates2"], tally("dn_gates2"))
                ln.passed("dn_gates", 2)

            def dn_conv():
                with ln.loop(6, [("c_y", 1)]):
                    act.wait_ge(sems["c_y"], nth("c_y", 1, 1))
                    A(cv_t, cv_y, ACT.Tanh, scale=0.5).then_inc(sems["c_tanh"], tally("c_tanh"))

            def dn_norm():
                for j in NORM_ORDER:
                    A(n_sq[:, j, :], raw[:, j, 0:NTOK], ACT.Square).then_inc(sems["d_sq"], tally("d_sq"))
                act.wait_ge(sems["d_stage"], nth("d_stage", 1))
                n_ = 0
                for j in NORM_ORDER:
                    for lo, hi in norm_segments:
                        act.wait_ge(sems["d_sum"], nth("d_sum", n_ + 1))
                        if n_ >= 4:
                            act.wait_ge(sems["d_norm"], nth("d_norm", n_ - 3))
                        q_ = 0 if j < 2 else 1
                        A(n_root[:, n_ % 4, 0:hi - lo], ps[:, n_ % 4, 0:hi - lo], ACT.Sqrt, bias=n_eps[:, q_:q_ + 1],
                          scale=(64.0, 1.0)[q_]).then_inc(sems["d_root"], tally("d_root"))
                        n_ += 1
                for t in range(NT):
                    act.wait_ge(sems["d_kT"], nth("d_kT", t + 1))
                    A(kv_tok[:, t, 0:256], ps[:, 4 + t % 4, 0:256], ACT.Copy)
                    A(kv_tok[:, t, 256:512], ps[:, 4 + t % 4, 256:512], ACT.Copy, scale=0.5).then_inc(sems["d_kTs"], tally("d_kTs"))

            def dn_scan(count, first, last):
                sig = [(f"{n_}{q}", 1) for n_ in ("u_arg", "u_wmm", "u_e") for q in range(2)] + [(f"u_tmm{q}", 6) for q in range(2)]
                with ln.loop(count, sig, down_from=last) as i:
                    for q in range(2):
                        b = sc[q]
                        act.wait_ge(sems[f"u_arg{q}"], nth(f"u_arg{q}", 1, 1))
                        A(egt[q], tl[q], ACT.Exp)
                        A(flat(b["dt"]), flat(b["dt"]), ACT.Exp).then_inc(sems[f"u_dt{q}"], tally(f"u_dt{q}"))
                    for lv in range(LEVELS - 1):
                        for q in range(2):
                            act.wait_ge(sems[f"u_tmm{q}"], nth(f"u_tmm{q}", lv + 1, 6))
                            A(flat(sc[q]["dt"]), ps[:, 4 * q, :], ACT.Copy).then_inc(sems[f"u_tsb{q}"], tally(f"u_tsb{q}"))
                    for q in range(2):
                        act.wait_ge(sems[f"u_wmm{q}"], nth(f"u_wmm{q}", 1, 1))
                        A(sc[q]["wt"], ps[:, 4 * q + 3, 0:256], ACT.Copy, scale=-1.0).then_inc(sems[f"u_wsb{q}"], tally(f"u_wsb{q}"))

            def gate(g_):
                A(g_["sq"].rearrange("p a b -> p (a b)"), g_["o"], ACT.Square).then_inc(sems["g_sq"], tally("g_sq"))
                A(flat(g_["th"]), flat(g_["z"]), ACT.Tanh, scale=0.5).then_inc(sems["g_tanh"], tally("g_tanh"))
                act.wait_ge(sems["g_veps"], nth("g_veps", 1))
                A(g_["root"], g_["root"], ACT.Sqrt).then_inc(sems["g_rstd"], tally("g_rstd"))
                for c in range(NT // 2):
                    act.wait_ge(sems["yT_mm"], nth("yT_mm", c + 1))
                    A(Y[:, g_["rows"]:g_["rows"] + 2, 2 * c * P:2 * (c + 1) * P], ps[:, 5 + c % 2, :].rearrange("p (a b) -> p a b", a=2), ACT.Copy)\
                        .then_inc(sems["yT_sb"], tally("yT_sb"))

            def mlp(L):
                cols = tokens(L)
                up, all_ = 4 * len(cols), 12 * len(cols)
                first = cols[0][0]
                for k in range(KT):
                    A(H_hi[:, k, first:NTOK], Hm[:, k, first:NTOK], ACT.Copy).then_inc(sems["h_high"], tally("h_high"))
                with ln.loop(FG, [("prod", all_)]):
                    for n_ in range(up):
                        j, (lo, hi) = n_ // len(cols), cols[n_ % len(cols)]
                        act.wait_ge(sems["prod"], nth("prod", n_ + 1, all_))
                        ln.link(A(U[:, j, lo:hi], ps[:, n_ % 4, 0:hi - lo], ACT.Relu))
                        act.sem_inc(sems["relu"], tally("relu"))
                        A(U_hi[:, j, lo:hi], U[:, j, lo:hi], ACT.Square).then_inc(sems["sq_done"], tally("sq_done"))

            def layer_norm(L, g_, b_):
                for c, (lo, hi) in enumerate(tokens(L)):
                    act.wait_ge(sems["ln_centred"], nth("ln_centred", c + 1))
                    A(Hm[:, :, lo:hi], X[:, :, lo:hi], ACT.Square).then_inc(sems["ln_square"], tally("ln_square"))
                for c, (lo, hi) in enumerate(tokens(L)):
                    act.wait_ge(sems["ln_veps"], nth("ln_veps", c + 1))
                    A(ln_r[:, c, 0:hi - lo], ln_r[:, c, 0:hi - lo], ACT.Sqrt).then_inc(sems["ln_root"], tally("ln_root"))
                for c, (lo, hi) in enumerate(tokens(L)):
                    act.wait_ge(sems["ln_scaled"], nth("ln_scaled", c + 1))
                    for k in range(KT):
                        A(X[:, k, lo:hi], X[:, k, lo:hi], ACT.Identity, bias=par[b_][:, k:k + 1], scale=par[g_][:, k:k + 1])
                ln.passed("ln_centred", len(tokens(L)))
                ln.passed("ln_scaled", len(tokens(L)))

            act.dma_start(consts[:], d["consts"]).then_inc(sems["consts_in"], 16)
            act.dma_start(ada_b[:], d["ada_b"]).then_inc(sems["consts_in"], 16)
            act.dma_start(cc[:], d["cc"]).then_inc(sems["x_in"], 16)
            act.dma_start(X[:], d["x"]).then_inc(sems["x_in"], 16)
            act.wait_ge(sems["x_in"], 32)
            for L in range(DEPTH):
                act.dma_start(params[:], d["params"][L]).then_inc(sems["params_in"], 16)
                act.wait_ge(sems["params_in"], 16 * (L + 1))
                ln.barrier()
                if L == 0:
                    silu_conditions()
                ln.barrier()
                modulate(L, SH1, SC1)
                act.dma_start(m_uq, d["w_uq"][L]).then_inc(sems["weights_in"], 16)
                act.dma_start(m_ukv, d["w_ukv"][L]).then_inc(sems["weights_in"], 16)
                ln.barrier()
                mla_prep()
                ln.barrier()
                latent_attention(L)
                ln.barrier()
                ret_tables()
                ln.barrier()
                ret_forward()
                ln.barrier()
                ln.barrier()
                gate(gate_ret)
                ln.barrier()
                swa_prep()
                ln.barrier()
                if L == 0:
                    run(CT, 2, 0.125, True, 0, 0)
                run(1, 4, 0.125, True, 0, CT, False)
                run(NT - CT - 2, 5, 0.125, True, 0, CT + 1)
                run(1, 4, 0.125, True, 0, NT - 1, False)
                ln.barrier()
                dn_project()
                ln.barrier()
                act.dma_start(Hn[:, j0:j1], d["levels"]).then_inc(sems["masks_in"], 16)
                dn_gates_()
                dn_conv()
                ln.barrier()
                dn_norm()
                ln.barrier()
                act.wait_ge(sems["masks_in"], 16 * (L + 1))
                dn_scan(CT, 0, CT - 1)
                dn_scan(NT - CT, CT, NT - 1)
                ln.barrier()
                gate(gate_dn)
                ln.barrier()
                ln.barrier()
                layer_norm(L, "ln1_g", "ln1_b")
                ln.barrier()
                modulate(L, SH2, SC2)
                ln.barrier()
                mlp(L)
                ln.barrier()
                layer_norm(L, "ln2_g", "ln2_b")
                ln.barrier()

        @block.vector
        def _(dve):
            ln = Lane(dve, "dve", sems, book)
            start(ln)
            nth, tally, link = ln.nth, ln.tally, ln.link
            state = {"ada": 0}
            TT, TS, STT = dve.tensor_tensor, dve.tensor_scalar, dve.scalar_tensor_tensor

            def flat(ap):
                return ap.rearrange("p a b -> p (a b)")

            def ada(L, v):
                if state["ada"] == 0:
                    dve.wait_ge(sems["silu_c"], 1)
                    link(STT(silu_c[:], silu_c[:], 1.0, cc[:], ALU.add, ALU.mult))
                    dve.sem_inc(sems["silu_ready"], 1)
                state["ada"] += 1
                dve.wait_ge(sems["ada_mm"], state["ada"])
                out = mods[:, L, 8 * v:8 * v + 8, :]
                m = STT(out, ps[:, 7, 0:16].rearrange("p (a b) -> p a b", b=2), 0.5, spread(ada_b[:, L, 8 * v:8 * v + 8], 2, 2),
                        ALU.mult, ALU.add)
                if v in (1, 4):
                    link(m)
                    m = TS(out, out, 1.0, None, ALU.add)
                m.then_inc(sems["ada_sum"], 1)

            def modulate(L, shift, scale):
                mod = mods[:, L]
                for k in range(KT):
                    link(TS(Hm[:, k, 0:NCTX], X[:, k, 0:NCTX], mod[:, scale + k, 1:2], mod[:, shift + k, 1:2], ALU.mult, ALU.add))
                    dve.wait_ge(sems["h_lat"], nth("h_lat", k + 1))
                    TS(X[:, k, :], X[:, k, :], ALPHA, None, ALU.mult)

            def rotate(x, a_, b_, cos, sin, out, n):
                heads = x.shape[1]
                c_ = spread(spread(cos, 1, 2), 1, heads)
                s_ = spread(spread(sin, 1, 2), 1, heads)
                TT(a_, x, c_, ALU.mult)
                link(TT(b_, x, s_, ALU.mult))
                TT(out[:, :, 0, :], a_[:, :, 0, :], b_[:, :, 1, :], ALU.subtract)
                return TT(out[:, :, 1, :], b_[:, :, 0, :], a_[:, :, 1, :], ALU.add)

            def mla_prep():
                halves = lambda ap: ap.rearrange("p h (a c) -> p h a c", a=2)
                with ln.loop(NT, [(n_, 1) for n_ in ("ss", "rstd", "up_mm", "qkT_mm", "up_v")]) as i:
                    dve.wait_ge(sems["ss"], nth("ss", 1, 1))
                    TS(rs[:, 0:1], ss[:, 0:1], 1.0 / 256, EPS, ALU.mult, ALU.add)
                    TS(rs[:, 1:2], ss[:, 1:2], 1.0 / 128, EPS, ALU.mult, ALU.add).then_inc(sems["veps"], tally("veps"))
                    dve.wait_ge(sems["rstd"], nth("rstd", 1, 1))
                    TS(zst[:, 0:256], zst[:, 0:256], rs2[:, 0:1], None, ALU.mult)
                    TS(zst[:, 256:384], zst[:, 256:384], rs2[:, 1:2], None, ALU.mult).then_inc(sems["normed"], tally("normed"))
                    dve.wait_ge(sems["up_mm"], nth("up_mm", 1, 1))
                    TS(m_qk[:, 0:4, :], ps[:, 2, 0:384].rearrange("p (h c) -> p h c", h=H), 1.0, None, ALU.mult)
                    link(TS(m_qk[:, 4:8, 64:96], spread(zst[:, 384:416], 1, H), 1.0, None, ALU.mult))
                    x = halves(m_qk[:, :, 64:96])
                    rotate(x, halves(m_a), halves(m_b), rope[:, i, 96:112], rope[:, i, 112:128], x, 16).then_inc(sems["qk_roped"], tally("qk_roped"))
                    dve.wait_ge(sems["qkT_mm"], nth("qkT_mm", 1, 1))

            def attend(nk, scale, sink, masks):
                per = {"scores": 4, "pv": 4, "probs": 4, "yT_mm": 1}

                def row_max(h):
                    flatps = ps[:, 3 * (h % 2):3 * (h % 2) + 3, :].rearrange("p a b -> p (a b)")
                    dve.wait_ge(sems["scores"], nth("scores", h + 1, 4))
                    for j, side in masks:
                        s_ = flatps[:, j * P:(j + 1) * P]
                        m = TT(s_, s_, window[:, side, :], ALU.add)
                    if masks:
                        link(m)
                    link(dve.tensor_reduce(sume[:, h:h + 1], flatps[:, 0:nk * P], AX.X, ALU.max))
                    if sink:
                        m = TS(rowneg[:, h:h + 1], sume[:, h:h + 1], -scale, nsink[:, h:h + 1], ALU.mult, ALU.min)
                    else:
                        m = TS(rowneg[:, h:h + 1], sume[:, h:h + 1], -scale, None, ALU.mult)
                    m.then_inc(sems["rowmax"], tally("rowmax"))

                def body():
                    for h in range(H):
                        row_max(h)
                    dve.wait_ge(sems["probs"], nth("probs", 4, 4))
                    if sink:
                        link(TT(den, den, esink, ALU.add))
                    link(dve.reciprocal(rden, den))
                    dve.wait_ge(sems["pv"], nth("pv", 4, 4))
                    TT(yst, ps[:, 7, 0:256].rearrange("p (h c) -> p h c", h=H), spread(rden, 2, 64), ALU.mult).then_inc(sems["y_norm"], tally("y_norm"))
                    dve.wait_ge(sems["yT_mm"], nth("yT_mm", 1, 1))
                return body, per

            def run(count, nk, scale, sink, masks, looped=True):
                body, per = attend(nk, scale, sink, masks)
                if looped:
                    with ln.loop(count):
                        body()
                else:
                    body()
                for n_, k_ in per.items():
                    ln.passed(n_, k_ * count)

            def latent_attention(L):
                units, plan = latent_plan(L)
                n_max = n_weigh = 0
                flatps = ps[:, 0:3, :].rearrange("p a b -> p (a b)")
                for what, u, j in plan:
                    h, lo, hi, nk = units[u] if what != "ada" else units[0]
                    if what == "max":
                        n_max += 1
                        dve.wait_ge(sems["scores"], nth("scores", n_max))
                        dve.tensor_reduce(m_max[:, u % 2, j:j + 1], flatps[:, 0:nk * P], AX.X, ALU.max)\
                           .then_inc(sems["rowmax"], tally("rowmax"))
                    if what == "rows":
                        dve.wait_ge(sems["maxrow_mm"], nth("maxrow_mm", u + 1))
                        TS(m_q[96:97, h, lo:hi], ps[0:1, 7, 0:hi - lo], -1.0, None, ALU.mult)\
                            .then_inc(sems["maxrow"], tally("maxrow"))
                    if what == "done":
                        n_weigh += nk
                        dve.wait_ge(sems["weighed"], nth("weighed", n_weigh))
                        if u:
                            dve.wait_ge(sems["y_done"], nth("y_done", u))
                        y_, l_ = (slice(0, 64), slice(64, 128)) if h % 2 == 0 else (slice(64, 128), slice(0, 64))
                        link(dve.reciprocal(m_rec[y_, 0:hi - lo], ps[l_, 5 + u % 2, 0:hi - lo]))
                        TT(Y[y_, 6 + h // 2, lo:hi], ps[y_, 5 + u % 2, 0:hi - lo], m_rec[y_, 0:hi - lo], ALU.mult)\
                            .then_inc(sems["y_done"], tally("y_done"))
                    if what == "ada":
                        ada(L, u)

            def swa_prep():
                x = lambda ap: ap.rearrange("p (h a c) -> p h a c", h=6, a=2)
                link(TS(nsink, par["sink"], -1.0, None, ALU.mult))
                with ln.loop(NT, [("z_sb", 1), ("qkT_mm", 1)]) as i:
                    dve.wait_ge(sems["z_sb"], nth("z_sb", 1, 1))
                    TS(w_v[:, i, :], zst[:, 384:512], 1.0, None, ALU.mult)
                    rotate(x(zst[:, 0:384]), x(w_a), x(w_b), rope[:, i, 0:32], rope[:, i, 32:64], x(w_qk), 32).then_inc(sems["qk_roped"], tally("qk_roped"))
                    dve.wait_ge(sems["qkT_mm"], nth("qkT_mm", 1, 1))

            def ret_tables():
                dve.wait_ge(sems["tables"], nth("tables", 1))
                TS(lg_ret, lg_ret, -1.0, 1.0, ALU.mult, ALU.add)
                TS(lg_row, lg_row, -1.0, 1.0, ALU.mult, ALU.add).then_inc(sems["sk"], tally("sk"))
                dve.wait_ge(sems["tables"], nth("tables", 2))
                ln.passed("tables", 2)
                TT(r_qst, r_qst, spread(tri[:, 0, :], 1, H), ALU.mult)
                link(TT(r_p, r_p, spread(tri[:, 1, :], 1, H), ALU.mult))
                link(TT(r_dt, r_qst, r_p, ALU.add))
                link(dve.memset(r_S[:, 0, :], 0.0))

            def ret_forward():
                x = lambda ap: ap.rearrange("p (h a c) -> p h a c", h=8, a=2)
                hd = lambda ap: ap.rearrange("p (h c) -> p h c", h=H)
                with ln.loop(NT, [(n_, 1) for n_ in ("z_sb", "r_kT_mm", "r_kv", "r_kT_sb")]) as i:
                    dve.wait_ge(sems["z_sb"], nth("z_sb", 1, 1))
                    out = r_R.rearrange("p a (h b c) -> p (a h) b c", h=H, b=2)
                    rotate(x(r_z[:, 0:256]), x(r_a), x(r_b), rope[:, i, 64:80], rope[:, i, 80:96], out, 16).then_inc(sems["r_roped"], tally("r_roped"))
                    link(dve.drain())
                    TT(hd(r_kz), hd(r_R[:, 1, :]), spread(zeta[:, 0, :], 2, 32), ALU.mult).then_inc(sems["r_kz"], tally("r_kz"))
                    dve.wait_ge(sems["r_kv"], nth("r_kv", 1, 1))
                    link(STT(r_tmp, r_S[:, i, :], gch[:, 0:1], ps[:, 3, 0:256], ALU.mult, ALU.add))
                    link(TT(r_S[:, i + 1, :], r_tmp, cst["heads_diag"], ALU.mult))
                    dve.sem_inc(sems["r_state"], tally("r_state"))
                    dve.wait_ge(sems["r_kT_sb"], nth("r_kT_sb", 1, 1))

            def ret_backward(count, first):
                with ln.loop(count, [(n_, 1) for n_ in ("r_scores", "r_out", "r_kv")], down_from=first) as i:
                    t = ln.down
                    dve.wait_ge(sems["r_scores"], nth("r_scores", 1, 1))
                    TT(r_p, ps[:, 0:4, 0:P], r_dt, ALU.mult).then_inc(sems["r_probs"], tally("r_probs"))
                    dve.wait_ge(sems["r_out"], nth("r_out", 1, 1))
                    link(dve.tensor_reduce(ss[:, 0:4], ps[:, 4, 0:256].rearrange("p (h c) -> p h c", h=H), AX.X, ALU.add))
                    link(TS(musum, ss[:, 0:4], 1.0 / 64, None, ALU.mult))
                    by_pair = lambda ap: ap.rearrange("p a (h c) -> p a h c", h=2)
                    TT(by_pair(r_o[:, :, tile_cols(t)]), by_pair(ps[:, 4, 0:256].rearrange("p (a x) -> p a x", a=2)),
                       spread(musum.rearrange("p (a b) -> p a b", a=2), 3, 64), ALU.subtract).then_inc(sems["r_o"], tally("r_o"))
                    dve.wait_ge(sems["r_kv"], nth("r_kv", 1, 1))
                    link(STT(r_tmp, r_Sb, gch[:, 1:2], ps[:, 3, 0:256], ALU.mult, ALU.add))
                    link(TT(r_Sb, r_tmp, cst["heads_diag"], ALU.mult))
                    dve.sem_inc(sems["r_state"], tally("r_state"))

            def dn_project():
                for lo in (0, 2 + NCTX, 6 + NTOK):
                    m = dve.memset(raw[:, :, lo:lo + (4 if lo == 2 + NCTX else 2)], 0.0)
                for n_ in range(1, 18, 2):
                    j, (lo, hi) = n_ // 3, SEGMENTS[n_ % 3]
                    dve.wait_ge(sems["prod"], nth("prod", n_ + 1))
                    off = 2 if lo < NCTX else 6
                    TS(raw[:, j, lo + off:hi + off], ps[:, n_ % 4, 0:hi - lo], 1.0, None, ALU.mult).then_inc(sems["evac_dve"], tally("evac_dve"))
                ln.passed("prod", 18)

            def dn_gates_():
                ab = d_ab.rearrange("p t (q a h) -> p t q a h", q=2, a=2)
                for q in range(2):
                    m = TT(d_x[:, :, 4 * q:4 * q + 4], ab[:, :, q, 0, :], spread(par["dt"][:, 4 * q:4 * q + 4], 1, NT), ALU.add)
                link(m)
                link(TS(flat(d_w), flat(d_x), -1.0, None, ALU.mult))
                TT(flat(d_w), flat(d_w), flat(d_x), ALU.min).then_inc(sems["dn_gates"], tally("dn_gates"))
                link(dve.drain())
                TS(flat(d_x), flat(d_x), 0.0, None, ALU.max)
                dve.wait_ge(sems["dn_gates2"], nth("dn_gates2", 1))
                TS(flat(d_bt), flat(d_bt), 1.0, 0.5, ALU.add, ALU.mult)
                TS(flat(d_w), flat(d_w), 1.0, None, ALU.add).then_inc(sems["dn_gates"], tally("dn_gates"))
                dve.wait_ge(sems["dn_gates2"], nth("dn_gates2", 2))
                link(TT(flat(d_x), flat(d_x), flat(d_w), ALU.add))
                link(STT(d_lg, d_x, -1.0, spread(nega, 1, NT), ALU.mult, ALU.mult))
                ln.passed("dn_gates2", 2)

            def dn_conv():
                taps = par["conv"].rearrange("p (j k) -> p j k", j=6)
                n_ = PADDED - 4
                with ln.loop(6, [("c_tanh", 1)]) as j:
                    for k in range(5):
                        src = raw[:, j, k:k + n_]
                        w_ = taps[:, j, k:k + 1]
                        m = TS(cv_y, src, w_, None, ALU.mult) if k == 0 else STT(cv_y, src, w_, cv_y, ALU.mult, ALU.add)
                        link(m)
                    dve.sem_inc(sems["c_y"], tally("c_y"))
                    dve.wait_ge(sems["c_tanh"], nth("c_tanh", 1, 1))
                    STT(raw[:, j, 0:NCTX], cv_t[:, 0:NCTX], 1.0, cv_y[:, 0:NCTX], ALU.add, ALU.mult)
                    link(STT(raw[:, j, NCTX:NTOK], cv_t[:, NCTX + 4:NTOK + 4], 1.0, cv_y[:, NCTX + 4:NTOK + 4],
                             ALU.add, ALU.mult))

            def dn_norm():
                n_ = 0
                for j in NORM_ORDER:
                    for lo, hi in norm_segments:
                        dve.wait_ge(sems["d_root"], nth("d_root", n_ + 1))
                        r_ = n_root[:, n_ % 4, 0:hi - lo]
                        link(dve.reciprocal(r_, r_))
                        TT(raw[:, j, lo:hi], raw[:, j, lo:hi], r_, ALU.mult).then_inc(sems["d_norm"], tally("d_norm"))
                        n_ += 1

            def dn_scan(count, first, last):
                sig = [(f"{n_}{q}", 1) for n_ in ("u_g", "u_dt", "u_gram", "u_vmm", "u_omm") for q in range(2)]
                sig += [(f"{n_}{q}", 6) for n_ in ("u_ymm", "u_umm") for q in range(2)]
                hd = lambda ap: ap.rearrange("p (h c) -> p h c", h=H)
                with ln.loop(count, sig, down_from=last) as i:
                    tt = (first + i, ln.down)
                    for q in range(2):
                        b, Ab, Bb, Cb, Db = sc[q], *(ps[:, 4 * q + z, :] for z in range(4))
                        dve.wait_ge(sems[f"u_g{q}"], nth(f"u_g{q}", 1, 1))
                        link(TS(gc[q], Db[:, 0:8], 1.0, None, ALU.mult))
                        TS(tl[q][:, 0:4], gc[q][:, 0:4], 1.0, None, ALU.mult)
                        TT(tl[q][:, 4:8], gc[q][:, 4:8], gc[q][:, 0:4], ALU.subtract)
                        TS(tl[q][:, 8:12], gc[q][:, 4:8], 1.0, None, ALU.mult)
                        for h in range(H):
                            m = STT(b["dt"][:, h, :], hd(Ab)[:, h, :], gc[q][:, h:h + 1], upto[:, q, :], ALU.subtract, ALU.min)
                        m.then_inc(sems[f"u_arg{q}"], tally(f"u_arg{q}"))
                    for q in range(2):
                        b, Ab, Bb, Cb, Db = sc[q], *(ps[:, 4 * q + z, :] for z in range(4))
                        dve.wait_ge(sems[f"u_gram{q}"], nth(f"u_gram{q}", 1, 1))
                        dve.wait_ge(sems[f"u_dt{q}"], nth(f"u_dt{q}", 1, 1))
                        gram = ps[:, 4 * q + 1:4 * q + 3, :].rearrange("p e (a j c) -> p e a j c", a=2, j=2)
                        for h in range(H):
                            STT(b["at"][:, h, :], gram[:, h % 2, 0, h // 2, :], d_bt[:, tt[q], 4 * q + h:4 * q + h + 1], b["dt"][:, h, :],
                                ALU.mult, ALU.mult)
                        by_half = lambda ap: ap.rearrange("p (j e) c -> p e j c", e=2)
                        link(TT(by_half(b["qkd"]), gram[:, :, 1, :, :], by_half(b["dt"]), ALU.mult))
                        link(TT(b["u"], b["at"], spread(levels[:, 1 - q, 0, :], 1, H), ALU.mult))
                        TT(b["u"], b["u"], spread(ident, 1, H), ALU.add).then_inc(sems[f"u_inv{q}"], tally(f"u_inv{q}"))
                    for lv in range(1, LEVELS):
                        for q in range(2):
                            b = sc[q]
                            dve.wait_ge(sems[f"u_ymm{q}"], nth(f"u_ymm{q}", lv, 6))
                            TT(b["ym"], hd(ps[:, 4 * q + 1, :]), spread(levels[:, q, lv, :], 1, H), ALU.mult).then_inc(sems[f"u_ysb{q}"], tally(f"u_ysb{q}"))
                        for q in range(2):
                            b = sc[q]
                            dve.wait_ge(sems[f"u_umm{q}"], nth(f"u_umm{q}", lv, 6))
                            TT(b["u"], hd(ps[:, 4 * q + 2, :]), b["u"], ALU.add).then_inc(sems[f"u_usb{q}"], tally(f"u_usb{q}"))
                    for q in range(2):
                        b = sc[q]
                        dve.wait_ge(sems[f"u_vmm{q}"], nth(f"u_vmm{q}", 1, 1))
                        TT(hd(b["vn"]), hd(ps[:, 4 * q + 1, 0:256]), spread(d_bt[:, tt[q], 4 * q:4 * q + 4], 2, 64), ALU.mult).then_inc(sems[f"u_vsb{q}"], tally(f"u_vsb{q}"))
                    for q in range(2):
                        b, Ab, Cb = sc[q], ps[:, 4 * q, :], ps[:, 4 * q + 2, :]
                        dve.wait_ge(sems[f"u_omm{q}"], nth(f"u_omm{q}", 1, 1))
                        for h in range(H):
                            rows = slice(64 * (h % 2), 64 * (h % 2) + 64)
                            S_ = b["S"][rows, h // 2, 64 * (h % 2):64 * (h % 2) + 64]
                            STT(S_, S_, egt[q][rows, 8 + h:9 + h], Ab[rows, h * 64:(h + 1) * 64], ALU.mult, ALU.add)
                        link(TT(b["o"], hd(Cb[:, 0:256]), spread(egt[q][:, 0:4], 2, 64), ALU.mult))
                        link(TT(flat(b["o"]), Cb[:, 256:512], flat(b["o"]), ALU.add))
                        link(TT(d_o[:, tt[q], :], d_o[:, tt[q], :], flat(b["o"]), ALU.add))
                        dve.sem_inc(sems[f"u_done{q}"], tally(f"u_done{q}"))

            def gate(g_):
                heads, th = (lambda ap, n: ap.rearrange("p (h c) -> p h c", h=n)), flat(g_["th"])
                n_gain = g_["gain"].shape[1]
                dve.wait_ge(sems["g_sq"], nth("g_sq", 1))
                link(dve.tensor_reduce(g_["root"], g_["sq"], AX.X, ALU.add))
                TS(g_["root"], g_["root"], 1.0 / 64, EPS, ALU.mult, ALU.add).then_inc(sems["g_veps"], tally("g_veps"))
                dve.wait_ge(sems["g_tanh"], nth("g_tanh", 1))
                link(STT(th, th, 1.0, flat(g_["z"]), ALU.add, ALU.mult))
                th_ = heads(th, NT * 256 // n_gain)
                link(TT(th_, th_, spread(g_["gain"], 1, NT * 256 // n_gain), ALU.mult))
                dve.wait_ge(sems["g_rstd"], nth("g_rstd", 1))
                link(dve.reciprocal(g_["rs"], g_["root"]))
                for c in range(NT // 2):
                    o_ = g_["o_pair"](c)
                    if g_["rs_pair"]:
                        for a in range(2):
                            oa = o_[:, a].rearrange("p t (h c) -> p (t h) c", h=2)
                            m = TT(oa, oa, spread(g_["rs_pair"](g_["rs"], c)[:, a, :], 2, 64), ALU.mult)
                    else:
                        o2 = heads(flat(d_o[:, 2 * c:2 * c + 2, :]), 2 * H)
                        m = TT(o2, o2, spread(g_["rs"][:, 2 * c * H:2 * (c + 1) * H], 2, 64), ALU.mult)
                    link(m)
                    for a in range(2):
                        m = STT(pairs(g_["out"], c)[:, a], o_[:, a], 0.5, pairs(g_["th"], c)[:, a], ALU.mult, ALU.mult)
                    m.then_inc(sems["g_y"], tally("g_y"))

            def add_gated(L, n_, bank, cols, gate_):
                j, (lo, hi) = n_ // len(cols), cols[n_ % len(cols)]
                which = 1 if lo < NCTX else 0
                STT(X[:, j, lo:hi], ps[:, bank, 0:hi - lo], mods[:, L, gate_ + j, which:which + 1], X[:, j, lo:hi],
                        ALU.mult, ALU.add).then_inc(sems["evac_dve"], tally("evac_dve"))

            def project_out(L):
                cols = tokens(L)
                for n_ in range(8 * len(cols)):
                    dve.wait_ge(sems["prod"], nth("prod", n_ + 1))
                    add_gated(L, n_, n_ % 4, cols, G1)
                ln.passed("prod", 8 * len(cols))

            def mlp(L):
                cols = tokens(L)
                up, down = 4 * len(cols), 8 * len(cols)
                first = cols[0][0]
                for k in range(KT):
                    dve.wait_ge(sems["h_high"], nth("h_high", k + 1))
                    TT(H_lo[:, k, first:NTOK], Hm[:, k, first:NTOK], H_hi[:, k, first:NTOK].bitcast(F32), ALU.subtract)\
                        .then_inc(sems["h_split"], tally("h_split"))
                with ln.loop(FG, [("sq_done", up), ("prod", up + down)]):
                    for n_ in range(up):
                        j, (lo, hi) = n_ // len(cols), cols[n_ % len(cols)]
                        dve.wait_ge(sems["sq_done"], nth("sq_done", n_ + 1, up))
                        u_ = U[:, j, lo:hi]
                        link(TT(u_, u_, u_, ALU.mult))
                        TT(U_lo[:, j, lo:hi], u_, U_hi[:, j, lo:hi].bitcast(F32), ALU.subtract).then_inc(sems["hidden"], tally("hidden"))
                    for n_ in range(down):
                        dve.wait_ge(sems["prod"], nth("prod", up + n_ + 1, up + down))
                        add_gated(L, n_, 4 + n_ % 4, cols, G2)

            def layer_norm(L):
                n = len(tokens(L))
                for c, (lo, hi) in enumerate(tokens(L)):
                    dve.wait_ge(sems["ln_mean"], nth("ln_mean", c + 1))
                    TT(X[:, :, lo:hi], X[:, :, lo:hi], spread(ps[:, c, 0:hi - lo], 1, KT), ALU.subtract).then_inc(sems["ln_centred"], tally("ln_centred"))
                for c, (lo, hi) in enumerate(tokens(L)):
                    dve.wait_ge(sems["ln_var"], nth("ln_var", c + 1))
                    TS(ln_r[:, c, 0:hi - lo], ps[:, c + 3, 0:hi - lo], LN_EPS, None, ALU.add).then_inc(sems["ln_veps"], tally("ln_veps"))
                for c, (lo, hi) in enumerate(tokens(L)):
                    dve.wait_ge(sems["ln_root"], nth("ln_root", c + 1))
                    link(dve.reciprocal(ln_r[:, c, 0:hi - lo], ln_r[:, c, 0:hi - lo]))
                    TT(X[:, :, lo:hi], X[:, :, lo:hi], spread(ln_r[:, c, 0:hi - lo], 1, KT), ALU.mult).then_inc(sems["ln_scaled"], tally("ln_scaled"))
                for n_ in ("ln_mean", "ln_var", "ln_root"):
                    ln.passed(n_, n)

            dve.wait_ge(sems["consts_in"], 32)
            dve.wait_ge(sems["x_in"], nth("x_in", 32))
            for L in range(DEPTH):
                ln.barrier()
                if L == 0:
                    ada(0, 0)
                    ada(0, 1)
                ln.barrier()
                modulate(L, SH1, SC1)
                ln.barrier()
                mla_prep()
                ln.barrier()
                latent_attention(L)
                ln.barrier()
                ret_tables()
                ln.barrier()
                ret_forward()
                ln.barrier()
                ada(L, 5)
                link(dve.memset(r_Sb, 0.0))
                dve.sem_inc(sems["r_kcopy"], tally("r_kcopy"))
                ret_backward(CT, CT - 1)
                ret_backward(NT - CT, NT - 1)
                ln.barrier()
                gate(gate_ret)
                ln.barrier()
                swa_prep()
                ln.barrier()
                if L == 0:
                    ada(1, 0)
                    run(CT, 2, 0.125, True, [])
                run(1, 4, 0.125, True, [(3, 1)], False)
                run(NT - CT - 2, 5, 0.125, True, [(2, 0), (4, 1)])
                run(1, 4, 0.125, True, [(2, 0)], False)
                ln.barrier()
                dn_project()
                ln.barrier()
                dn_gates_()
                dn_conv()
                ln.barrier()
                dn_norm()
                ln.barrier()
                dn_scan(CT, 0, CT - 1)
                dn_scan(NT - CT, CT, NT - 1)
                ln.barrier()
                gate(gate_dn)
                ln.barrier()
                project_out(L)
                ln.barrier()
                if L == 0:
                    ada(1, 1)
                layer_norm(L)
                ln.barrier()
                modulate(L, SH2, SC2)
                ln.barrier()
                mlp(L)
                ln.barrier()
                layer_norm(L)
                ln.barrier()

        @block.gpsimd
        def _(pool):
            ln = Lane(pool, "pool", sems, book)
            start(ln)
            nth, tally, link = ln.nth, ln.tally, ln.link
            TT, TS, COPY = pool.tensor_tensor, pool.tensor_scalar, pool.tensor_copy

            def root(dst, src, n):
                return TT(dst[:, 0:n], src[:, 0:n], mhalf[:, 0:n], ALU.pow)

            def mla_prep():
                with ln.loop(NT, [("veps", 1)]) as i:
                    COPY(hst, Hm[:, :, tile_cols(i)]).then_inc(sems["tile_in"], tally("tile_in"))
                    pool.wait_ge(sems["veps"], nth("veps", 1, 1))
                    root(rs2, rs, 2).then_inc(sems["rstd"], tally("rstd"))

            def attend(count, stage, per_looped=True):
                if per_looped:
                    with ln.loop(count, [("yT_mm", 1)]) as i:
                        stage(i)
                        pool.wait_ge(sems["yT_mm"], nth("yT_mm", 1, 1))
                else:
                    stage(0)
                    pool.wait_ge(sems["yT_mm"], nth("yT_mm", 1))
                    ln.passed("yT_mm", count)

            def swa_stage(first, nband):
                def stage(i):
                    t = first + i
                    if nband:
                        lo = lowest(t, nband)
                        COPY(kst[:, 0:nband, :].rearrange("p a b -> p (a b)"), w_kT[:, bass.ds(lo * P, nband * P)])
                    COPY(qst[:, 0:2, :], w_qT[:, :, tile_cols(t)]).then_inc(sems["q_staged"], tally("q_staged"))
                return stage

            def plain_prep():
                with ln.loop(NT, [("z_mm", 1)]) as i:
                    COPY(hst, Hm[:, :, tile_cols(i)]).then_inc(sems["tile_in"], tally("tile_in"))
                    pool.wait_ge(sems["z_mm"], nth("z_mm", 1, 1))

            def dn_stage():
                with ln.loop(NT // 2, [("z_mm", 2)]) as i:
                    for s_ in range(2):
                        pool.wait_ge(sems["z_mm"], nth("z_mm", s_ - 1, 2))
                        COPY(d_hst[s_], Hm[:, :, tile_cols(2 * i + s_)]).then_inc(sems["tile_in"], tally("tile_in"))

            def ret_backward(count, first):
                hd = lambda ap: ap.rearrange("p (h c) -> p h c", h=H)
                with ln.loop(count, [("r_kv", 1)], down_from=first) as i:
                    t = ln.down
                    COPY(r_qst[:, 0:2, :], r_qkT[:, :, tile_cols(t)])
                    TT(r_qst[:, 2, :], r_qkT[:, 0, tile_cols(t)], r_xi[:, 0, :], ALU.mult)
                    TT(r_qst[:, 3, :], r_qkT[:, 0, tile_cols(t)], r_xi[:, 1, :], ALU.mult).then_inc(sems["r_stage"], tally("r_stage"))
                    TT(hd(r_kz), hd(r_k[:, t, :]), spread(zeta[:, 1, :], 2, 32), ALU.mult).then_inc(sems["r_kz"], tally("r_kz"))
                    pool.wait_ge(sems["r_kv"], nth("r_kv", 1, 1))

            def dn_norm():
                link(pool.memset(n_block, 0.0))
                link(pool.memset(n_block[0:64, 0:64], 1.0))
                link(pool.memset(n_block[64:128, 64:128], 1.0))
                link(pool.memset(n_eps[:, 0:1], 4 * 64 * EPS))
                pool.memset(n_eps[:, 1:2], 4 * EPS).then_inc(sems["d_stage"], tally("d_stage"))

            def dn_scan(count, first, last):
                hd = lambda ap: ap.rearrange("p (h c) -> p h c", h=H)
                with ln.loop(count, [(f"{n_}{q}", 1) for n_ in ("u_dt", "u_omm") for q in range(2)], down_from=last) as i:
                    tt = (first + i, ln.down)
                    for q in range(2):
                        b = sc[q]
                        COPY(b["qk"], raw[:, 0:4, tile_cols(tt[q])])
                        TT(b["gm"], spread(tri[:, q, :], 1, H), spread(d_lg[:, tt[q], 4 * q:4 * q + 4], 2, P), ALU.mult).then_inc(sems[f"u_stage{q}"], tally(f"u_stage{q}"))
                    for q in range(2):
                        b = sc[q]
                        pool.wait_ge(sems[f"u_dt{q}"], nth(f"u_dt{q}", 1, 1))
                        k_ = hd(kv_tok[:, tt[q], 0:256])
                        TT(hd(b["kt"]), k_, spread(egt[q][:, 4:8], 2, 64), ALU.mult)
                        TT(hd(b["keg"]), k_, spread(egt[q][:, 0:4], 2, 64), ALU.mult).then_inc(sems[f"u_keg{q}"], tally(f"u_keg{q}"))
                    for q in range(2):
                        pool.wait_ge(sems[f"u_omm{q}"], nth(f"u_omm{q}", 1, 1))

            def latent_attention(L):
                units, plan = latent_plan(L)
                last = {}
                for n_, (h, lo, hi, nk) in enumerate(units):
                    last[h] = n_
                link(pool.memset(m_k[96:97, :, :], 1.0))
                link(pool.memset(v_ones[0][:, :, 64:128], 1.0))
                link(pool.memset(v_ones[1][:, :, 0:64], 1.0))
                for h in range(H):
                    if h >= 2:
                        pool.wait_ge(sems["y_done"], nth("y_done", last[h - 2] + 1))
                    at_ = 64 * (h % 2)
                    COPY(v_ones[h % 2][:, :, at_:at_ + 64], m_v[:, :, h * 64:(h + 1) * 64]).then_inc(sems["v_staged"], tally("v_staged"))

            def mlp(L):
                with ln.loop(2 * FG) as i:
                    for s in range(2):
                        pool.wait_ge(sems[f"half_in_{s}"], i * 16 + 16 * (2 * FG * L + 1))
                        by = lambda ap: ap.rearrange("p (a b) -> p a b", b=P)
                        link(TT(by(half_hi[s]), by(half[s]), spread(ones, 1, HALF // P), ALU.mult))
                        TT(half_lo[s], half[s], half_hi[s].bitcast(F32), ALU.subtract).then_inc(sems["split"], tally("split"))

            pool.memset(mhalf, -0.5)
            pool.wait_ge(sems["consts_in"], 32)
            for L in range(DEPTH):
                ln.barrier()
                ln.barrier()
                ln.barrier()
                mla_prep()
                ln.barrier()
                latent_attention(L)
                ln.barrier()
                ln.barrier()
                plain_prep()
                ln.barrier()
                pool.wait_ge(sems["r_kcopy"], nth("r_kcopy", 1))
                ln.passed("r_kcopy", 1)
                ret_backward(CT, CT - 1)
                ret_backward(NT - CT, NT - 1)
                ln.barrier()
                ln.barrier()
                plain_prep()
                ln.barrier()
                if L == 0:
                    attend(CT, swa_stage(0, 0))
                attend(1, swa_stage(CT, 2), False)
                attend(NT - CT - 2, swa_stage(CT + 1, 3))
                attend(1, swa_stage(NT - 1, 2), False)
                ln.barrier()
                dn_stage()
                ln.barrier()
                ln.barrier()
                dn_norm()
                ln.barrier()
                link(pool.memset(d_o[:], 0.0))
                for q in range(2):
                    pool.memset(sc[q]["S"], 0.0)
                dn_scan(CT, 0, CT - 1)
                dn_scan(NT - CT, CT, NT - 1)
                ln.barrier()
                ln.barrier()
                ln.barrier()
                ln.barrier()
                ln.barrier()
                mlp(L)
                ln.barrier()
                ln.barrier()


def pack_chunk(w, rows, cols):
    part = w[rows:rows + DM][:, cols]
    out = np.zeros((KT, P, CW), np.float32)
    out[:, :, :part.shape[1]] = part.reshape(KT, P, -1)
    return out.transpose(1, 0, 2).reshape(P, KT * CW)


def pack_weights(w):
    r = np.arange
    out = []
    ada = lambda L, v: [pack_chunk(w["ada_w"][L], 0, r(c * CW, (c + 1) * CW)) for c in (2 * v, 2 * v + 1)]
    heads = np.concatenate([r(64 * h, 64 * h + 64) for h in (0, 2, 1, 3)])
    for L in range(DEPTH):
        mixers = [pack_chunk(w["w_in"][L], 0, cols) for cols in (
            r(2320, 2736), r(1552, 2064), r(2064, 2320), np.concatenate([heads, r(256, 512)]),
            r(512, 896), r(896, 1280), r(1280, 1552))]
        if L == 0:
            out += ada(0, 0) + ada(0, 1)
        out += mixers[:1] + ada(L, 2) + ada(L, 3) + ada(L, 4) + mixers[1:3] + ada(L, 5) + mixers[3:4]
        if L == 0:
            out += ada(1, 0)
        out += mixers[4:]
        out += [pack_chunk(w["w_out"][L], 0, r(c * CW, (c + 1) * CW)) for c in range(2)]
        if L == 0:
            out += ada(1, 1)
    return np.stack(out)


def pack_mlp(w):
    out = []
    for L in range(DEPTH):
        for g in range(FG):
            for c in range(2):
                cols = slice(g * FW + c * FW // 2, g * FW + (c + 1) * FW // 2)
                out.append(w["w_ff1"][L][:, cols].reshape(KT, P, -1).transpose(1, 0, 2).reshape(P, HALF))
            for c in range(2):
                part = w["w_ff2"][L][g * FW:(g + 1) * FW, c * DM // 2:(c + 1) * DM // 2]
                out.append(part.reshape(FW // P, P, -1).transpose(1, 0, 2).reshape(P, HALF))
    return np.stack(out)


def pack_params(w, L):
    rows = lambda a: np.broadcast_to(np.ravel(a)[None, :], (P, np.size(a)))
    chan = lambda a: np.reshape(a, (-1, P)).T
    out = np.zeros((P, NPARAM), np.float32)
    g = w["ret_log1m_gamma"][L]
    conv = np.asarray(w["dn_conv_w"][L]).reshape(5, 6, P).transpose(2, 1, 0).reshape(P, 30)
    values = {
        "sink": rows(w["swa_sink"][L]), "log1m": rows(g),
        "log1m_row": np.repeat(g, 32, axis=1).T, "a_log": rows(w["dn_a_log"][L]), "dt": rows(w["dn_dt_bias"][L]),
        "dn_g": rows(w["dn_norm_g"][L]), "ret_g": rows(w["ret_norm_g"][L]), "ln1_g": chan(w["ln1_g"][L]),
        "ln1_b": chan(w["ln1_b"][L]), "ln2_g": chan(w["ln2_g"][L]), "ln2_b": chan(w["ln2_b"][L]), "conv": conv,
        "q_norm": chan(w["mla_q_norm"][L]), "kv_norm": chan(w["mla_kv_norm"][L]),
    }
    for name, v in values.items():
        a, b = PARAMS[name]
        out[:, a:b] = v
    return out


def kernel(**inputs):
    import concourse.bacc as _bacc
    from concourse.bass_utils import run_bass_kernel_spmd as _run

    w = {k: np.asarray(v) for k, v in inputs.items()}
    channels = lambda a: a.T.reshape(KT, P, -1).transpose(1, 0, 2)
    arrays = {
        "x": channels(np.concatenate([w["ctx"][0], w["x"][0]], 0)),
        "cc": channels(np.stack([w["c"][0], w["c_ctx"]], 0)),
        "weights": pack_weights(w),
        "ff": pack_mlp(w),
        "params": np.stack([pack_params(w, L) for L in range(DEPTH)]),
        "w_uq": w["mla_w_uq"].reshape(DEPTH, 2, P, 384).transpose(0, 2, 1, 3),
        "w_ukv": w["mla_w_ukv"],
        "consts": np.concatenate(list(constants().values()), 1),
        "levels": level_masks(),
        "ada_b": w["ada_b"].reshape(DEPTH, 48, P).transpose(2, 0, 1),
    }
    arrays = {k: np.ascontiguousarray(v, dtype=np.float32) for k, v in arrays.items()}

    def program(book):
        nc = _bacc.Bacc("TRN2", target_bir_lowering=False, num_devices=1)
        d = {k: nc.dram_tensor("in_" + k, v.shape, F32, kind="ExternalInput").ap() for k, v in arrays.items()}
        d["out"] = nc.dram_tensor("out_x", (P, KT, NLAT), F32, kind="ExternalOutput").ap()
        build(nc, d, book)
        return nc

    book = {"links": {}, "new": {}, "old": {}}
    program(book)
    book = {"links": book["links"], "old": book["new"], "new": {}, "phases_old": book["phases"]}
    nc = program(book)
    r = _run(nc, [{"in_" + k: v for k, v in arrays.items()}], core_ids=[0])
    out = r.results[0]["out_x"]
    return np.ascontiguousarray(out.transpose(2, 1, 0).reshape(1, NLAT, DM))
```
